# Optimizing a Trainium2 kernel written in Bass

```python
import math
import jax, jax.numpy as jnp
from jax import lax
import numpy as np

D_MODEL = 1024
BATCH = 1
SEQ = 512
DEPTH = 1

CHUNK = 64
N_META = 16
D_CONV = D_MODEL // 4
CONV_WIDTH = 31
N_Q_HEADS = 8
N_KV_HEADS = 2
HEAD_DIM = 64
D_ATTN = N_Q_HEADS * HEAD_DIM
D_KV = N_KV_HEADS * HEAD_DIM
WINDOW = 128
N_PREV_CHUNKS = WINDOW // CHUNK - 1
N_HGRN_HEADS = 4
HGRN_DIM = 64
D_HGRN = N_HGRN_HEADS * HGRN_DIM
D_MIX = D_CONV + D_ATTN + D_HGRN
IN_SPLITS = (2 * D_CONV, D_ATTN, D_KV, D_KV, D_HGRN, D_HGRN, D_HGRN, D_HGRN)
D_IN_PROJ = 2 * D_CONV + D_ATTN + 2 * D_KV + 4 * D_HGRN
N_GROUPS = 4
EXPERTS_PER_GROUP = 8
N_EXPERTS = N_GROUPS * EXPERTS_PER_GROUP
TOP_K = 2
D_EXPERT = D_MODEL // 4
EPS = 1e-6

kernel_name = "hymba_chunked_conv_swa_hgrn2_hmoe"

def _rmsnorm(x, g):
    xf = x.astype(jnp.float32)
    y = xf * lax.rsqrt(jnp.mean(xf * xf, axis=-1, keepdims=True) + EPS)
    return (y * g.astype(jnp.float32)).astype(x.dtype)

def _split_cols(u):
    pts = [int(p) for p in np.cumsum(np.array(IN_SPLITS))[:-1]]
    return jnp.split(u, pts, axis=-1)

def _alibi_slopes(n_heads):
    return jnp.exp2(-8.0 * (jnp.arange(n_heads, dtype=jnp.float32) + 1.0) / n_heads)

def _conformer_conv(u, dw_w, dw_b, ln_g, ln_b):
    a, gate = jnp.split(u, 2, axis=-1)
    h = a * jax.nn.sigmoid(gate)
    h = lax.conv_general_dilated(
        h, dw_w[:, None, :].astype(h.dtype), window_strides=(1,),
        padding=[(CONV_WIDTH - 1, 0)],
        dimension_numbers=('NWC', 'WIO', 'NWC'), feature_group_count=D_CONV)
    hf = (h + dw_b).astype(jnp.float32)
    mu = jnp.mean(hf, axis=-1, keepdims=True)
    var = jnp.mean(jnp.square(hf - mu), axis=-1, keepdims=True)
    hf = (hf - mu) * lax.rsqrt(var + EPS) * ln_g.astype(jnp.float32) + ln_b.astype(jnp.float32)
    return jax.nn.silu(hf).astype(u.dtype)

def _sink_attention(q, k, v, bias, valid, sinks):
    s = jnp.einsum('...ikgd,...jkd->...kgij', q, k).astype(jnp.float32) * (HEAD_DIM ** -0.5)
    s = jnp.where(valid, s + bias, -jnp.inf)
    sink = jnp.broadcast_to(sinks.astype(jnp.float32)[:, :, None, None], s.shape[:-1] + (1,))
    p = jax.nn.softmax(jnp.concatenate([s, sink], axis=-1), axis=-1)[..., :-1]
    return jnp.einsum('...kgij,...jkd->...ikgd', p.astype(v.dtype), v)

def _swa_mixer(q, k, v, sinks):
    B, L, _ = q.shape
    G = N_Q_HEADS // N_KV_HEADS
    q = q.reshape(B, L, N_KV_HEADS, G, HEAD_DIM)
    k = k.reshape(B, L, N_KV_HEADS, HEAD_DIM)
    v = v.reshape(B, L, N_KV_HEADS, HEAD_DIM)
    slopes = _alibi_slopes(N_Q_HEADS).reshape(N_KV_HEADS, G)
    sinks = sinks.reshape(N_KV_HEADS, G)
    qm, km, vm = q[:, :N_META], k[:, :N_META], v[:, :N_META]
    pm = jnp.arange(N_META)
    dist_m = jnp.abs(pm[:, None] - pm[None, :]).astype(jnp.float32)
    out_m = _sink_attention(qm, km, vm, -slopes[:, :, None, None] * dist_m, True, sinks)
    nc = (L - N_META) // CHUNK
    qr = q[:, N_META:].reshape(B, nc, CHUNK, N_KV_HEADS, G, HEAD_DIM)
    kr = k[:, N_META:].reshape(B, nc, CHUNK, N_KV_HEADS, HEAD_DIM)
    vr = v[:, N_META:].reshape(B, nc, CHUNK, N_KV_HEADS, HEAD_DIM)

    def shift(a, p):
        return jnp.pad(a, ((0, 0), (p, 0), (0, 0), (0, 0), (0, 0)))[:, :nc]

    prevs = list(range(N_PREV_CHUNKS, 0, -1))
    kb = jnp.concatenate([jnp.broadcast_to(km[:, None], (B, nc, N_META, N_KV_HEADS, HEAD_DIM))]
                         + [shift(kr, p) for p in prevs] + [kr], axis=2)
    vb = jnp.concatenate([jnp.broadcast_to(vm[:, None], (B, nc, N_META, N_KV_HEADS, HEAD_DIM))]
                         + [shift(vr, p) for p in prevs] + [vr], axis=2)
    c = jnp.arange(nc)[:, None]
    j = jnp.arange(CHUNK)[None, :]
    qpos = N_META + c * CHUNK + j
    kpos = jnp.concatenate([jnp.broadcast_to(pm[None], (nc, N_META))]
                           + [N_META + (c - p) * CHUNK + j for p in prevs] + [qpos], axis=1)
    kvalid = jnp.concatenate([jnp.ones((nc, N_META), bool)]
                             + [jnp.broadcast_to(c >= p, (nc, CHUNK)) for p in prevs]
                             + [jnp.ones((nc, CHUNK), bool)], axis=1)
    dist = jnp.abs(qpos[:, :, None] - kpos[:, None, :]).astype(jnp.float32)
    bias = -slopes[None, :, :, None, None] * dist[:, None, None]
    out_r = _sink_attention(qr, kb, vb, bias, kvalid[:, None, None, None, :], sinks)
    return jnp.concatenate([out_m.reshape(B, N_META, D_ATTN),
                            out_r.reshape(B, nc * CHUNK, D_ATTN)], axis=1)

def _hgrn2_chunk_step(S, inp):
    q, k, v, g = inp
    b = jnp.cumsum(g, axis=2)
    causal = jnp.tril(jnp.ones((CHUNK, CHUNK), bool))[:, :, None]
    decay = jnp.exp(jnp.where(causal, b[:, :, :, None, :] - b[:, :, None, :, :], -jnp.inf))
    A = jnp.einsum('bhtd,bhsd,bhtsd->bhts', q, k, decay)
    o = jnp.einsum('bhtd,bhde->bhte', q * jnp.exp(b), S) + jnp.einsum('bhts,bhse->bhte', A, v)
    b_last = b[:, :, -1:, :]
    S_new = jnp.exp(b_last[:, :, 0])[..., None] * S + jnp.einsum('bhsd,bhse->bhde', k * jnp.exp(b_last - b), v)
    return S_new, o

def _hgrn2_mixer(q, f_logit, i_in, g_out, lb, norm_g):
    B, L, _ = q.shape
    H, dk = N_HGRN_HEADS, HGRN_DIM
    f32 = jnp.float32
    qf = jax.nn.silu(q.astype(f32))
    z = f_logit.astype(f32)
    log_f = jnp.logaddexp(jnp.log(lb), jnp.log1p(-lb) + jax.nn.log_sigmoid(z))
    kf = (1.0 - lb) * jax.nn.sigmoid(-z)
    vf = i_in.astype(f32)
    pad = (-L) % CHUNK
    n = (L + pad) // CHUNK

    def to_chunks(a):
        a = jnp.pad(a, ((0, 0), (pad, 0), (0, 0)))
        return a.reshape(B, n, CHUNK, H, dk).transpose(1, 0, 3, 2, 4)

    S0 = jnp.zeros((B, H, dk, dk), f32)
    _, o = lax.scan(_hgrn2_chunk_step, S0, (to_chunks(qf), to_chunks(kf), to_chunks(vf), to_chunks(log_f)))
    o = o.transpose(1, 0, 3, 2, 4).reshape(B, n * CHUNK, H, dk)[:, pad:]
    o = o * lax.rsqrt(jnp.mean(o * o, axis=-1, keepdims=True) + EPS) * norm_g.astype(f32).reshape(H, dk)
    o = o.reshape(B, L, D_HGRN) * jax.nn.silu(g_out.astype(f32))
    return o.astype(q.dtype)

def _hier_moe(h, w_rg, b_rg, w_re, b_re, w_gate, w_up, w_down):
    B, L, D = h.shape
    f32 = jnp.float32
    x = h.reshape(-1, D)
    N = x.shape[0]
    p_group = jax.nn.softmax((x @ w_rg).astype(f32) + b_rg.astype(f32), axis=-1)
    g_w, g_idx = lax.top_k(p_group, 1)
    e_logits = ((x @ w_re).astype(f32) + b_re.astype(f32)).reshape(N, N_GROUPS, EXPERTS_PER_GROUP)
    e_logits = jnp.take_along_axis(
        e_logits, jnp.broadcast_to(g_idx[:, :, None], (N, 1, EXPERTS_PER_GROUP)), axis=1)[:, 0]
    p_exp = jax.nn.softmax(e_logits, axis=-1)
    e_w, e_idx = lax.top_k(p_exp, TOP_K)
    e_w = e_w / jnp.sum(e_w, axis=-1, keepdims=True)
    comb = jnp.sum(jax.nn.one_hot(e_idx, EXPERTS_PER_GROUP, dtype=f32) * e_w[..., None], axis=1) * g_w
    comb = jax.nn.one_hot(g_idx[:, 0], N_GROUPS, dtype=f32)[:, :, None] * comb[:, None, :]
    wg = w_gate.reshape(N_GROUPS, EXPERTS_PER_GROUP, D, D_EXPERT)
    wu = w_up.reshape(N_GROUPS, EXPERTS_PER_GROUP, D, D_EXPERT)
    wd = w_down.reshape(N_GROUPS, EXPERTS_PER_GROUP, D_EXPERT, D)
    y = jnp.zeros((N, D), f32)
    for grp in range(N_GROUPS):
        act = jax.nn.silu(jnp.einsum('nd,edf->nef', x, wg[grp])) * jnp.einsum('nd,edf->nef', x, wu[grp])
        act = act * comb[:, grp, :, None].astype(act.dtype)
        y = y + jnp.einsum('nef,efd->nd', act, wd[grp]).astype(f32)
    return y.reshape(B, L, D).astype(h.dtype)

def setup_inputs(seed: int = 0) -> dict:
    key = jax.random.key(seed)
    ks = jax.random.split(key, 24)

    def n(k, shape, scale):
        return scale * jax.random.normal(k, shape, jnp.float32)

    return {
        "x": n(ks[0], (BATCH, SEQ, D_MODEL), 1.0),
        "meta_tokens": n(ks[1], (N_META, D_MODEL), 1.0),
        "mix_norm": 1.0 + n(ks[2], (DEPTH, D_MODEL), 0.02),
        "w_in": n(ks[3], (DEPTH, D_MODEL, D_IN_PROJ), D_MODEL ** -0.5),
        "conv_dw_w": n(ks[4], (DEPTH, CONV_WIDTH, D_CONV), CONV_WIDTH ** -0.5),
        "conv_dw_b": n(ks[5], (DEPTH, D_CONV), 0.02),
        "conv_ln_g": 1.0 + n(ks[6], (DEPTH, D_CONV), 0.02),
        "conv_ln_b": n(ks[7], (DEPTH, D_CONV), 0.02),
        "attn_sinks": n(ks[8], (DEPTH, N_Q_HEADS), 0.5),
        "hgrn_lb_logits": n(ks[9], (DEPTH, D_HGRN), 0.5),
        "hgrn_norm_g": 1.0 + n(ks[10], (DEPTH, D_HGRN), 0.02),
        "w_out": n(ks[11], (DEPTH, D_MIX, D_MODEL), D_MIX ** -0.5),
        "ffn_norm": 1.0 + n(ks[12], (DEPTH, D_MODEL), 0.02),
        "w_router_group": n(ks[13], (DEPTH, D_MODEL, N_GROUPS), D_MODEL ** -0.5),
        "b_router_group": n(ks[14], (DEPTH, N_GROUPS), 0.01),
        "w_router_expert": n(ks[15], (DEPTH, D_MODEL, N_EXPERTS), D_MODEL ** -0.5),
        "b_router_expert": n(ks[16], (DEPTH, N_EXPERTS), 0.01),
        "w_exp_gate": n(ks[17], (DEPTH, N_EXPERTS, D_MODEL, D_EXPERT), D_MODEL ** -0.5),
        "w_exp_up": n(ks[18], (DEPTH, N_EXPERTS, D_MODEL, D_EXPERT), D_MODEL ** -0.5),
        "w_exp_down": n(ks[19], (DEPTH, N_EXPERTS, D_EXPERT, D_MODEL), D_EXPERT ** -0.5),
        "final_norm": 1.0 + n(ks[20], (D_MODEL,), 0.02),
    }

def reference(x, meta_tokens, mix_norm, w_in, conv_dw_w, conv_dw_b, conv_ln_g, conv_ln_b,
              attn_sinks, hgrn_lb_logits, hgrn_norm_g, w_out, ffn_norm, w_router_group,
              b_router_group, w_router_expert, b_router_expert, w_exp_gate, w_exp_up,
              w_exp_down, final_norm):
    B = x.shape[0]
    h_res = jnp.concatenate([jnp.broadcast_to(meta_tokens[None].astype(x.dtype), (B, N_META, D_MODEL)), x], axis=1)
    lbs = jnp.cumsum(jax.nn.softmax(hgrn_lb_logits.astype(jnp.float32), axis=0), axis=0)
    lbs = lbs - lbs[0]
    for l in range(DEPTH):
        h = _rmsnorm(h_res, mix_norm[l])
        u = h @ w_in[l]
        u_conv, q_a, k_a, v_a, q_h, f_h, i_h, g_h = _split_cols(u)
        y_conv = _conformer_conv(u_conv, conv_dw_w[l], conv_dw_b[l], conv_ln_g[l], conv_ln_b[l])
        y_attn = _swa_mixer(q_a, k_a, v_a, attn_sinks[l])
        y_hgrn = _hgrn2_mixer(q_h, f_h, i_h, g_h, lbs[l], hgrn_norm_g[l])
        h_res = h_res + jnp.concatenate([y_conv, y_attn, y_hgrn], axis=-1) @ w_out[l]
        h_res = h_res + _hier_moe(_rmsnorm(h_res, ffn_norm[l]), w_router_group[l], b_router_group[l],
                                  w_router_expert[l], b_router_expert[l], w_exp_gate[l],
                                  w_exp_up[l], w_exp_down[l])
    return _rmsnorm(h_res, final_norm)[:, N_META:]


_drawn_inputs = setup_inputs


def setup_inputs(seed=0):
    import zlib

    import numpy as np

    out = dict(_drawn_inputs(seed))
    spreads = {}
    factors = {'conv_ln_g': 9.369,
     'conv_ln_b': 3.949,
     'attn_sinks': 15.319,
     'hgrn_norm_g': 11.845,
     'b_router_group': 11.442,
     'b_router_expert': 12.745,
     'final_norm': 8.67,
     'ffn_norm': 2.673}
    for name, (base, spread) in spreads.items():
        noise = np.random.default_rng([zlib.crc32(name.encode()), seed]).standard_normal(out[name].shape)
        drawn = base * np.exp(spread * noise) if base else spread * noise
        out[name] = __import__('jax').numpy.asarray(drawn.astype(out[name].dtype))
    for name, factor in factors.items():
        out[name] = (out[name] * factor).astype(out[name].dtype)
    return out
```

```python
import numpy as np
import concourse.bass as bass
from concourse import mybir
from contextlib import ExitStack

F32 = mybir.dt.float32
I32 = mybir.dt.int32
U32 = mybir.dt.uint32
ALU = mybir.AluOpType
ACT = mybir.ActivationFunctionType
AX = mybir.AxisListType.X

P = 128
D = 1024
KT = D // P
SEQ = 512
NT = SEQ // P
META = 16
CHUNK = 64
NC_ = SEQ // CHUNK
TAPS = 31
HD = 64
NQ, NKV = 8, 2
NE, NG, EPG = 32, 4, 8
DE = 256
EPS = 1e-6
LEVELS = (32, 16, 8, 4, 2, 1)
BC = 64
NBLK = NE + 2 * SEQ // BC
FAR = 8192
NEG = -1.0e30

C_A, C_GATE, C_Q, C_K, C_V = 0, 256, 512, 1024, 1152
C_HQ, C_HF, C_HI, C_HG = 1280, 1536, 1792, 2048
D_IN = 2304

K_ID = 0
K_TRI = K_ID + P
K_ONE = K_TRI + P
K_MEAN = K_ONE + P
K_HEAD = K_MEAN + P
K_RESET = K_HEAD + P
K_MASK = K_RESET + SEQ
K_DIST = K_MASK + (len(LEVELS) + 1) * CHUNK
DW = CHUNK + META + P
K_IOTA = K_DIST + NT * DW
K_TOK = K_IOTA + 64
K_THR = K_TOK + NT
K_EPS = K_THR + 7
K_ALL = K_EPS + 1


def shape_constants():
    c = np.zeros((P, K_ALL), np.float32)
    i = np.arange(P)
    c[:, K_ID:K_ID + P] = np.eye(P)
    c[:, K_TRI:K_TRI + P] = i[:, None] < i[None, :]
    c[:, K_ONE:K_ONE + P] = 1.0
    c[:, K_MEAN:K_MEAN + P] = 1.0 / 256
    c[:, K_HEAD:K_HEAD + P] = (i[:, None] // HD == i[None, :] // HD) / HD
    c[:, K_RESET:K_RESET + SEQ] = np.arange(SEQ)[None] % CHUNK != 0
    s, t = i[:, None] % CHUNK, np.arange(CHUNK)[None, :]
    for n, h in enumerate(LEVELS):
        same = s // (2 * h) == t // (2 * h)
        c[:, K_MASK + n * CHUNK:K_MASK + (n + 1) * CHUNK] = same & (s % (2 * h) < h) & (t % (2 * h) >= h)
    n = len(LEVELS)
    c[:, K_MASK + n * CHUNK:K_MASK + (n + 1) * CHUNK] = s == t
    for p in range(NT):
        q = META + P * p + i[:, None]
        k = np.concatenate([META + P * p - CHUNK + np.arange(CHUNK), np.arange(META), META + P * p + np.arange(P)])
        d = -np.abs(q - k[None, :]).astype(np.float32)
        d[CHUNK:, :CHUNK] = NEG
        d[:CHUNK, CHUNK + META + CHUNK:] = NEG
        c[:, K_DIST + p * DW:K_DIST + (p + 1) * DW] = d
    c[:, K_IOTA:K_IOTA + 64] = np.arange(64)[None]
    c[:, K_TOK:K_TOK + NT] = i[:, None] + P * np.arange(NT)[None]
    c[:, K_THR:K_THR + 7] = BC * np.arange(1, 8)[None]
    c[:, K_EPS] = EPS
    return c


def trunk(nc, x, meta_tokens, mix_norm, w_in, conv_dw_w, conv_dw_b, conv_ln_g, conv_ln_b, attn_sinks,
          hgrn_norm_g, w_out, ffn_norm, w_router_group, b_router_group, w_router_expert,
          b_router_expert, w_exp_gate, w_exp_up, w_exp_down, final_norm, table, normed, expert_out, out):
    ctx = ExitStack()
    with ctx:
        def sb(name, shape, dt=F32):
            return ctx.enter_context(nc.sbuf_tensor(name, shape, dt))

        def sem(name):
            return ctx.enter_context(nc.semaphore(name))

        bank = [ctx.enter_context(nc.psum_tensor(f"bank{i}", [P, 512], F32)) for i in range(8)]

        area_w = sb("area_w", [P, KT * D_IN])
        area_x = sb("area_x", [P, NT * D])
        area_h = sb("area_h", [P, KT * (META + SEQ)])
        area_m = sb("area_m", [P, KT * SEQ])
        area_g = sb("area_g", [P, 19264])
        cst = sb("cst", [P, K_ALL])
        cols = sb("cols", [P, 78])
        rows = sb("rows", [78, P])
        sink = sb("sink", [P, NQ])
        stat = sb("stat", [P, 64])
        rbias = sb("rbias", [P, NG + NE])

        at = [0]

        def cut(area, n, shape=None):
            a = area[:, at[0]:at[0] + n]
            at[0] += n
            return a

        w_in_sb = area_w[:, :].rearrange("p (k n) -> p k n", k=KT)
        w_out_sb = area_w[:, 0:KT * D].rearrange("p (k n) -> p k n", k=KT)
        xs = area_x[:, :].rearrange("p (j d) -> p j d", j=NT)
        hT = area_h[:, :].rearrange("p (k t) -> p k t", k=KT)
        mixT = area_m[:, :].rearrange("p (k t) -> p k t", k=KT)
        TT = META + SEQ
        glu = cut(area_g, 2 * (TAPS - 1 + TT)).rearrange("p (c t) -> p c t", c=2)
        qf = cut(area_g, 2 * SEQ).rearrange("p (c t) -> p c t", c=2)
        kf = cut(area_g, 2 * TT).rearrange("p (c t) -> p c t", c=2)
        lf = cut(area_g, 2 * TT).rearrange("p (c t) -> p c t", c=2)
        b = cut(area_g, 2 * TT).rearrange("p (c t) -> p c t", c=2)
        eb = cut(area_g, 2 * SEQ).rearrange("p (c t) -> p c t", c=2)
        qb = cut(area_g, 2 * SEQ).rearrange("p (c t) -> p c t", c=2)
        kb = cut(area_g, 2 * TT).rearrange("p (c t) -> p c t", c=2)
        lev = [area_x[:, n * 1024:(n + 1) * 1024].rearrange("p (c t) -> p c t", c=2) for n in range(4)]
        lev += [cut(area_g, 2 * SEQ).rearrange("p (c t) -> p c t", c=2) for n in range(2)]
        v2 = cut(area_g, NC_ * 128).rearrange("p (c i e) -> p c i e", c=NC_, i=2)
        v2m = cut(area_g, 128).rearrange("p (i e) -> p i e", i=2)
        qT = cut(area_g, 4 * SEQ).rearrange("p (c t) -> p c t", c=4)
        kT = cut(area_g, 2 * TT).rearrange("p (c t) -> p c t", c=2)
        va = cut(area_g, NT * P).rearrange("p (j e) -> p j e", j=NT)
        vp = cut(area_g, NT * P).rearrange("p (j e) -> p j e", j=NT)
        vm = cut(area_g, P)
        zt_flat = cut(area_g, 2 * TT)
        zt = zt_flat.rearrange("p (c t) -> p c t", c=2)
        meta_x = zt_flat[0:META, 0:D]
        gain = cut(area_g, D)
        gain_out = cut(area_g, D)
        wr = cut(area_g, KT * (NG + NE)).rearrange("p (k n) -> p k n", k=KT)
        at[0] = 0
        k2 = cut(area_h, NC_ * 128).rearrange("p (c i e) -> p c i e", c=NC_, i=2)
        k2m = cut(area_h, 128).rearrange("p (i e) -> p i e", i=2)
        state = cut(area_h, NC_ * 128).rearrange("p (c i e) -> p c i e", c=NC_, i=2)
        A = cut(area_h, 1024).rearrange("p (c t) -> p c t", c=2)
        osq = cut(area_h, 1024).rearrange("p (c t) -> p c t", c=2)
        at[0] = KT * D + 3 * KT * DE
        sc = [cut(area_w, 4 * DW).rearrange("p (h k) -> p h k", h=4) for _ in range(2)]
        pa = cut(area_w, 512)
        pb = cut(area_w, 512)
        sig = area_m[:, 2 * SEQ:2 * SEQ + 2 * TT].rearrange("p (c t) -> p c t", c=2)
        ed = [area_m[:, 2 * SEQ:4 * SEQ].rearrange("p (c t) -> p c t", c=2),
              area_m[:, 4 * SEQ:6 * SEQ].rearrange("p (c t) -> p c t", c=2)]
        dm = stat[:, 32:64].rearrange("p (c t) -> p c t", c=2)
        ident = cst[:, K_ID:K_ID + P]
        eps = cst[:, K_EPS:K_EPS + 1]
        one = cst[:, K_ONE:K_ONE + 1]
        ss, rstd = stat[:, 0:5], stat[:, 5:10]
        mx = [stat[:, 10:14], stat[:, 14:18]]
        rs = [stat[:, 18:22], stat[:, 22:26]]
        es = [stat[:, 26:30], area_w[:, KT * D + 3 * KT * DE + 8 * DW + 1024:KT * D + 3 * KT * DE + 8 * DW + 1028]]

        d_cst, d_par, d_meta, d_sink = sem("d_cst"), sem("d_par"), sem("d_meta"), sem("d_sink")
        d_x = [sem(f"d_x{j}") for j in range(NT)]
        d_win = [sem(f"d_win{i}") for i in range(8)]
        d_wout = [sem("d_wout0"), sem("d_wout1")]
        d_resid = sem("d_resid")
        sumsq = sem("sumsq"); rstd_ready = sem("rstd_ready"); xn_ready = sem("xn_ready")
        par_T = sem("par_T"); cols_ready = sem("cols_ready")
        xT_done = sem("xT_done"); metaT = sem("metaT"); hT_v = sem("hT_v"); hT_a = sem("hT_a")
        product = sem("product"); evac = sem("evac"); glu_done = sem("glu_done")
        a_step = sem("a_step"); v_step = sem("v_step")
        softplus = sem("softplus"); gates = sem("gates"); kf_ready = sem("kf_ready")
        b_ready = sem("b_ready"); eb_ready = sem("eb_ready"); lev_d = sem("lev_d"); lev_e = sem("lev_e"); lev_w = sem("lev_w")
        kb_ready = sem("kb_ready"); kbT = sem("kbT"); k2_a = sem("k2_a"); k2_v = sem("k2_v")
        u_done = sem("u_done"); state_done = sem("state_done"); g_done = sem("g_done"); g_used = sem("g_used")
        o_done = sem("o_done"); osq_done = sem("osq_done"); ms_done = sem("ms_done"); orstd = sem("orstd"); y_h = sem("y_h")
        conv_done = sem("conv_done"); mean_done = sem("mean_done"); cen_done = sem("cen_done")
        csq = sem("csq"); var_done = sem("var_done"); crstd = sem("crstd"); cnorm = sem("cnorm"); y_c = sem("y_c")
        s_done = sem("s_done"); s_ready = sem("s_ready"); p_exp = sem("p_exp"); p_ready = sem("p_ready")
        pT = sem("pT"); pa_ready = sem("pa_ready"); pb_ready = sem("pb_ready"); pv = sem("pv"); y_a = sem("y_a")
        den = sem("den"); pads = sem("pads")

        EW = KT * DE
        ring = [area_w[:, KT * D:KT * D + 3 * EW], area_w[:, 0:3 * EW], area_g[:, 0:3 * EW], area_g[:, 3 * EW:6 * EW]]
        ring = [ring[0], ring[2], ring[3], ring[1]]
        w_gate = [a[:, 0:EW].rearrange("p (k n) -> p k n", k=KT) for a in ring]
        w_up = [a[:, EW:2 * EW].rearrange("p (k n) -> p k n", k=KT) for a in ring]
        w_down = [a[:, 2 * EW:3 * EW].rearrange("p (f d) -> p f d", f=2) for a in ring]
        JUNK = KT * D + 3 * EW
        xf = area_h[:, 0:NT * D].rearrange("p (j d) -> p j d", j=NT)
        xg = [area_m[0:BC, i * D:(i + 1) * D] for i in range(2)]
        yb = [area_m[0:BC, (2 + i) * D:(3 + i) * D] for i in range(2)]
        xgT = [area_h[:, i * 512:(i + 1) * 512].rearrange("p (k t) -> p k t", k=KT) for i in range(2)]
        sg = [area_h[:, 1024 + i * 128:1152 + i * 128] for i in range(2)]
        aT = [area_h[:, 1280 + i * 128:1408 + i * 128] for i in range(2)]
        ye = [area_h[:, 0:NT * D].rearrange("p (j d) -> p j d", j=NT), area_m[:, :].rearrange("p (j d) -> p j d", j=NT)]
        at[0] = 6 * EW
        NR = NG + NE
        logit = cut(area_g, NT * NR).rearrange("p (j n) -> p j n", j=NT)
        glog, gexp = (cut(area_g, NT * NG).rearrange("p (j n) -> p j n", j=NT) for _ in range(2))
        t4, oh4 = (cut(area_g, NT * NG).rearrange("p (j n) -> p j n", j=NT) for _ in range(2))
        ev, t32, oh1, oh2, both, rank = (cut(area_g, NT * NE).rearrange("p (j n) -> p j n", j=NT) for _ in range(6))
        count, blocks, incl, first = (cut(area_g, NE) for _ in range(4))
        over = cut(area_g, NE * 7).rearrange("p (e m) -> p e m", e=NE)
        over4 = cut(area_g, NT * 7).rearrange("p (j m) -> p j m", j=NT)
        gm, gi, m1, i1, m2, i2, gsum, w1, w2, wd, qk, tokf, tokf2 = (cut(area_g, NT) for _ in range(13))
        rk, bk, ck = ([cut(area_g, NT) for _ in range(2)] for _ in range(3))
        slot_is = cut(area_g, 2 * NT * BC).rearrange("p (k j c) -> p k j c", k=2, j=NT)
        block_is = cut(area_g, 2 * NT * 2 * NBLK).rearrange("p (k j w b) -> p k j w b", k=2, j=NT, w=2)
        idx = cut(area_g, 2 * NBLK + 1 + 7).bitcast(I32)
        TW = NE + 2
        tab = cut(area_g, 3 * TW).bitcast(I32)
        ig = [cut(area_g, 1).bitcast(I32) for _ in range(2)]
        isc = [cut(area_g, 1).bitcast(I32) for _ in range(2)]
        assert at[0] <= 16924

        oproj = sem("oproj"); h2_done = sem("h2_done"); fstat = sem("fstat"); xf_ready = sem("xf_ready")
        d_norm = sem("d_norm"); xfT = sem("xfT"); hfT_a = sem("hfT_a"); hfT_v = sem("hfT_v"); d_rt = sem("d_rt"); d_gain = sem("d_gain")
        logits = sem("logits"); gdiff = sem("gdiff"); gprob = sem("gprob"); ediff = sem("ediff"); eprob = sem("eprob")
        picks = sem("picks"); ranks = sem("ranks"); match = sem("match"); slots = sem("slots"); routed = sem("routed")
        d_ring = [sem(f"d_ring{i}") for i in range(4)]
        d_xg = [sem(f"d_xg{i}") for i in range(2)]; d_sc = [sem(f"d_sc{i}") for i in range(2)]
        xgT_made = [sem(f"xgT_made{i}") for i in range(2)]; xgT_ready = [sem(f"xgT_ready{i}") for i in range(2)]
        gu_done = [sem(f"gu_done{i}") for i in range(2)]; sg_ready = [sem(f"sg_ready{i}") for i in range(2)]
        act_ready = [sem(f"act_ready{i}") for i in range(2)]; down_done = [sem(f"down_done{i}") for i in range(2)]
        y_half = [sem(f"y_half{i}") for i in range(2)]; y_rest = [sem(f"y_rest{i}") for i in range(2)]
        i_step = sem("i_step")
        d_ye = [sem(f"d_ye{j}") for j in range(NT)]; summed = sem("summed"); ostat = sem("ostat"); o_ready = sem("o_ready"); d_out = sem("d_out")

        passed = sem("passed")

        def expert_counts(eng, g, r):
            nb = eng.value_load(tab[0:1, bass.ds(g * 4 + r, 1)], min_val=1, max_val=SEQ // BC)
            own = eng.value_load(tab[0:1, bass.ds(g * 4 + (TW + r), 1)], min_val=0, max_val=NBLK)
            return nb, own

        PROD = (["gate0", "gate1", "a0", "a1", "hq0", "hq1", "hg0", "hg1", "hf0", "hf1", "k",
                 "v0", "v1", "v2", "v3", "vm", "q0", "q1", "q2", "q3"])
        WITH_META = ["gate0", "gate1", "a0", "a1", "hf0", "hf1", "k"]
        COL = {"gate0": C_GATE, "gate1": C_GATE + P, "a0": C_A, "a1": C_A + P, "hq0": C_HQ, "hq1": C_HQ + P,
               "hg0": C_HG, "hg1": C_HG + P, "hf0": C_HF, "hf1": C_HF + P, "k": C_K,
               "q0": C_Q, "q1": C_Q + P, "q2": C_Q + 2 * P, "q3": C_Q + 3 * P}
        LOADS = [(C_GATE, 256), (C_A, 256), (C_HQ, 256), (C_HG, 256), (C_HF, 256), (C_K, 256), (C_HI, 256), (C_Q, 512)]
        LOAD_OF = {"gate": 0, "a": 1, "hq": 2, "hg": 3, "hf": 4, "k": 5, "v": 6, "q": 7}
        EVAC = [n for n in PROD if n not in ("a0", "a1")]

        def made(n):
            return PROD.index(n) + 1

        def taken(n):
            return EVAC.index(n) + 1

        def pbank(n):
            return bank[PROD.index(n) % 4]

        def mcols(n):
            return bank[4 + WITH_META.index(n) % 2][:, 0:META]

        block = ctx.enter_context(nc.Block())

        @block.sync
        def _(sp):
            sp.dma_start(meta_x[:, :], meta_tokens).then_inc(d_meta, 16)
            for j in range(NT):
                sp.dma_start(xs[:, j, :], x[0, j * P:(j + 1) * P, :]).then_inc(d_x[j], 16)
            w_v = w_in[0].rearrange("(k p) n -> p k n", p=P)
            for i, (c0, n) in enumerate(LOADS):
                sp.dma_start(w_in_sb[:, :, c0:c0 + n], w_v[:, :, c0:c0 + n]).then_inc(d_win[i], 16)
            sp.wait_ge(product, len(PROD))
            wo_v = w_out[0].rearrange("(k p) n -> p k n", p=P)
            for i in range(2):
                sp.dma_start(w_out_sb[:, :, i * 512:(i + 1) * 512], wo_v[:, :, i * 512:(i + 1) * 512]).then_inc(d_wout[i], 16)
            sp.wait_ge(g_done, 14)
            sp.dma_start(xs, x[0].rearrange("(j p) d -> p j d", p=P)).then_inc(d_resid, 16)

            def load_expert(e, r):
                d = d_ring[r]
                sp.dma_start(w_gate[r], e(w_exp_gate).rearrange("(k p) n -> p k n", p=P)).then_inc(d, 16)
                sp.dma_start(w_up[r], e(w_exp_up).rearrange("(k p) n -> p k n", p=P)).then_inc(d, 16)
                sp.dma_start(w_down[r], e(w_exp_down).rearrange("(f p) n -> p f n", p=P)).then_inc(d, 16)

            load_expert(lambda w: w[0, 0], 0)
            sp.wait_ge(y_c, 2)
            sp.wait_ge(y_a, 2 * NT)
            for r in (1, 2):
                load_expert(lambda w: w[0, r], r)
            sp.wait_ge(oproj, 2 * NT)
            load_expert(lambda w: w[0, 3], 3)
            for j in range(NT):
                sp.wait_ge(xf_ready, j + 1)
                sp.dma_start(normed[j * P:(j + 1) * P, :], xf[:, j, :]).then_inc(d_norm, 16)
            sp.wait_ge(routed, 1)
            with sp.Fori(1, NE // 4) as g:
                for r in range(4):
                    n = sp.value_load(tab[0:1, bass.ds(g * 4 + (TW + r - 2), 1)], min_val=1, max_val=NBLK)
                    sp.wait_ge(down_done[r % 2], n)
                    sp.sem_inc(passed, 1)
                    load_expert(lambda w: w[0, bass.ds(g * 4 + r, 1)].rearrange("a k n -> (a k) n"), r)
            for u in range(2):
                n = sp.value_load(tab[0:1, TW + NE + u:TW + NE + u + 1], min_val=16, max_val=NBLK)
                sp.wait_ge(d_sc[u], n * 16 + 16)
                sp.sem_inc(passed, 1)
            for j in range(NT):
                for k in range(2):
                    sp.dma_start(ye[k][:, j, :], expert_out[k * SEQ + j * P:k * SEQ + (j + 1) * P, :]).then_inc(d_ye[j], 16)
            for j in range(NT):
                sp.wait_ge(o_ready, j + 1)
                sp.dma_start(out[0, j * P:(j + 1) * P, :], xs[:, j, :]).then_inc(d_out, 16)
            sp.wait_ge(d_out, 16 * NT)
            sp.wait_ge(d_norm, 16 * NT)

        @block.scalar
        def _(act):
            an = [0]

            def step(ins):
                an[0] += 1
                ins.then_inc(a_step, 1)
                act.wait_ge(a_step, an[0])

            act.dma_start(cst[:, :], table).then_inc(d_cst, 16)
            act.dma_start(rows[0:62, :], conv_dw_w[0].rearrange("t (c p) -> (t c) p", p=P)).then_inc(d_par, 16)
            act.dma_start(rows[62:70, :], mix_norm[0].rearrange("(c p) -> c p", p=P)).then_inc(d_par, 16)
            for i, a in enumerate((conv_dw_b, conv_ln_g, conv_ln_b, hgrn_norm_g)):
                act.dma_start(rows[70 + 2 * i:72 + 2 * i, :], a[0].rearrange("(c p) -> c p", p=P)).then_inc(d_par, 16)
            act.dma_start(sink[:, :], attn_sinks.to_broadcast([P, NQ])).then_inc(d_sink, 16)
            act.wait_ge(d_cst, 16)
            act.preload_act_table_set("natural_log_exp_and_others")
            for j in [4, 0, 1, 2, 3]:
                rws = META if j == 4 else P
                src = meta_x[:, :] if j == 4 else xs[:, j, :]
                act.wait_ge(d_meta if j == 4 else d_x[j], 16)
                junk = area_g[0:rws, 2 * (TAPS - 1 + TT):2 * (TAPS - 1 + TT) + D]
                step(nc.scalar.activation(junk, src, ACT.Square, accum_out=ss[0:rws, j:j + 1]))
                step(nc.scalar.activation(rstd[0:rws, j:j + 1], ss[0:rws, j:j + 1], ACT.Ln, bias=eps[0:rws], scale=1.0 / D))
                nc.scalar.activation(rstd[0:rws, j:j + 1], rstd[0:rws, j:j + 1], ACT.Exp, scale=-0.5).then_inc(rstd_ready, 1)
            act.wait_ge(rstd_ready, 5)
            act.wait_ge(xT_done, NT)
            act.wait_ge(cols_ready, 1)
            for k in range(1, KT, 2):
                nc.scalar.activation(hT[:, k, META:], bank[k][:, :], ACT.Copy, scale=cols[:, 62 + k:63 + k]).then_inc(hT_a, 1)
            for n in EVAC:
                act.wait_ge(product, made(n))
                src = pbank(n)
                i = int(n[1:]) if n[1:].isdigit() else int(n[-1]) if n[-1].isdigit() else 0
                if n.startswith("gate"):
                    nc.scalar.activation(sig[:, i, 0:META], mcols(n), ACT.Sigmoid).then_inc(a_step, 1); an[0] += 1
                    nc.scalar.activation(sig[:, i, META:], src[:, :], ACT.Sigmoid).then_inc(evac, 1)
                elif n.startswith("hq"):
                    nc.scalar.activation(qf[:, i, :], src[:, :], ACT.Silu).then_inc(evac, 1)
                elif n.startswith("hg"):
                    nc.scalar.activation(mixT[:, 6 + i, :], src[:, :], ACT.Silu).then_inc(evac, 1)
                elif n.startswith("hf"):
                    nc.scalar.activation(zt[:, i, 0:META], mcols(n), ACT.Identity).then_inc(a_step, 1); an[0] += 1
                    nc.scalar.activation(zt[:, i, META:], src[:, :], ACT.Identity).then_inc(evac, 1)
                    if i == 1:
                        act.wait_ge(evac, taken(n))
                        act.wait_ge(a_step, an[0])
                        act.preload_act_table_set("natural_log_exp_and_others")
                        step(nc.scalar.activation(lf, zt, ACT.Abs))
                        step(nc.scalar.activation(lf, lf, ACT.Exp, scale=-1.0))
                        nc.scalar.activation(b, lf, ACT.Ln, bias=one).then_inc(softplus, 1)
                        act.wait_ge(gates, 2)
                        nc.scalar.activation(kf, kf, ACT.Exp, scale=-1.0).then_inc(kf_ready, 1)
                elif n == "k":
                    for g in range(2):
                        for half in range(2):
                            dst, s = slice(half * HD, half * HD + HD), slice(g * HD, g * HD + HD)
                            nc.scalar.activation(kT[dst, g, 0:META], mcols(n)[s, :], ACT.Copy).then_inc(a_step, 1); an[0] += 1
                            last = nc.scalar.activation(kT[dst, g, META:], src[s, :], ACT.Copy)
                            if g == half == 1:
                                last.then_inc(evac, 1)
                            else:
                                last.then_inc(a_step, 1); an[0] += 1
                elif n == "vm":
                    act.wait_ge(pads, 1)
                    for j in range(1, NT):
                        nc.scalar.activation(vp[HD:HD + META, j, :], src[0:META, 0:P], ACT.Copy).then_inc(a_step, 1); an[0] += 1
                    nc.scalar.activation(vm[0:META, :], src[0:META, 0:P], ACT.Copy).then_inc(a_step, 1); an[0] += 1
                    s = src[0:META, P:P + 256].rearrange("p (i h e) -> p i h e", i=2, h=2)
                    nc.scalar.activation(v2m[0:META], s[:, :, 0, :], ACT.Copy).then_inc(a_step, 1); an[0] += 1
                    nc.scalar.activation(v2m[HD:HD + META], s[:, :, 1, :], ACT.Copy).then_inc(evac, 1)
                elif n.startswith("v"):
                    nc.scalar.activation(va[:, i, :], src[:, 0:P], ACT.Copy).then_inc(a_step, 1); an[0] += 1
                    if i + 1 < NT:
                        nc.scalar.activation(vp[0:HD, i + 1, :], src[HD:P, 0:P], ACT.Copy).then_inc(a_step, 1); an[0] += 1
                    s = src[:, P:P + 256].rearrange("p (i h e) -> p i h e", i=2, h=2)
                    for cp in range(2):
                        for hp in range(2):
                            last = nc.scalar.activation(v2[hp * HD:hp * HD + HD, 2 * i + cp, :, :],
                                                        s[cp * HD:cp * HD + HD, :, hp, :], ACT.Copy)
                            if cp == hp == 1:
                                last.then_inc(evac, 1)
                            else:
                                last.then_inc(a_step, 1); an[0] += 1
                else:
                    nc.scalar.activation(qT[:, i, :], src[:, :], ACT.Copy, scale=HD ** -0.5).then_inc(evac, 1)
                if n == "k":
                    act.wait_ge(b_ready, 1)
                    nc.scalar.activation(eb, b[:, :, META:], ACT.Exp).then_inc(eb_ready, 1)
                    act.wait_ge(lev_d, 1)
                    nc.scalar.activation(dm, dm, ACT.Exp).then_inc(a_step, 1); an[0] += 1
                    nc.scalar.activation(ed[0], ed[0], ACT.Exp).then_inc(lev_e, 1)
                if n in ("v0", "v1", "v2", "v3", "vm", "q0"):
                    l = ("v0", "v1", "v2", "v3", "vm", "q0").index(n)
                    act.wait_ge(lev_d, l + 2)
                    e = ed[(l + 1) % 2]
                    nc.scalar.activation(e, e, ACT.Exp).then_inc(lev_e, 1)
            act.wait_ge(kbT, 2)
            for ti in range(2):
                src = bank[5 + ti][:, :].rearrange("p (r h e) -> p r h e", r=4, h=2)
                for hp in range(2):
                    nc.scalar.activation(k2[hp * HD:hp * HD + HD, 0::2, ti, :], src[0:HD, :, hp, :], ACT.Copy).then_inc(k2_a, 1)
            act.wait_ge(cen_done, 2)
            nc.scalar.activation(osq, mixT[:, 0:2, :], ACT.Square).then_inc(csq, 1)
            act.wait_ge(var_done, 1)
            step(nc.scalar.activation(ed[0][:, 0, :], bank[4][:, :], ACT.Ln, bias=eps))
            nc.scalar.activation(ed[0][:, 0, :], ed[0][:, 0, :], ACT.Exp, scale=-0.5).then_inc(crstd, 1)
            act.wait_ge(o_done, 2)
            for ti in range(2):
                nc.scalar.activation(osq[:, ti, :], bank[ti][:, :], ACT.Square).then_inc(osq_done, 1)
            act.wait_ge(ms_done, 2)
            for ti in range(2):
                step(nc.scalar.activation(ed[1][:, ti, :], bank[2 + ti][:, :], ACT.Ln, bias=eps))
                nc.scalar.activation(ed[1][:, ti, :], ed[1][:, ti, :], ACT.Exp, scale=-0.5).then_inc(orstd, 1)

            def probs(u):
                act.wait_ge(s_ready, u + 1)
                i = u % 2
                for h in range(4):
                    lo = HD if u < 2 else 0
                    nc.scalar.activation(sc[i][:, h, lo:], sc[i][:, h, lo:], ACT.Exp, bias=mx[i][:, h:h + 1],
                                         accum_out=rs[i][:, h:h + 1]).then_inc(a_step, 1); an[0] += 1
                nc.scalar.activation(es[i], es[i], ACT.Exp).then_inc(p_exp, 1)

            def tile_a(u):
                act.wait_ge(pT, u + 1)
                if u >= 1:
                    act.wait_ge(pv, u)
                lo = META if u < 2 else HD + META
                nc.scalar.activation(pa[0:lo, :], bank[5][0:lo, :], ACT.Copy).then_inc(pa_ready, 1)

            def heads_out(u):
                act.wait_ge(pv, u + 1)
                p, g = u // 2, u % 2
                src = bank[7 - 3 * (u % 2)][:, 0:256].rearrange("p (i t) -> p i t", i=2)
                nc.scalar.activation(mixT[:, 2 + 2 * g:4 + 2 * g, p * P:(p + 1) * P], src, ACT.Copy).then_inc(y_a, 1)

            act.wait_ge(y_h, 2)
            act.wait_ge(cnorm, 2)
            U = 2 * NT
            probs(0)
            for u in range(U):
                if u + 1 < U:
                    probs(u + 1)
                tile_a(u)
                heads_out(u)
            for i in range(2):
                nc.scalar.activation(mixT[:, i, :], mixT[:, i, :], ACT.Silu, scale=cols[:, 72 + i:73 + i],
                                     bias=cols[:, 74 + i:75 + i]).then_inc(y_c, 1)

            act.preload_act_table_set("natural_log_exp_and_others")
            for j in range(NT):
                act.wait_ge(h2_done, 2 * j + 2)
                if j == 0:
                    act.wait_ge(oproj, 2 * NT)
                step(nc.scalar.activation(area_w[:, JUNK:JUNK + D], xs[:, j, :], ACT.Square, accum_out=ss[:, j:j + 1]))
                step(nc.scalar.activation(rstd[:, j:j + 1], ss[:, j:j + 1], ACT.Ln, bias=eps, scale=1.0 / D))
                nc.scalar.activation(rstd[:, j:j + 1], rstd[:, j:j + 1], ACT.Exp, scale=-0.5).then_inc(fstat, 1)
            for j in range(NT):
                act.wait_ge(xfT, j + 1)
                src = bank[2 * j + 1][:, :].rearrange("p (k t) -> p k t", k=4)
                nc.scalar.activation(mixT[:, 4:8, j * P:(j + 1) * P], src, ACT.Copy).then_inc(hfT_a, 1)
            act.wait_ge(gdiff, 1)
            nc.scalar.activation(gexp, gexp, ACT.Exp).then_inc(gprob, 1)
            act.wait_ge(ediff, 1)
            nc.scalar.activation(wd, wd, ACT.Exp).then_inc(eprob, 1)

            act.wait_ge(routed, 1)

            def block_act(u, n):
                act.wait_ge(gu_done[u], n + 1)
                nc.scalar.activation(sg[u], bank[2 + u][:, 0:2 * BC], ACT.Silu).then_inc(sg_ready[u], 1)
                act.wait_ge(down_done[u], n + 1)
                act.wait_ge(d_sc[u], n * 16 + 16)
                nc.scalar.activation(yb[u][:, 0:512], bank[4 + 2 * u][0:BC, :], ACT.Copy).then_inc(y_half[u], 1)

            with act.Fori(0, NE // 4) as g:
                for r in range(4):
                    nb, own = expert_counts(act, g, r)
                    block_act(r % 2, own)
                    with act.If(nb > 1):
                        with act.Fori(1, nb) as i:
                            block_act(r % 2, own + i)
            act.preload_act_table_set("natural_log_exp_and_others")
            for j in range(NT):
                act.wait_ge(summed, j + 1)
                step(nc.scalar.activation(area_w[:, JUNK:JUNK + D], xs[:, j, :], ACT.Square, accum_out=ss[:, j:j + 1]))
                step(nc.scalar.activation(rstd[:, j:j + 1], ss[:, j:j + 1], ACT.Ln, bias=eps, scale=1.0 / D))
                nc.scalar.activation(rstd[:, j:j + 1], rstd[:, j:j + 1], ACT.Exp, scale=-0.5).then_inc(ostat, 1)

        @block.vector
        def _(dve):
            vn = [0]

            def step(ins):
                vn[0] += 1
                ins.then_inc(v_step, 1)
                dve.wait_ge(v_step, vn[0])

            def mark(ins):
                vn[0] += 1
                ins.then_inc(v_step, 1)
                return vn[0]

            V = nc.vector
            mark(V.memset(glu[:, :, 0:TAPS - 1], 0.0))
            V.memset(vp[:, :, :], 0.0).then_inc(pads, 1)
            dve.wait_ge(par_T, 1)
            V.tensor_copy(cols[:, :], bank[6][:, 0:78]).then_inc(cols_ready, 1)
            dve.wait_ge(cols_ready, 1)
            for n, j in enumerate([4, 0, 1, 2, 3]):
                dve.wait_ge(rstd_ready, n + 1)
                if j == 4:
                    V.tensor_scalar(meta_x[:, :], meta_x[:, :], rstd[0:META, 4:5], None, ALU.mult).then_inc(xn_ready, 1)
                else:
                    V.tensor_scalar(xs[:, j, :], xs[:, j, :], rstd[:, j:j + 1], None, ALU.mult).then_inc(xn_ready, 1)
                if j == 0:
                    dve.wait_ge(metaT, 1)
                    V.tensor_tensor(hT[:, :, 0:META], bank[7][:, 0:P].rearrange("p (k t) -> p k t", k=KT),
                                    cols[:, 62:70].unsqueeze(2).to_broadcast([P, KT, META]), ALU.mult).then_inc(hT_v, 1)
            dve.wait_ge(xT_done, NT)
            for k in range(0, KT, 2):
                V.tensor_scalar(hT[:, k, META:], bank[k][:, :], cols[:, 62 + k:63 + k], None, ALU.mult).then_inc(hT_v, 1)
            dve.wait_ge(evac, taken("gate1"))
            for i in range(2):
                n = f"a{i}"
                dve.wait_ge(product, made(n))
                mark(V.tensor_tensor(glu[:, i, TAPS - 1:TAPS - 1 + META], mcols(n), sig[:, i, 0:META], ALU.mult))
                V.tensor_tensor(glu[:, i, TAPS - 1 + META:], pbank(n)[:, :], sig[:, i, META:], ALU.mult).then_inc(glu_done, 1)
            dve.wait_ge(glu_done, 2)
            dve.wait_ge(v_step, vn[0])
            last = [0, 0]
            for t in range(TAPS):
                for i in range(2):
                    src = glu[:, i, META + t:META + t + SEQ]
                    w = cols[:, 2 * t + i:2 * t + i + 1]
                    if t == 0:
                        last[i] = mark(V.tensor_scalar(mixT[:, i, :], src, w, cols[:, 70 + i:71 + i], ALU.mult, ALU.add))
                    else:
                        dve.wait_ge(v_step, last[i])
                        ins = V.scalar_tensor_tensor(out=mixT[:, i, :], in0=src, scalar=w, in1=mixT[:, i, :],
                                                     op0=ALU.mult, op1=ALU.add)
                        if t == TAPS - 1:
                            ins.then_inc(conv_done, 1)
                        else:
                            last[i] = mark(ins)
            dve.wait_ge(softplus, 1)
            V.scalar_tensor_tensor(out=lf, in0=zt, scalar=0.0, in1=b, op0=ALU.min, op1=ALU.subtract).then_inc(gates, 1)
            V.scalar_tensor_tensor(out=kf, in0=zt, scalar=0.0, in1=b, op0=ALU.max, op1=ALU.add).then_inc(gates, 1)
            dve.wait_ge(gates, 2)
            for i in range(2):
                mark(V.tensor_tensor_scan(b[:, i, 0:META], cst[:, K_ONE:K_ONE + META], lf[:, i, 0:META], 0.0, ALU.mult, ALU.add))
                ins = V.tensor_tensor_scan(b[:, i, META:], cst[:, K_RESET:K_RESET + SEQ], lf[:, i, META:], 0.0, ALU.mult, ALU.add)
                if i == 0:
                    mark(ins)
                else:
                    ins.then_inc(b_ready, 1)
            dve.wait_ge(b_ready, 1)
            dve.wait_ge(v_step, vn[0])
            bc = b[:, :, META:].rearrange("p i (c t) -> p i c t", t=CHUNK)
            mark(V.tensor_tensor(dm, b[:, :, META - 1:META].to_broadcast([P, 2, META]), b[:, :, 0:META], ALU.subtract))
            V.tensor_tensor(ed[0].rearrange("p i (c t) -> p i c t", t=CHUNK),
                            bc[:, :, :, CHUNK - 1:CHUNK].to_broadcast([P, 2, NC_, CHUNK]), bc, ALU.subtract).then_inc(lev_d, 1)

            def level_decay(l):
                h = LEVELS[l]
                e = ed[(l + 1) % 2].rearrange("p i (c t) -> p i c t", t=2 * h)
                bl = b[:, :, META:].rearrange("p i (c t) -> p i c t", t=2 * h)
                mid = bl[:, :, :, h - 1:h].to_broadcast([P, 2, SEQ // (2 * h), h])
                mark(V.tensor_tensor(e[:, :, :, 0:h], mid, bl[:, :, :, 0:h], ALU.subtract))
                V.tensor_tensor(e[:, :, :, h:], bl[:, :, :, h:], mid, ALU.subtract).then_inc(lev_d, 1)

            def level_pair(l):
                h = LEVELS[l]
                dve.wait_ge(lev_e, l + 2)
                e = ed[(l + 1) % 2].rearrange("p i (c t) -> p i c t", t=2 * h)
                w = lev[l].rearrange("p i (c t) -> p i c t", t=2 * h)
                kk = kf[:, :, META:].rearrange("p i (c t) -> p i c t", t=2 * h)
                qq = qf.rearrange("p i (c t) -> p i c t", t=2 * h)
                mark(V.tensor_tensor(w[:, :, :, 0:h], kk[:, :, :, 0:h], e[:, :, :, 0:h], ALU.mult))
                V.tensor_tensor(w[:, :, :, h:], qq[:, :, :, h:], e[:, :, :, h:], ALU.mult).then_inc(lev_w, 1)
                dve.wait_ge(lev_w, l + 1)
                dve.wait_ge(v_step, vn[0])

            level_decay(0)
            dve.wait_ge(lev_e, 1)
            dve.wait_ge(kf_ready, 1)
            mark(V.tensor_tensor(kb[:, :, 0:META], kf[:, :, 0:META], dm, ALU.mult))
            V.tensor_tensor(kb[:, :, META:], kf[:, :, META:], ed[0], ALU.mult).then_inc(kb_ready, 1)
            dve.wait_ge(kb_ready, 1)
            for l in range(len(LEVELS)):
                if l + 1 < len(LEVELS):
                    level_decay(l + 1)
                level_pair(l)
            dve.wait_ge(eb_ready, 1)
            mark(V.tensor_tensor(qb, qf, eb, ALU.mult))
            dve.wait_ge(kbT, 2)
            for ti in range(2):
                src = bank[5 + ti][:, :].rearrange("p (r h e) -> p r h e", r=4, h=2)
                for hp in range(2):
                    V.tensor_copy(k2[hp * HD:hp * HD + HD, 1::2, ti, :], src[HD:P, :, hp, :]).then_inc(k2_v, 1)
            src = bank[7][0:META, 0:256].rearrange("p (i h e) -> p i h e", i=2, h=2)
            for hp in range(2):
                V.tensor_copy(k2m[hp * HD:hp * HD + META, :, :], src[:, :, hp, :]).then_inc(k2_v, 1)
            dve.wait_ge(u_done, 1)
            step(V.tensor_copy(state[:, 0, :, :], bank[0][:, 0:P].rearrange("p (i e) -> p i e", i=2)))
            for c in range(1, NC_):
                u = bank[c // 4][:, (c % 4) * P:(c % 4) * P + P].rearrange("p (i e) -> p i e", i=2)
                for i in range(2):
                    ins = V.scalar_tensor_tensor(out=state[:, c, i, :], in0=state[:, c - 1, i, :],
                                                 scalar=eb[:, i, c * CHUNK - 1:c * CHUNK], in1=u[:, i, :],
                                                 op0=ALU.mult, op1=ALU.add)
                    if i == 0:
                        mark(ins)
                    elif c < NC_ - 1:
                        step(ins)
                    else:
                        ins.then_inc(state_done, 1)
            nl = len(LEVELS)
            for n in range(2 * (nl + 1)):
                ti, l = n % 2, (nl - n // 2)
                dve.wait_ge(g_done, n + 1)
                m = cst[:, K_MASK + l * CHUNK:K_MASK + (l + 1) * CHUNK].unsqueeze(1).to_broadcast([P, NC_, CHUNK])
                g = bank[2 + n % 2][:, :].rearrange("p (c t) -> p c t", t=CHUNK)
                a = A[:, ti, :].rearrange("p (c t) -> p c t", t=CHUNK)
                if n >= 2:
                    dve.wait_ge(g_used, n - 1)
                if l == nl:
                    V.tensor_tensor(a, g, m, ALU.mult).then_inc(g_used, 1)
                else:
                    V.copy_predicated(a, m.bitcast(I32), g).then_inc(g_used, 1)
            dve.wait_ge(mean_done, 1)
            for i in range(2):
                V.tensor_tensor(mixT[:, i, :], mixT[:, i, :], bank[7][:, :], ALU.subtract).then_inc(cen_done, 1)
            dve.wait_ge(crstd, 1)
            for i in range(2):
                V.tensor_tensor(mixT[:, i, :], mixT[:, i, :], ed[0][:, 0, :], ALU.mult).then_inc(cnorm, 1)
            for ti in range(2):
                dve.wait_ge(orstd, ti + 1)
                step(V.tensor_tensor(ed[1][:, ti, :], bank[ti][:, :], ed[1][:, ti, :], ALU.mult))
                V.scalar_tensor_tensor(out=mixT[:, 6 + ti, :], in0=ed[1][:, ti, :], scalar=cols[:, 76 + ti:77 + ti],
                                       in1=mixT[:, 6 + ti, :], op0=ALU.mult, op1=ALU.mult).then_inc(y_h, 1)

            def biased(u):
                dve.wait_ge(s_done, u + 1)
                p, g, i = u // 2, u % 2, u % 2
                if u >= 2:
                    dve.wait_ge(pT, u - 1)
                lo = HD if p == 0 else 0
                dist = cst[:, K_DIST + p * DW + lo:K_DIST + (p + 1) * DW]
                for h in range(4):
                    s = bank[2 * i + h % 2][:, (h // 2) * DW + lo:(h // 2 + 1) * DW]
                    mark(V.scalar_tensor_tensor(out=sc[i][:, h, lo:], in0=dist, scalar=2.0 ** -(4 * g + h + 1), in1=s,
                                                op0=ALU.mult, op1=ALU.add))
                dve.wait_ge(v_step, vn[0])
                if u < 2:
                    dve.wait_ge(d_sink, 16)
                step(V.tensor_reduce(mx[i], sc[i][:, :, lo:], AX, ALU.max))
                step(V.tensor_tensor(mx[i], mx[i], sink[:, 4 * g:4 * g + 4], ALU.max))
                step(V.tensor_scalar(mx[i], mx[i], -1.0, None, ALU.mult))
                V.tensor_tensor(es[i], mx[i], sink[:, 4 * g:4 * g + 4], ALU.add).then_inc(s_ready, 1)

            def normal(u):
                i = u % 2
                lo = HD if u < 2 else 0
                dve.wait_ge(p_exp, u + 1)
                step(V.tensor_tensor(rs[i], rs[i], es[i], ALU.add))
                step(V.reciprocal(rs[i], rs[i]))
                V.tensor_tensor(sc[i][:, :, lo:], sc[i][:, :, lo:], rs[i].unsqueeze(2).to_broadcast([P, 4, DW - lo]), ALU.mult)\
                    .then_inc(p_ready, 1)

            def tile_b(u):
                dve.wait_ge(pT, u + 1)
                if u >= 1:
                    dve.wait_ge(pv, u)
                V.tensor_copy(pb, bank[6][:, :]).then_inc(pb_ready, 1)

            U = 2 * NT
            biased(0)
            for u in range(U):
                if u + 1 < U:
                    biased(u + 1)
                normal(u)
                tile_b(u)

            dve.wait_ge(d_resid, 16)
            for j in range(NT):
                for n in range(2):
                    dve.wait_ge(oproj, 2 * j + n + 1)
                    h = xs[:, j, n * 512:(n + 1) * 512]
                    V.tensor_tensor(h, h, bank[2 * j + n][:, :], ALU.add).then_inc(h2_done, 1)
                if j == 0:
                    dve.wait_ge(d_gain, 48)
                dve.wait_ge(h2_done, 2 * j + 2)
                dve.wait_ge(fstat, j + 1)
                V.scalar_tensor_tensor(out=xf[:, j, :], in0=xs[:, j, :], scalar=rstd[:, j:j + 1], in1=gain,
                                       op0=ALU.mult, op1=ALU.mult).then_inc(xf_ready, 1)
            for j in range(NT):
                dve.wait_ge(xfT, j + 1)
                src = bank[2 * j][:, :].rearrange("p (k t) -> p k t", k=4)
                V.tensor_copy(mixT[:, 0:4, j * P:(j + 1) * P], src).then_inc(hfT_v, 1)

            def first_max(v, n, m, i, t, oh):
                iota = cst[:, K_IOTA:K_IOTA + n].unsqueeze(1).to_broadcast([P, NT, n])
                step(V.tensor_reduce(m, v, AX, ALU.max))
                step(V.tensor_tensor(t, v, m.unsqueeze(2).to_broadcast([P, NT, n]), ALU.is_equal))
                step(V.scalar_tensor_tensor(out=t, in0=t, scalar=-float(FAR), in1=iota, op0=ALU.mult, op1=ALU.add))
                step(V.tensor_reduce(i, t, AX, ALU.min))
                step(V.tensor_tensor(oh, t, i.unsqueeze(2).to_broadcast([P, NT, n]), ALU.is_equal))

            dve.wait_ge(logits, NT)
            step(V.tensor_tensor(logit, bank[0][:, 0:NT * NR].rearrange("p (j n) -> p j n", j=NT),
                                 rbias[:, :].unsqueeze(1).to_broadcast([P, NT, NR]), ALU.add))
            step(V.tensor_copy(glog, logit[:, :, 0:NG]))
            first_max(glog, NG, gm, gi, t4, oh4)
            V.tensor_tensor(gexp, glog, gm.unsqueeze(2).to_broadcast([P, NT, NG]), ALU.subtract).then_inc(gdiff, 1)
            step(V.tensor_scalar(oh4, oh4, -NEG, NEG, ALU.mult, ALU.add))
            for j in range(NT):
                ins = V.tensor_tensor(ev[:, j, :].rearrange("p (g e) -> p g e", g=NG),
                                      logit[:, j, NG:].rearrange("p (g e) -> p g e", g=NG),
                                      oh4[:, j, :].unsqueeze(2).to_broadcast([P, NG, EPG]), ALU.add)
                mark(ins)
            dve.wait_ge(v_step, vn[0])
            first_max(ev, NE, m1, i1, t32, oh1)
            step(V.scalar_tensor_tensor(out=ev, in0=oh1, scalar=3 * NEG, in1=ev, op0=ALU.mult, op1=ALU.add))
            first_max(ev, NE, m2, i2, t32, oh2)
            V.tensor_tensor(wd, m2, m1, ALU.subtract).then_inc(ediff, 1)
            V.tensor_tensor(both, oh1, oh2, ALU.add).then_inc(picks, 1)
            dve.wait_ge(gprob, 1)
            step(V.tensor_reduce(gsum, gexp, AX, ALU.add))
            dve.wait_ge(eprob, 1)
            step(V.tensor_scalar(w1, wd, 1.0, None, ALU.add))
            step(V.tensor_tensor(w1, w1, gsum, ALU.mult))
            step(V.reciprocal(w1, w1))
            step(V.tensor_tensor(w2, w1, wd, ALU.mult))
            dve.wait_ge(ranks, 1)
            mark(V.tensor_copy(rank, bank[1][:, 0:NT * NE].rearrange("p (j e) -> p j e", j=NT)))
            step(V.tensor_copy(count, bank[1][:, NT * NE:NT * NE + NE]))
            thr = cst[:, K_THR:K_THR + 7]
            step(V.tensor_tensor(over, count.unsqueeze(2).to_broadcast([P, NE, 7]),
                                 thr.unsqueeze(1).to_broadcast([P, NE, 7]), ALU.is_gt))
            step(V.tensor_reduce(blocks, over, AX, ALU.add))
            step(V.tensor_scalar(blocks, blocks, 1.0, None, ALU.add))
            ones = cst[:, K_ONE:K_ONE + NE]
            step(V.tensor_tensor_scan(incl, ones, blocks, 0.0, ALU.mult, ALU.add))
            step(V.tensor_tensor(first, incl, blocks, ALU.subtract))
            mark(V.tensor_copy(tab[0:1, 0:NE], blocks[0:1, :]))
            mark(V.memset(tab[0:1, 2 * TW:2 * TW + 1], 0))
            step(V.tensor_copy(tab[0:1, 2 * TW + 1:2 * TW + 1 + NE], incl[0:1, :]))
            for u in range(2):
                step(V.tensor_tensor_scan(incl[:, u::2], ones[:, 0:NE // 2], blocks[:, u::2], 0.0, ALU.mult, ALU.add))
            mark(V.memset(tab[0:1, TW:TW + 2], 0))
            mark(V.tensor_copy(tab[0:1, TW + 2:TW + 2 + NE], incl[0:1, :]))
            for k, oh in ((0, oh1), (1, oh2)):
                step(V.tensor_tensor(t32, oh, rank, ALU.mult))
                step(V.tensor_reduce(rk[k], t32, AX, ALU.add))
                step(V.tensor_tensor(t32, oh, first.unsqueeze(1).to_broadcast([P, NT, NE]), ALU.mult))
                step(V.tensor_reduce(bk[k], t32, AX, ALU.add))
                step(V.tensor_tensor(over4, rk[k].unsqueeze(2).to_broadcast([P, NT, 7]),
                                     thr.unsqueeze(1).to_broadcast([P, NT, 7]), ALU.is_ge))
                step(V.tensor_reduce(qk, over4, AX, ALU.add))
                mark(V.tensor_tensor(bk[k], bk[k], qk, ALU.add))
                step(V.scalar_tensor_tensor(out=ck[k], in0=qk, scalar=-float(BC), in1=rk[k], op0=ALU.mult, op1=ALU.add))
            step(V.tensor_scalar(tokf, cst[:, K_TOK:K_TOK + NT], -float(FAR), None, ALU.add))
            step(V.tensor_scalar(tokf2, tokf, float(SEQ), None, ALU.add))
            for k in range(2):
                for j in range(NT):
                    mark(V.tensor_scalar(slot_is[:, k, j, :], cst[:, K_IOTA:K_IOTA + BC], ck[k][:, j:j + 1], None, ALU.is_equal))
                    for w, v in ((0, tokf), (1, tokf2 if k else tokf)):
                        ins = V.tensor_scalar(block_is[:, k, j, w, :], cst[:, K_IOTA:K_IOTA + NBLK], bk[k][:, j:j + 1],
                                              v[:, j:j + 1], ALU.is_equal, ALU.mult)
                        mark(ins)
            dve.wait_ge(v_step, vn[0])
            V.memset(idx[0:BC, NBLK:NBLK + 1], FAR).then_inc(match, 1)
            dve.wait_ge(slots, 1)
            mark(V.tensor_scalar(idx[0:BC, 0:NBLK], bank[2][0:BC, 0:NBLK], float(FAR), None, ALU.add))
            mark(V.tensor_scalar(idx[0:BC, NBLK + 1:2 * NBLK + 1], bank[2][0:BC, NBLK:2 * NBLK], float(FAR), None, ALU.add))
            dve.wait_ge(v_step, vn[0])
            V.memset(count[0:1, 0:1], 0.0).then_inc(routed, 1)

            def block_dve(u, n):
                dve.wait_ge(xgT_made[u], n + 2)
                V.tensor_copy(xgT[u], bank[u][:, :].rearrange("p (k t) -> p k t", k=KT)).then_inc(xgT_ready[u], 1)
                dve.wait_ge(sg_ready[u], n + 1)
                V.tensor_tensor(aT[u], sg[u], bank[2 + u][:, 2 * BC:4 * BC], ALU.mult).then_inc(act_ready[u], 1)
                dve.wait_ge(down_done[u], n + 1)
                dve.wait_ge(d_sc[u], n * 16 + 16)
                V.tensor_copy(yb[u][:, 512:], bank[5 + 2 * u][0:BC, :]).then_inc(y_rest[u], 1)

            with dve.Fori(0, NE // 4) as g:
                for r in range(4):
                    nb, own = expert_counts(dve, g, r)
                    block_dve(r % 2, own)
                    with dve.If(nb > 1):
                        with dve.Fori(1, nb) as i:
                            block_dve(r % 2, own + i)
            for j in range(NT):
                dve.wait_ge(d_ye[j], 32)
                step(V.scalar_tensor_tensor(out=xs[:, j, :], in0=ye[0][:, j, :], scalar=w1[:, j:j + 1], in1=xs[:, j, :],
                                            op0=ALU.mult, op1=ALU.add))
                V.scalar_tensor_tensor(out=xs[:, j, :], in0=ye[1][:, j, :], scalar=w2[:, j:j + 1], in1=xs[:, j, :],
                                       op0=ALU.mult, op1=ALU.add).then_inc(summed, 1)
            for j in range(NT):
                dve.wait_ge(ostat, j + 1)
                V.scalar_tensor_tensor(out=xs[:, j, :], in0=xs[:, j, :], scalar=rstd[:, j:j + 1], in1=gain_out,
                                       op0=ALU.mult, op1=ALU.mult).then_inc(o_ready, 1)

        @block.tensor
        def _(pe):
            T = nc.tensor
            pe.wait_ge(d_cst, 16)
            pe.wait_ge(d_par, 96)
            T.transpose(bank[6][:, 0:78], rows[:, :], ident[0:78, 0:78]).then_inc(par_T, 1)
            pe.wait_ge(xn_ready, 1)
            for k in range(KT):
                ins = T.transpose(bank[7][:, k * META:(k + 1) * META], meta_x[:, k * P:(k + 1) * P], ident[0:META, 0:META])
            ins.then_inc(metaT, 1)
            for j in range(NT):
                pe.wait_ge(xn_ready, j + 2)
                if j == 0:
                    pe.wait_ge(cols_ready, 1)
                    pe.wait_ge(hT_v, 1)
                for k in range(KT):
                    ins = T.transpose(bank[k][:, j * P:(j + 1) * P], xs[:, j, k * P:(k + 1) * P], ident)
                ins.then_inc(xT_done, 1)
            pe.wait_ge(hT_v, 5)
            pe.wait_ge(hT_a, 4)

            def freed(n):
                i = PROD.index(n) - 4
                old = [PROD[i]] if i >= 0 else []
                if n in WITH_META and WITH_META.index(n) >= 2:
                    old.append(WITH_META[WITH_META.index(n) - 2])
                for o in old:
                    if o[0] == "a":
                        pe.wait_ge(glu_done, int(o[1]) + 1)
                    else:
                        pe.wait_ge(evac, taken(o))

            def product_of(n):
                freed(n)
                out_b = pbank(n)
                if n[0] == "v":
                    pe.wait_ge(d_win[5], 16)
                    pe.wait_ge(d_win[6], 16)
                    rws = META if n == "vm" else P
                    t0 = 0 if n == "vm" else META + P * int(n[1])
                    for c0, n0, w in ((C_V, 0, P), (C_HI, P, 256)):
                        for k in range(KT):
                            ins = T.matmul(out_b[0:rws, n0:n0 + w], hT[:, k, t0:t0 + rws], w_in_sb[:, k, c0:c0 + w],
                                           start=(k == 0), stop=(k == KT - 1))
                else:
                    pe.wait_ge(d_win[LOAD_OF[n.rstrip("0123")]], 16)
                    for k in range(KT):
                        w = w_in_sb[:, k, COL[n]:COL[n] + P]
                        ins = T.matmul(out_b[:, :], w, hT[:, k, META:], start=(k == 0), stop=(k == KT - 1))
                        if n in WITH_META:
                            ins = T.matmul(mcols(n), w, hT[:, k, 0:META], start=(k == 0), stop=(k == KT - 1))
                ins.then_inc(product, 1)

            for n in PROD:
                product_of(n)

            pe.wait_ge(kb_ready, 1)
            for ti in range(2):
                for r in range(4):
                    T.transpose(bank[5 + ti][:, r * P:(r + 1) * P], kb[:, ti, META + r * P:META + (r + 1) * P], ident)
                ins = T.transpose(bank[7][0:META, ti * P:(ti + 1) * P], kb[:, ti, 0:META], ident)
                ins.then_inc(kbT, 1)
            pe.wait_ge(evac, len(EVAC))
            pe.wait_ge(k2_a, 4)
            pe.wait_ge(k2_v, 6)
            for c in range(NC_):
                o = bank[c // 4][:, (c % 4) * P:(c % 4) * P + P].rearrange("p (i e) -> p i e", i=2)
                for ti in range(2):
                    for hp in range(2):
                        s = slice(hp * HD, hp * HD + HD)
                        if c == 0:
                            sm = slice(hp * HD, hp * HD + META)
                            ins = T.matmul(o[s, ti, :], k2m[sm, ti, :], v2m[sm, ti, :], start=True, stop=True)
                        else:
                            ins = T.matmul(o[s, ti, :], k2[s, c - 1, ti, :], v2[s, c - 1, ti, :], start=True, stop=True)
            ins.then_inc(u_done, 1)
            pe.wait_ge(conv_done, 2)
            mean = cst[:, K_MEAN:K_MEAN + P]
            for i in range(2):
                ins = T.matmul(bank[7][:, :], mean, mixT[:, i, :], start=(i == 0), stop=(i == 1))
            ins.then_inc(mean_done, 1)
            nl = len(LEVELS)
            pe.wait_ge(kf_ready, 1)
            for n in range(2 * (nl + 1)):
                ti, l = n % 2, (nl - n // 2)
                if l < nl:
                    pe.wait_ge(lev_w, l + 1)
                if n >= 2:
                    pe.wait_ge(g_used, n - 1)
                for c in range(NC_):
                    for hp in range(2):
                        s = slice(hp * HD, hp * HD + HD)
                        t = slice(c * CHUNK, (c + 1) * CHUNK)
                        if l == nl:
                            kk, qq = kf[s, ti, META + c * CHUNK:META + (c + 1) * CHUNK], qf[s, ti, t]
                        else:
                            kk = qq = lev[l][s, ti, t]
                        ins = T.matmul(bank[2 + n % 2][s, t], kk, qq, start=True, stop=True)
                ins.then_inc(g_done, 1)
            pe.wait_ge(csq, 1)
            for i in range(2):
                ins = T.matmul(bank[4][:, :], mean, osq[:, i, :], start=(i == 0), stop=(i == 1))
            ins.then_inc(var_done, 1)
            pe.wait_ge(g_used, 2 * (nl + 1))
            pe.wait_ge(state_done, 1)
            for ti in range(2):
                for c in range(NC_):
                    for hp in range(2):
                        s = slice(hp * HD, hp * HD + HD)
                        t = slice(c * CHUNK, (c + 1) * CHUNK)
                        T.matmul(bank[ti][s, t], v2[s, c, ti, :], A[s, ti, t], start=True, stop=False)
                        ins = T.matmul(bank[ti][s, t], state[s, c, ti, :], qb[s, ti, t], start=False, stop=True)
                ins.then_inc(o_done, 1)
            for ti in range(2):
                pe.wait_ge(osq_done, ti + 1)
                T.matmul(bank[2 + ti][:, :], cst[:, K_HEAD:K_HEAD + P], osq[:, ti, :], start=True, stop=True).then_inc(ms_done, 1)

            def scores(u):
                p, g, i = u // 2, u % 2, u % 2
                if u >= 2:
                    pe.wait_ge(s_ready, u - 1)
                for h in range(4):
                    s = slice((h % 2) * HD, (h % 2) * HD + HD)
                    q = qT[s, 2 * g + h // 2, p * P:(p + 1) * P]
                    o = bank[2 * i + h % 2][:, (h // 2) * DW:(h // 2 + 1) * DW]
                    t0 = META + p * P
                    if p:
                        T.matmul(o[:, 0:HD], q, kT[s, g, t0 - CHUNK:t0], start=True, stop=True)
                    T.matmul(o[:, HD:HD + META], q, kT[s, g, 0:META], start=True, stop=True)
                    ins = T.matmul(o[:, HD + META:], q, kT[s, g, t0:t0 + P], start=True, stop=True)
                ins.then_inc(s_done, 1)

            def turn(u):
                pe.wait_ge(p_ready, u + 1)
                i = u % 2
                if u >= 1:
                    pe.wait_ge(pa_ready, u)
                    pe.wait_ge(pb_ready, u)
                lo = HD if u < 2 else 0
                for h in range(4):
                    T.transpose(bank[5][0:HD + META - lo, h * P:(h + 1) * P], sc[i][:, h, lo:HD + META], ident)
                    ins = T.transpose(bank[6][:, h * P:(h + 1) * P], sc[i][:, h, HD + META:], ident)
                ins.then_inc(pT, 1)

            def values(u):
                p, g = u // 2, u % 2
                pe.wait_ge(pa_ready, u + 1)
                pe.wait_ge(pb_ready, u + 1)
                if u >= 2:
                    pe.wait_ge(y_a, u - 1)
                for h in range(4):
                    o = bank[7 - 3 * (u % 2)][(h % 2) * HD:(h % 2) * HD + HD, (h // 2) * P:(h // 2 + 1) * P]
                    e = slice(g * HD, g * HD + HD)
                    if p == 0:
                        T.matmul(o, vm[0:META, e], pa[0:META, h * P:(h + 1) * P], start=True, stop=False)
                    else:
                        T.matmul(o, vp[0:HD + META, p, e], pa[0:HD + META, h * P:(h + 1) * P], start=True, stop=False)
                    ins = T.matmul(o, va[:, p, e], pb[:, h * P:(h + 1) * P], start=False, stop=True)
                ins.then_inc(pv, 1)

            pe.wait_ge(y_h, 2)
            pe.wait_ge(cen_done, 2)
            U = 2 * NT
            scores(0)
            for u in range(U):
                if u + 1 < U:
                    scores(u + 1)
                turn(u)
                values(u)

            for i in range(2):
                pe.wait_ge(d_wout[i], 16)
            pe.wait_ge(y_c, 2)
            pe.wait_ge(y_a, 2 * NT)
            for j in range(NT):
                for n in range(2):
                    for k in range(KT):
                        ins = T.matmul(bank[2 * j + n][:, :], mixT[:, k, j * P:(j + 1) * P], w_out_sb[:, k, n * 512:(n + 1) * 512],
                                       start=(k == 0), stop=(k == KT - 1))
                    ins.then_inc(oproj, 1)
            for j in range(NT):
                pe.wait_ge(xf_ready, j + 1)
                for k in range(KT):
                    ins = T.transpose(bank[2 * j + k // 4][:, (k % 4) * P:(k % 4 + 1) * P], xf[:, j, k * P:(k + 1) * P], ident)
                ins.then_inc(xfT, 1)
            pe.wait_ge(d_rt, 64)
            for j in range(NT):
                pe.wait_ge(hfT_a, j + 1)
                pe.wait_ge(hfT_v, j + 1)
                for k in range(KT):
                    ins = T.matmul(bank[0][:, j * NR:(j + 1) * NR], mixT[:, k, j * P:(j + 1) * P], wr[:, k, :],
                                   start=(k == 0), stop=(k == KT - 1))
                ins.then_inc(logits, 1)
            pe.wait_ge(picks, 1)
            tri, ones = cst[:, K_TRI:K_TRI + P], cst[:, K_ONE:K_ONE + P]
            for j in range(NT + 1):
                o = bank[1][:, j * NE:(j + 1) * NE]
                for i in range(j):
                    ins = T.matmul(o, ones, both[:, i, :], start=(i == 0), stop=(i == j - 1 and j == NT))
                if j < NT:
                    T.matmul(o, tri, both[:, j, :], start=(j == 0), stop=True)
            ins.then_inc(ranks, 1)
            pe.wait_ge(match, 1)
            for k in range(2):
                for j in range(NT):
                    ins = T.matmul(bank[2][0:BC, 0:2 * NBLK], slot_is[:, k, j, :],
                                   block_is[:, k, j, :, :].rearrange("p w b -> p (w b)"),
                                   start=(k == j == 0), stop=(k == 1 and j == NT - 1))
            ins.then_inc(slots, 1)
            pe.wait_ge(routed, 1)

            def block_pe(r, n):
                u = r % 2
                pe.wait_ge(d_xg[u], n * 16 + 16)
                pe.sem_inc(passed, 1)
                for k in range(KT):
                    ins = T.transpose(bank[u][:, k * BC:(k + 1) * BC], xg[u][:, k * P:(k + 1) * P], ident[0:BC, 0:BC])
                ins.then_inc(xgT_made[u], 1)
                pe.wait_ge(xgT_ready[u], n + 1)
                for w, m in ((0, w_gate[r]), (1, w_up[r])):
                    for f in range(2):
                        c = (2 * w + f) * BC
                        for k in range(KT):
                            ins = T.matmul(bank[2 + u][:, c:c + BC], m[:, k, f * P:(f + 1) * P], xgT[u][:, k, :],
                                           start=(k == 0), stop=(k == KT - 1))
                ins.then_inc(gu_done[u], 1)
                pe.wait_ge(act_ready[u], n + 1)
                pe.wait_ge(y_half[u], n + 1)
                pe.wait_ge(y_rest[u], n + 1)
                for h in range(2):
                    for f in range(2):
                        ins = T.matmul(bank[4 + 2 * u + h][0:BC, :], aT[u][:, f * BC:(f + 1) * BC],
                                       w_down[r][:, f, h * 512:(h + 1) * 512], start=(f == 0), stop=(f == 1))
                ins.then_inc(down_done[u], 1)

            with pe.Fori(0, NE // 4) as g:
                for r in range(4):
                    nb, own = expert_counts(pe, g, r)
                    pe.wait_ge(d_ring[r], g * 48 + 48)
                    block_pe(r, own)
                    with pe.If(nb > 1):
                        with pe.Fori(1, nb) as i:
                            block_pe(r, own + i)

        @block.gpsimd
        def _(pool):

            Q = nc.gpsimd
            Q.dma_start(wr[:, :, 0:NG], w_router_group[0].rearrange("(k p) n -> p k n", p=P)).then_inc(d_rt, 16)
            Q.dma_start(wr[:, :, NG:], w_router_expert[0].rearrange("(k p) n -> p k n", p=P)).then_inc(d_rt, 16)
            Q.dma_start(rbias[:, 0:NG], b_router_group[0:1, :].to_broadcast([P, NG])).then_inc(d_rt, 16)
            Q.dma_start(rbias[:, NG:], b_router_expert[0:1, :].to_broadcast([P, NE])).then_inc(d_rt, 16)
            Q.dma_start(gain, ffn_norm[0:1, :].to_broadcast([P, D])).then_inc(d_gain, 16)
            Q.dma_start(gain_out, final_norm.rearrange("(a d) -> a d", a=1).to_broadcast([P, D])).then_inc(d_gain, 32)
            pool.wait_ge(logits, NT)
            for i in range(2):
                Q.memset(xg[i], 0.0).then_inc(xgT_made[i], 1)
                Q.memset(yb[i][:, 0:512], 0.0).then_inc(y_half[i], 1)
                Q.memset(yb[i][:, 512:], 0.0).then_inc(y_rest[i], 1)
            pool.wait_ge(routed, 1)
            pool.wait_ge(d_norm, 16 * NT)

            def gather(u, n, column, used):
                pool.wait_ge(xgT_made[u], n + 1)
                pool.sem_inc(passed, 1)
                Q.tensor_copy(ig[u][0:BC, :], idx[0:BC, column]).then_inc(i_step, 1)
                pool.wait_ge(i_step, used)
                pool.sem_inc(passed, 1)
                Q.indirect_dma_start(xg[u], None, normed, bass.IndirectOffsetOnAxis(ap=ig[u][0:BC, :].bitcast(U32), axis=0),
                                     bounds_check=SEQ - 1, oob_is_err=False).then_inc(d_xg[u], 16)

            def scatter(u, n, column, used):
                pool.wait_ge(y_half[u], n + 1)
                pool.wait_ge(y_rest[u], n + 1)
                pool.sem_inc(passed, 1)
                Q.tensor_copy(isc[u][0:BC, :], idx[0:BC, column]).then_inc(i_step, 1)
                pool.wait_ge(i_step, used)
                pool.sem_inc(passed, 1)
                Q.indirect_dma_start(expert_out, bass.IndirectOffsetOnAxis(ap=isc[u][0:BC, :].bitcast(U32), axis=0), yb[u], None,
                                     bounds_check=2 * SEQ - 1, oob_is_err=False).then_inc(d_sc[u], 16)

            NONE, TO = NBLK, NBLK + 1
            scatter(0, 0, slice(NONE, NONE + 1), 1)
            with pool.Fori(0, NE // 4) as g:
                for r in range(4):
                    u = r % 2
                    nb, own = expert_counts(pool, g, r)
                    other = pool.value_load(tab[0:1, bass.ds(g * 4 + (TW + r + 1), 1)], min_val=0, max_val=NBLK)
                    base = pool.value_load(tab[0:1, bass.ds(g * 4 + (2 * TW + r), 1)], min_val=0, max_val=NBLK - 1)
                    gather(u, own, bass.ds(base, 1), base * 2 + 2)
                    scatter(1 - u, other, bass.ds(base + NONE, 1), base * 2 + 3)
                    with pool.If(nb > 1):
                        with pool.Fori(1, nb) as i:
                            at_b = base + i
                            gather(u, own + i, bass.ds(at_b, 1), at_b * 2 + 2)
                            scatter(u, own + i, bass.ds(at_b + NONE, 1), at_b * 2 + 3)
            last = pool.value_load(tab[0:1, TW + NE + 1:TW + NE + 2], min_val=16, max_val=NBLK)
            total = pool.value_load(tab[0:1, 2 * TW + NE:2 * TW + NE + 1], min_val=NE, max_val=NBLK)
            scatter(1, last, bass.ds(total + NONE, 1), total * 2 + 2)


_INS = ["x", "meta_tokens", "mix_norm", "w_in", "conv_dw_w", "conv_dw_b", "conv_ln_g", "conv_ln_b", "attn_sinks",
        "hgrn_norm_g", "w_out", "ffn_norm", "w_router_group", "b_router_group", "w_router_expert",
        "b_router_expert", "w_exp_gate", "w_exp_up", "w_exp_down", "final_norm"]


def kernel(**inputs):
    import numpy as _np
    import concourse.bacc as _bacc
    from concourse import mybir as _mybir
    from concourse.bass_utils import run_bass_kernel_spmd as _run

    nc = _bacc.Bacc("TRN2", target_bir_lowering=False, num_devices=1)
    arrays, args = {}, []
    for name in _INS:
        a = _np.ascontiguousarray(inputs[name])
        arrays[f"in_{name}"] = a
        args.append(nc.dram_tensor(f"in_{name}", a.shape, _mybir.dt.from_np(a.dtype), kind="ExternalInput").ap())
    arrays["in_table"] = shape_constants()
    args.append(nc.dram_tensor("in_table", arrays["in_table"].shape, F32, kind="ExternalInput").ap())
    normed = nc.dram_tensor("normed", (SEQ, D), F32, kind="Internal").ap()
    expert_out = nc.dram_tensor("expert_out", (2 * SEQ, D), F32, kind="Internal").ap()
    out = nc.dram_tensor("out_0", (1, SEQ, D), F32, kind="ExternalOutput").ap()
    trunk(nc, *args, normed, expert_out, out)
    r = _run(nc, [arrays], core_ids=[0])
    return r.results[0]["out_0"]
```

```python
import numpy as np
import concourse.bass as bass
from concourse import mybir
from contextlib import ExitStack

F32 = mybir.dt.float32
F32R = mybir.dt.float32r
I32 = mybir.dt.int32
U32 = mybir.dt.uint32
ALU = mybir.AluOpType
ACT = mybir.ActivationFunctionType
AX = mybir.AxisListType.X

P = 128
D = 1024
KT = D // P
SEQ = 512
NT = SEQ // P
META = 16
CHUNK = 64
NC_ = SEQ // CHUNK
TAPS = 31
HD = 64
NQ, NKV = 8, 2
NE, NG, EPG = 32, 4, 8
DE = 256
EPS = 1e-6
LEVELS = (32, 16, 8, 4, 2, 1)
BC = 128
MORE = 2 * SEQ // BC
NBLK = NE + MORE
FAR = 8192
NEG = -1.0e30

C_A, C_GATE, C_Q, C_K, C_V = 0, 256, 512, 1024, 1152
C_HQ, C_HF, C_HI, C_HG = 1280, 1536, 1792, 2048
D_IN = 2304

K_ID = 0
K_TRI = K_ID + P
K_ONE = K_TRI + P
K_MEAN = K_ONE + P
K_HEAD = K_MEAN + P
K_RESET = K_HEAD + P
K_MASK = K_RESET + SEQ
K_DIST = K_MASK + (len(LEVELS) + 1) * CHUNK
DW = CHUNK + META + P
K_IOTA = K_DIST + NT * DW
K_TOK = K_IOTA + P
K_THR = K_TOK + NT
NTHR = SEQ // BC - 1
K_EPS = K_THR + NTHR
K_ALL = K_EPS + 1


def shape_constants():
    c = np.zeros((P, K_ALL), np.float32)
    i = np.arange(P)
    c[:, K_ID:K_ID + P] = np.eye(P)
    c[:, K_TRI:K_TRI + P] = i[:, None] < i[None, :]
    c[:, K_ONE:K_ONE + P] = 1.0
    c[:, K_MEAN:K_MEAN + P] = 1.0 / 256
    c[:, K_HEAD:K_HEAD + P] = (i[:, None] // HD == i[None, :] // HD) / HD
    c[:, K_RESET:K_RESET + SEQ] = np.arange(SEQ)[None] % CHUNK != 0
    s, t = i[:, None] % CHUNK, np.arange(CHUNK)[None, :]
    for n, h in enumerate(LEVELS):
        same = s // (2 * h) == t // (2 * h)
        c[:, K_MASK + n * CHUNK:K_MASK + (n + 1) * CHUNK] = same & (s % (2 * h) < h) & (t % (2 * h) >= h)
    n = len(LEVELS)
    c[:, K_MASK + n * CHUNK:K_MASK + (n + 1) * CHUNK] = s == t
    for p in range(NT):
        q = META + P * p + i[:, None]
        k = np.concatenate([META + P * p - CHUNK + np.arange(CHUNK), np.arange(META), META + P * p + np.arange(P)])
        d = -np.abs(q - k[None, :]).astype(np.float32)
        d[CHUNK:, :CHUNK] = NEG
        d[:CHUNK, CHUNK + META + CHUNK:] = NEG
        c[:, K_DIST + p * DW:K_DIST + (p + 1) * DW] = d
    c[:, K_IOTA:K_IOTA + P] = np.arange(P)[None]
    c[:, K_TOK:K_TOK + NT] = i[:, None] + P * np.arange(NT)[None]
    c[:, K_THR:K_THR + NTHR] = BC * np.arange(1, NTHR + 1)[None]
    c[:, K_EPS] = EPS
    return c


def trunk(nc, x, meta_tokens, mix_norm, w_in, conv_dw_w, conv_dw_b, conv_ln_g, conv_ln_b, attn_sinks,
          hgrn_norm_g, w_out, ffn_norm, w_router_group, b_router_group, w_router_expert,
          b_router_expert, w_exp_gate, w_exp_up, w_exp_down, final_norm, table, normed, expert_out, out):
    ctx = ExitStack()
    with ctx:
        mixer_ctx = ExitStack()

        def sb(name, shape, dt=F32, of=ctx):
            return of.enter_context(nc.sbuf_tensor(name, shape, dt))

        def sem(name):
            return ctx.enter_context(nc.semaphore(name))

        bank = [ctx.enter_context(nc.psum_tensor(f"bank{i}", [P, 512], F32)) for i in range(8)]

        area_w = sb("area_w", [P, KT * D_IN])
        area_x = sb("area_x", [P, NT * D])
        cst = sb("cst", [P, K_ALL])
        cols = sb("cols", [P, 78])
        rows = sb("rows", [78, P])
        sink = sb("sink", [P, NQ])
        stat = sb("stat", [P, 64])
        rbias = sb("rbias", [P, NG + NE])
        gain_out = sb("gain_out", [P, D])[:, :]
        w1, w2 = sb("w1", [P, NT])[:, :], sb("w2", [P, NT])[:, :]
        idx = sb("idx", [P, 2 * NBLK], I32)[:, :]
        tab = sb("tab", [1, 1 + MORE], I32)
        col_g = [sb(f"col_g{i}", [P, 1], I32)[:, :] for i in range(2)]
        col_s = [sb(f"col_s{i}", [P, 1], I32)[:, :] for i in range(2)]
        area_h = sb("area_h", [P, KT * (META + SEQ)], of=mixer_ctx)
        area_m = sb("area_m", [P, KT * SEQ], of=mixer_ctx)
        area_g = sb("area_g", [P, 18240], of=mixer_ctx)

        at = [0]

        def cut(area, n, shape=None):
            a = area[:, at[0]:at[0] + n]
            at[0] += n
            return a

        w_in_sb = area_w[:, :].rearrange("p (k n) -> p k n", k=KT)
        w_out_sb = area_w[:, 0:KT * D].rearrange("p (k n) -> p k n", k=KT)
        xs = area_x[:, :].rearrange("p (j d) -> p j d", j=NT)
        hT = area_h[:, :].rearrange("p (k t) -> p k t", k=KT)
        mixT = area_m[:, :].rearrange("p (k t) -> p k t", k=KT)
        TT = META + SEQ
        glu = cut(area_g, 2 * (TAPS - 1 + TT)).rearrange("p (c t) -> p c t", c=2)
        qf = cut(area_g, 2 * SEQ).rearrange("p (c t) -> p c t", c=2)
        kf = cut(area_g, 2 * TT).rearrange("p (c t) -> p c t", c=2)
        lf = cut(area_g, 2 * TT).rearrange("p (c t) -> p c t", c=2)
        b = cut(area_g, 2 * TT).rearrange("p (c t) -> p c t", c=2)
        eb = cut(area_g, 2 * SEQ).rearrange("p (c t) -> p c t", c=2)
        qb = cut(area_g, 2 * SEQ).rearrange("p (c t) -> p c t", c=2)
        kb = cut(area_g, 2 * TT).rearrange("p (c t) -> p c t", c=2)
        lev = [area_x[:, n * 1024:(n + 1) * 1024].rearrange("p (c t) -> p c t", c=2) for n in range(4)]
        lev += [cut(area_g, 2 * SEQ).rearrange("p (c t) -> p c t", c=2) for n in range(2)]
        v2 = cut(area_g, NC_ * 128).rearrange("p (c i e) -> p c i e", c=NC_, i=2)
        v2m = cut(area_g, 128).rearrange("p (i e) -> p i e", i=2)
        qT = cut(area_g, 4 * SEQ).rearrange("p (c t) -> p c t", c=4)
        kT = cut(area_g, 2 * TT).rearrange("p (c t) -> p c t", c=2)
        va = cut(area_g, NT * P).rearrange("p (j e) -> p j e", j=NT)
        vp = cut(area_g, NT * P).rearrange("p (j e) -> p j e", j=NT)
        vm = cut(area_g, P)
        zt_flat = cut(area_g, 2 * TT)
        zt = zt_flat.rearrange("p (c t) -> p c t", c=2)
        meta_x = zt_flat[0:META, 0:D]
        gain = cut(area_g, D)
        wr = cut(area_g, KT * (NG + NE)).rearrange("p (k n) -> p k n", k=KT)
        at[0] = 0
        k2 = cut(area_h, NC_ * 128).rearrange("p (c i e) -> p c i e", c=NC_, i=2)
        k2m = cut(area_h, 128).rearrange("p (i e) -> p i e", i=2)
        state = cut(area_h, NC_ * 128).rearrange("p (c i e) -> p c i e", c=NC_, i=2)
        A = cut(area_h, 1024).rearrange("p (c t) -> p c t", c=2)
        osq = cut(area_h, 1024).rearrange("p (c t) -> p c t", c=2)
        at[0] = KT * D + 3 * KT * DE
        sc = [cut(area_w, 4 * DW).rearrange("p (h k) -> p h k", h=4) for _ in range(2)]
        pa = cut(area_w, 512)
        pb = cut(area_w, 512)
        sig = area_m[:, 2 * SEQ:2 * SEQ + 2 * TT].rearrange("p (c t) -> p c t", c=2)
        ed = [area_m[:, 2 * SEQ:4 * SEQ].rearrange("p (c t) -> p c t", c=2),
              area_m[:, 4 * SEQ:6 * SEQ].rearrange("p (c t) -> p c t", c=2)]
        dm = stat[:, 32:64].rearrange("p (c t) -> p c t", c=2)
        ident = cst[:, K_ID:K_ID + P]
        eps = cst[:, K_EPS:K_EPS + 1]
        one = cst[:, K_ONE:K_ONE + 1]
        ss, rstd = stat[:, 0:5], stat[:, 5:10]
        mx = [stat[:, 10:14], stat[:, 14:18]]
        rs = [stat[:, 18:22], stat[:, 22:26]]
        es = [stat[:, 26:30], area_w[:, KT * D + 3 * KT * DE + 8 * DW + 1024:KT * D + 3 * KT * DE + 8 * DW + 1028]]

        d_cst, d_par, d_meta, d_sink = sem("d_cst"), sem("d_par"), sem("d_meta"), sem("d_sink")
        d_x = [sem(f"d_x{j}") for j in range(NT)]
        d_win = [sem(f"d_win{i}") for i in range(8)]
        d_wout = [sem("d_wout0"), sem("d_wout1")]
        d_resid = sem("d_resid")
        sumsq = sem("sumsq"); rstd_ready = sem("rstd_ready"); xn_ready = sem("xn_ready")
        par_T = sem("par_T"); cols_ready = sem("cols_ready")
        xT_done = sem("xT_done"); metaT = sem("metaT"); hT_v = sem("hT_v"); hT_a = sem("hT_a")
        product = sem("product"); evac = sem("evac"); glu_done = sem("glu_done")
        a_step = sem("a_step"); v_step = sem("v_step")
        softplus = sem("softplus"); gates = sem("gates"); kf_ready = sem("kf_ready")
        b_ready = sem("b_ready"); eb_ready = sem("eb_ready"); lev_d = sem("lev_d"); lev_e = sem("lev_e"); lev_w = sem("lev_w")
        kb_ready = sem("kb_ready"); kbT = sem("kbT"); k2_a = sem("k2_a"); k2_v = sem("k2_v")
        u_done = sem("u_done"); state_done = sem("state_done"); g_done = sem("g_done"); g_used = sem("g_used")
        o_done = sem("o_done"); osq_done = sem("osq_done"); ms_done = sem("ms_done"); orstd = sem("orstd"); y_h = sem("y_h")
        conv_done = sem("conv_done"); mean_done = sem("mean_done"); cen_done = sem("cen_done")
        csq = sem("csq"); var_done = sem("var_done"); crstd = sem("crstd"); cnorm = sem("cnorm"); y_c = sem("y_c")
        s_done = sem("s_done"); s_ready = sem("s_ready"); p_exp = sem("p_exp"); p_ready = sem("p_ready")
        pT = sem("pT"); pa_ready = sem("pa_ready"); pb_ready = sem("pb_ready"); pv = sem("pv"); y_a = sem("y_a")
        den = sem("den"); pads = sem("pads")

        PIECE = 2 * KT // 2 * DE
        RAW = 4
        piece_at = [KT * D + i * PIECE for i in range(RAW - 1)] + [KT * D_IN - PIECE]
        raw = [area_w[:, a:a + PIECE] for a in piece_at]
        JUNK = KT * D + 3 * PIECE
        xf = area_h[:, 0:NT * D].rearrange("p (j d) -> p j d", j=NT)
        ye = [area_w[:, i * NT * D:(i + 1) * NT * D].rearrange("p (j d) -> p j d", j=NT) for i in range(2)]
        at[0] = 0
        NR = NG + NE
        logit = cut(area_g, NT * NR).rearrange("p (j n) -> p j n", j=NT)
        glog, gexp = (cut(area_g, NT * NG).rearrange("p (j n) -> p j n", j=NT) for _ in range(2))
        t4, oh4 = (cut(area_g, NT * NG).rearrange("p (j n) -> p j n", j=NT) for _ in range(2))
        ev, t32, oh1, oh2, both, rank = (cut(area_g, NT * NE).rearrange("p (j n) -> p j n", j=NT) for _ in range(6))
        count, extra, incl, first = (cut(area_g, NE) for _ in range(4))
        over = cut(area_g, NE * NTHR).rearrange("p (e m) -> p e m", e=NE)
        over4 = cut(area_g, NT * NTHR).rearrange("p (j m) -> p j m", j=NT)
        gm, gi, m1, i1, m2, i2, gsum, wd, qk, q1, tokf, tokf2 = (cut(area_g, NT) for _ in range(12))
        below = cut(area_g, MORE * NE).rearrange("p (m e) -> p m e", m=MORE)
        rk, bk, ck = ([cut(area_g, NT) for _ in range(2)] for _ in range(3))
        slot_is = cut(area_g, 2 * NT * BC).rearrange("p (k j c) -> p k j c", k=2, j=NT)
        block_is = cut(area_g, 2 * NT * 2 * NBLK).rearrange("p (k j w b) -> p k j w b", k=2, j=NT, w=2)
        assert at[0] <= 16924

        oproj = sem("oproj"); h2_done = sem("h2_done"); fstat = sem("fstat"); xf_ready = sem("xf_ready")
        d_norm = sem("d_norm"); xfT = sem("xfT"); hfT_a = sem("hfT_a"); hfT_v = sem("hfT_v"); d_rt = sem("d_rt"); d_gain = sem("d_gain")
        logits = sem("logits"); gdiff = sem("gdiff"); gprob = sem("gprob"); ediff = sem("ediff"); eprob = sem("eprob")
        picks = sem("picks"); ranks = sem("ranks"); match = sem("match"); slots = sem("slots"); routed = sem("routed")
        d_raw = [sem(f"d_raw{i}") for i in range(RAW)]
        hi_done = sem("hi_done"); lo_done = sem("lo_done"); piece_used = sem("piece_used")
        d_xg = [sem(f"d_xg{i}") for i in range(2)]; d_sc = [sem(f"d_sc{i}") for i in range(2)]
        xg_clear = sem("xg_clear"); xT_made = sem("xT_made"); xT_hi = sem("xT_hi"); xT_lo = sem("xT_lo")
        nstep = sem("nstep"); first_sum = sem("first_sum")
        sg_ready = sem("sg_ready"); act_ready = sem("act_ready")
        aT_made = sem("aT_made"); aT_hi = sem("aT_hi"); aT_lo = sem("aT_lo"); y_ready = sem("y_ready")
        col_ready = sem("col_ready")
        m_free = sem("m_free"); m_w = sem("m_w"); m_xg = sem("m_xg"); m_hi = sem("m_hi"); m_lo = sem("m_lo")
        m_xT = sem("m_xT"); m_xhi = sem("m_xhi"); m_xlo = sem("m_xlo"); m_gu = sem("m_gu"); m_sg = sem("m_sg"); m_act = sem("m_act")
        m_aT = sem("m_aT"); m_ahi = sem("m_ahi"); m_alo = sem("m_alo"); m_down = sem("m_down"); m_y = sem("m_y"); m_sc = sem("m_sc")
        d_ye = [sem(f"d_ye{j}") for j in range(NT)]; summed = sem("summed"); ostat = sem("ostat"); o_ready = sem("o_ready"); d_out = sem("d_out")

        passed = sem("passed")

        PROD = (["gate0", "gate1", "a0", "a1", "hq0", "hq1", "hg0", "hg1", "hf0", "hf1", "k",
                 "v0", "v1", "v2", "v3", "vm", "q0", "q1", "q2", "q3"])
        WITH_META = ["gate0", "gate1", "a0", "a1", "hf0", "hf1", "k"]
        COL = {"gate0": C_GATE, "gate1": C_GATE + P, "a0": C_A, "a1": C_A + P, "hq0": C_HQ, "hq1": C_HQ + P,
               "hg0": C_HG, "hg1": C_HG + P, "hf0": C_HF, "hf1": C_HF + P, "k": C_K,
               "q0": C_Q, "q1": C_Q + P, "q2": C_Q + 2 * P, "q3": C_Q + 3 * P}
        LOADS = [(C_GATE, 256), (C_A, 256), (C_HQ, 256), (C_HG, 256), (C_HF, 256), (C_K, 256), (C_HI, 256), (C_Q, 512)]
        LOAD_OF = {"gate": 0, "a": 1, "hq": 2, "hg": 3, "hf": 4, "k": 5, "v": 6, "q": 7}
        EVAC = [n for n in PROD if n not in ("a0", "a1")]

        def made(n):
            return PROD.index(n) + 1

        def taken(n):
            return EVAC.index(n) + 1

        def pbank(n):
            return bank[PROD.index(n) % 4]

        def mcols(n):
            return bank[4 + WITH_META.index(n) % 2][:, 0:META]

        def first_rows(w, e, half):
            return e(w).rearrange("(p k) n -> p k n", k=KT)[:, half * (KT // 2):(half + 1) * (KT // 2), :]

        def load_gate_up(sp, e, half, slot, d):
            v = raw[slot].rearrange("p (w k n) -> p w k n", w=2, n=DE)
            sp.dma_start(v[:, 0], first_rows(w_exp_gate, e, half)).then_inc(d, 16)
            sp.dma_start(v[:, 1], first_rows(w_exp_up, e, half)).then_inc(d, 16)

        def load_down(sp, e, slot, d):
            v = raw[slot].rearrange("p (f n) -> p f n", f=2)
            s_ = e(w_exp_down).rearrange("(p f) n -> p f n", f=2)
            for f in range(2):
                sp.dma_start(v[:, f], s_[:, f]).then_inc(d, 16)

        def through(v):
            if isinstance(v, int) and v < 2:
                return v + 1
            return v - 2 if isinstance(v, int) and v == 3 * NE + 2 else v

        block = mixer_ctx.enter_context(nc.Block())

        @block.sync
        def _(sp):
            sp.dma_start(meta_x[:, :], meta_tokens).then_inc(d_meta, 16)
            for j in range(NT):
                sp.dma_start(xs[:, j, :], x[0, j * P:(j + 1) * P, :]).then_inc(d_x[j], 16)
            w_v = w_in[0].rearrange("(k p) n -> p k n", p=P)
            for i, (c0, n) in enumerate(LOADS):
                sp.dma_start(w_in_sb[:, :, c0:c0 + n], w_v[:, :, c0:c0 + n]).then_inc(d_win[i], 16)
            sp.wait_ge(product, len(PROD))
            wo_v = w_out[0].rearrange("(k p) n -> p k n", p=P)
            for i in range(2):
                sp.dma_start(w_out_sb[:, :, i * 512:(i + 1) * 512], wo_v[:, :, i * 512:(i + 1) * 512]).then_inc(d_wout[i], 16)
            sp.wait_ge(g_done, 14)
            sp.dma_start(xs, x[0].rearrange("(j p) d -> p j d", p=P)).then_inc(d_resid, 16)

            load_gate_up(sp, lambda w: w[0, 0], 0, 0, d_raw[0])
            load_gate_up(sp, lambda w: w[0, 0], 1, 1, d_raw[1])
            sp.wait_ge(y_a, 2 * NT)
            load_gate_up(sp, lambda w: w[0, 1], 0, 3, d_raw[3])
            for j in range(NT):
                sp.wait_ge(xf_ready, j + 1)
                sp.dma_start(normed[j * P:(j + 1) * P, :], xf[:, j, :]).then_inc(d_norm, 16)
            sp.wait_ge(d_norm, 16 * NT)
            sp.wait_ge(routed, 1)

        @block.scalar
        def _(act):
            an = [0]

            def step(ins):
                an[0] += 1
                ins.then_inc(a_step, 1)
                act.wait_ge(a_step, an[0])

            act.dma_start(cst[:, :], table).then_inc(d_cst, 16)
            act.dma_start(rows[0:62, :], conv_dw_w[0].rearrange("t (c p) -> (t c) p", p=P)).then_inc(d_par, 16)
            act.dma_start(rows[62:70, :], mix_norm[0].rearrange("(c p) -> c p", p=P)).then_inc(d_par, 16)
            for i, a in enumerate((conv_dw_b, conv_ln_g, conv_ln_b, hgrn_norm_g)):
                act.dma_start(rows[70 + 2 * i:72 + 2 * i, :], a[0].rearrange("(c p) -> c p", p=P)).then_inc(d_par, 16)
            act.dma_start(sink[:, :], attn_sinks.to_broadcast([P, NQ])).then_inc(d_sink, 16)
            act.wait_ge(d_cst, 16)
            act.preload_act_table_set("natural_log_exp_and_others")
            for j in [4, 0, 1, 2, 3]:
                rws = META if j == 4 else P
                src = meta_x[:, :] if j == 4 else xs[:, j, :]
                act.wait_ge(d_meta if j == 4 else d_x[j], 16)
                junk = area_g[0:rws, 2 * (TAPS - 1 + TT):2 * (TAPS - 1 + TT) + D]
                step(nc.scalar.activation(junk, src, ACT.Square, accum_out=ss[0:rws, j:j + 1]))
                step(nc.scalar.activation(rstd[0:rws, j:j + 1], ss[0:rws, j:j + 1], ACT.Ln, bias=eps[0:rws], scale=1.0 / D))
                nc.scalar.activation(rstd[0:rws, j:j + 1], rstd[0:rws, j:j + 1], ACT.Exp, scale=-0.5).then_inc(rstd_ready, 1)
            act.wait_ge(rstd_ready, 5)
            act.wait_ge(xT_done, NT)
            act.wait_ge(cols_ready, 1)
            for k in range(1, KT, 2):
                nc.scalar.activation(hT[:, k, META:], bank[k][:, :], ACT.Copy, scale=cols[:, 62 + k:63 + k]).then_inc(hT_a, 1)
            for n in EVAC:
                act.wait_ge(product, made(n))
                src = pbank(n)
                i = int(n[1:]) if n[1:].isdigit() else int(n[-1]) if n[-1].isdigit() else 0
                if n.startswith("gate"):
                    nc.scalar.activation(sig[:, i, 0:META], mcols(n), ACT.Sigmoid).then_inc(a_step, 1); an[0] += 1
                    nc.scalar.activation(sig[:, i, META:], src[:, :], ACT.Sigmoid).then_inc(evac, 1)
                elif n.startswith("hq"):
                    nc.scalar.activation(qf[:, i, :], src[:, :], ACT.Silu).then_inc(evac, 1)
                elif n.startswith("hg"):
                    nc.scalar.activation(mixT[:, 6 + i, :], src[:, :], ACT.Silu).then_inc(evac, 1)
                elif n.startswith("hf"):
                    nc.scalar.activation(zt[:, i, 0:META], mcols(n), ACT.Identity).then_inc(a_step, 1); an[0] += 1
                    nc.scalar.activation(zt[:, i, META:], src[:, :], ACT.Identity).then_inc(evac, 1)
                    if i == 1:
                        act.wait_ge(evac, taken(n))
                        act.wait_ge(a_step, an[0])
                        act.preload_act_table_set("natural_log_exp_and_others")
                        step(nc.scalar.activation(lf, zt, ACT.Abs))
                        step(nc.scalar.activation(lf, lf, ACT.Exp, scale=-1.0))
                        nc.scalar.activation(b, lf, ACT.Ln, bias=one).then_inc(softplus, 1)
                        act.wait_ge(gates, 2)
                        nc.scalar.activation(kf, kf, ACT.Exp, scale=-1.0).then_inc(kf_ready, 1)
                elif n == "k":
                    for g in range(2):
                        for half in range(2):
                            dst, s = slice(half * HD, half * HD + HD), slice(g * HD, g * HD + HD)
                            nc.scalar.activation(kT[dst, g, 0:META], mcols(n)[s, :], ACT.Copy).then_inc(a_step, 1); an[0] += 1
                            last = nc.scalar.activation(kT[dst, g, META:], src[s, :], ACT.Copy)
                            if g == half == 1:
                                last.then_inc(evac, 1)
                            else:
                                last.then_inc(a_step, 1); an[0] += 1
                elif n == "vm":
                    act.wait_ge(pads, 1)
                    for j in range(1, NT):
                        nc.scalar.activation(vp[HD:HD + META, j, :], src[0:META, 0:P], ACT.Copy).then_inc(a_step, 1); an[0] += 1
                    nc.scalar.activation(vm[0:META, :], src[0:META, 0:P], ACT.Copy).then_inc(a_step, 1); an[0] += 1
                    s = src[0:META, P:P + 256].rearrange("p (i h e) -> p i h e", i=2, h=2)
                    nc.scalar.activation(v2m[0:META], s[:, :, 0, :], ACT.Copy).then_inc(a_step, 1); an[0] += 1
                    nc.scalar.activation(v2m[HD:HD + META], s[:, :, 1, :], ACT.Copy).then_inc(evac, 1)
                elif n.startswith("v"):
                    nc.scalar.activation(va[:, i, :], src[:, 0:P], ACT.Copy).then_inc(a_step, 1); an[0] += 1
                    if i + 1 < NT:
                        nc.scalar.activation(vp[0:HD, i + 1, :], src[HD:P, 0:P], ACT.Copy).then_inc(a_step, 1); an[0] += 1
                    s = src[:, P:P + 256].rearrange("p (i h e) -> p i h e", i=2, h=2)
                    for cp in range(2):
                        for hp in range(2):
                            last = nc.scalar.activation(v2[hp * HD:hp * HD + HD, 2 * i + cp, :, :],
                                                        s[cp * HD:cp * HD + HD, :, hp, :], ACT.Copy)
                            if cp == hp == 1:
                                last.then_inc(evac, 1)
                            else:
                                last.then_inc(a_step, 1); an[0] += 1
                else:
                    nc.scalar.activation(qT[:, i, :], src[:, :], ACT.Copy, scale=HD ** -0.5).then_inc(evac, 1)
                if n == "k":
                    act.wait_ge(b_ready, 1)
                    nc.scalar.activation(eb, b[:, :, META:], ACT.Exp).then_inc(eb_ready, 1)
                    act.wait_ge(lev_d, 1)
                    nc.scalar.activation(dm, dm, ACT.Exp).then_inc(a_step, 1); an[0] += 1
                    nc.scalar.activation(ed[0], ed[0], ACT.Exp).then_inc(lev_e, 1)
                if n in ("v0", "v1", "v2", "v3", "vm", "q0"):
                    l = ("v0", "v1", "v2", "v3", "vm", "q0").index(n)
                    act.wait_ge(lev_d, l + 2)
                    e = ed[(l + 1) % 2]
                    nc.scalar.activation(e, e, ACT.Exp).then_inc(lev_e, 1)
            act.wait_ge(kbT, 2)
            for ti in range(2):
                src = bank[5 + ti][:, :].rearrange("p (r h e) -> p r h e", r=4, h=2)
                for hp in range(2):
                    nc.scalar.activation(k2[hp * HD:hp * HD + HD, 0::2, ti, :], src[0:HD, :, hp, :], ACT.Copy).then_inc(k2_a, 1)
            act.wait_ge(cen_done, 2)
            nc.scalar.activation(osq, mixT[:, 0:2, :], ACT.Square).then_inc(csq, 1)
            act.wait_ge(var_done, 1)
            step(nc.scalar.activation(ed[0][:, 0, :], bank[4][:, :], ACT.Ln, bias=eps))
            nc.scalar.activation(ed[0][:, 0, :], ed[0][:, 0, :], ACT.Exp, scale=-0.5).then_inc(crstd, 1)
            act.wait_ge(o_done, 2)
            for ti in range(2):
                nc.scalar.activation(osq[:, ti, :], bank[ti][:, :], ACT.Square).then_inc(osq_done, 1)
            act.wait_ge(ms_done, 2)
            for ti in range(2):
                step(nc.scalar.activation(ed[1][:, ti, :], bank[2 + ti][:, :], ACT.Ln, bias=eps))
                nc.scalar.activation(ed[1][:, ti, :], ed[1][:, ti, :], ACT.Exp, scale=-0.5).then_inc(orstd, 1)

            def probs(u):
                act.wait_ge(s_ready, u + 1)
                i = u % 2
                for h in range(4):
                    lo = HD if u < 2 else 0
                    nc.scalar.activation(sc[i][:, h, lo:], sc[i][:, h, lo:], ACT.Exp, bias=mx[i][:, h:h + 1],
                                         accum_out=rs[i][:, h:h + 1]).then_inc(a_step, 1); an[0] += 1
                nc.scalar.activation(es[i], es[i], ACT.Exp).then_inc(p_exp, 1)

            def tile_a(u):
                act.wait_ge(pT, u + 1)
                if u >= 1:
                    act.wait_ge(pv, u)
                lo = META if u < 2 else HD + META
                nc.scalar.activation(pa[0:lo, :], bank[5][0:lo, :], ACT.Copy).then_inc(pa_ready, 1)

            def heads_out(u):
                act.wait_ge(pv, u + 1)
                p, g = u // 2, u % 2
                src = bank[7 - 3 * (u % 2)][:, 0:256].rearrange("p (i t) -> p i t", i=2)
                nc.scalar.activation(mixT[:, 2 + 2 * g:4 + 2 * g, p * P:(p + 1) * P], src, ACT.Copy).then_inc(y_a, 1)

            act.wait_ge(y_h, 2)
            act.wait_ge(cnorm, 2)
            U = 2 * NT
            probs(0)
            for u in range(U):
                if u + 1 < U:
                    probs(u + 1)
                tile_a(u)
                heads_out(u)
            for i in range(2):
                nc.scalar.activation(mixT[:, i, :], mixT[:, i, :], ACT.Silu, scale=cols[:, 72 + i:73 + i],
                                     bias=cols[:, 74 + i:75 + i]).then_inc(y_c, 1)

            act.preload_act_table_set("natural_log_exp_and_others")
            for j in range(NT):
                act.wait_ge(h2_done, 2 * j + 2)
                if j == 0:
                    act.wait_ge(oproj, 2 * NT)
                step(nc.scalar.activation(area_w[:, JUNK:JUNK + D], xs[:, j, :], ACT.Square, accum_out=ss[:, j:j + 1]))
                step(nc.scalar.activation(rstd[:, j:j + 1], ss[:, j:j + 1], ACT.Ln, bias=eps, scale=1.0 / D))
                nc.scalar.activation(rstd[:, j:j + 1], rstd[:, j:j + 1], ACT.Exp, scale=-0.5).then_inc(fstat, 1)
            for j in range(NT):
                act.wait_ge(xfT, j + 1)
                src = bank[2 * j + 1][:, :].rearrange("p (k t) -> p k t", k=4)
                nc.scalar.activation(mixT[:, 4:8, j * P:(j + 1) * P], src, ACT.Copy).then_inc(hfT_a, 1)
            act.wait_ge(gdiff, 1)
            nc.scalar.activation(gexp, gexp, ACT.Exp).then_inc(gprob, 1)
            act.wait_ge(ediff, 1)
            nc.scalar.activation(wd, wd, ACT.Exp).then_inc(eprob, 1)

        @block.vector
        def _(dve):
            vn = [0]

            def step(ins):
                vn[0] += 1
                ins.then_inc(v_step, 1)
                dve.wait_ge(v_step, vn[0])

            def mark(ins):
                vn[0] += 1
                ins.then_inc(v_step, 1)
                return vn[0]

            V = nc.vector
            mark(V.memset(glu[:, :, 0:TAPS - 1], 0.0))
            V.memset(vp[:, :, :], 0.0).then_inc(pads, 1)
            dve.wait_ge(par_T, 1)
            V.tensor_copy(cols[:, :], bank[6][:, 0:78]).then_inc(cols_ready, 1)
            dve.wait_ge(cols_ready, 1)
            for n, j in enumerate([4, 0, 1, 2, 3]):
                dve.wait_ge(rstd_ready, n + 1)
                if j == 4:
                    V.tensor_scalar(meta_x[:, :], meta_x[:, :], rstd[0:META, 4:5], None, ALU.mult).then_inc(xn_ready, 1)
                else:
                    V.tensor_scalar(xs[:, j, :], xs[:, j, :], rstd[:, j:j + 1], None, ALU.mult).then_inc(xn_ready, 1)
                if j == 0:
                    dve.wait_ge(metaT, 1)
                    V.tensor_tensor(hT[:, :, 0:META], bank[7][:, 0:P].rearrange("p (k t) -> p k t", k=KT),
                                    cols[:, 62:70].unsqueeze(2).to_broadcast([P, KT, META]), ALU.mult).then_inc(hT_v, 1)
            dve.wait_ge(xT_done, NT)
            for k in range(0, KT, 2):
                V.tensor_scalar(hT[:, k, META:], bank[k][:, :], cols[:, 62 + k:63 + k], None, ALU.mult).then_inc(hT_v, 1)
            dve.wait_ge(evac, taken("gate1"))
            for i in range(2):
                n = f"a{i}"
                dve.wait_ge(product, made(n))
                mark(V.tensor_tensor(glu[:, i, TAPS - 1:TAPS - 1 + META], mcols(n), sig[:, i, 0:META], ALU.mult))
                V.tensor_tensor(glu[:, i, TAPS - 1 + META:], pbank(n)[:, :], sig[:, i, META:], ALU.mult).then_inc(glu_done, 1)
            dve.wait_ge(glu_done, 2)
            dve.wait_ge(v_step, vn[0])
            last = [0, 0]
            for t in range(TAPS):
                for i in range(2):
                    src = glu[:, i, META + t:META + t + SEQ]
                    w = cols[:, 2 * t + i:2 * t + i + 1]
                    if t == 0:
                        last[i] = mark(V.tensor_scalar(mixT[:, i, :], src, w, cols[:, 70 + i:71 + i], ALU.mult, ALU.add))
                    else:
                        dve.wait_ge(v_step, last[i])
                        ins = V.scalar_tensor_tensor(out=mixT[:, i, :], in0=src, scalar=w, in1=mixT[:, i, :],
                                                     op0=ALU.mult, op1=ALU.add)
                        if t == TAPS - 1:
                            ins.then_inc(conv_done, 1)
                        else:
                            last[i] = mark(ins)
            dve.wait_ge(softplus, 1)
            V.scalar_tensor_tensor(out=lf, in0=zt, scalar=0.0, in1=b, op0=ALU.min, op1=ALU.subtract).then_inc(gates, 1)
            V.scalar_tensor_tensor(out=kf, in0=zt, scalar=0.0, in1=b, op0=ALU.max, op1=ALU.add).then_inc(gates, 1)
            dve.wait_ge(gates, 2)
            for i in range(2):
                mark(V.tensor_tensor_scan(b[:, i, 0:META], cst[:, K_ONE:K_ONE + META], lf[:, i, 0:META], 0.0, ALU.mult, ALU.add))
                ins = V.tensor_tensor_scan(b[:, i, META:], cst[:, K_RESET:K_RESET + SEQ], lf[:, i, META:], 0.0, ALU.mult, ALU.add)
                if i == 0:
                    mark(ins)
                else:
                    ins.then_inc(b_ready, 1)
            dve.wait_ge(b_ready, 1)
            dve.wait_ge(v_step, vn[0])
            bc = b[:, :, META:].rearrange("p i (c t) -> p i c t", t=CHUNK)
            mark(V.tensor_tensor(dm, b[:, :, META - 1:META].to_broadcast([P, 2, META]), b[:, :, 0:META], ALU.subtract))
            V.tensor_tensor(ed[0].rearrange("p i (c t) -> p i c t", t=CHUNK),
                            bc[:, :, :, CHUNK - 1:CHUNK].to_broadcast([P, 2, NC_, CHUNK]), bc, ALU.subtract).then_inc(lev_d, 1)

            def level_decay(l):
                h = LEVELS[l]
                e = ed[(l + 1) % 2].rearrange("p i (c t) -> p i c t", t=2 * h)
                bl = b[:, :, META:].rearrange("p i (c t) -> p i c t", t=2 * h)
                mid = bl[:, :, :, h - 1:h].to_broadcast([P, 2, SEQ // (2 * h), h])
                mark(V.tensor_tensor(e[:, :, :, 0:h], mid, bl[:, :, :, 0:h], ALU.subtract))
                V.tensor_tensor(e[:, :, :, h:], bl[:, :, :, h:], mid, ALU.subtract).then_inc(lev_d, 1)

            def level_pair(l):
                h = LEVELS[l]
                dve.wait_ge(lev_e, l + 2)
                e = ed[(l + 1) % 2].rearrange("p i (c t) -> p i c t", t=2 * h)
                w = lev[l].rearrange("p i (c t) -> p i c t", t=2 * h)
                kk = kf[:, :, META:].rearrange("p i (c t) -> p i c t", t=2 * h)
                qq = qf.rearrange("p i (c t) -> p i c t", t=2 * h)
                mark(V.tensor_tensor(w[:, :, :, 0:h], kk[:, :, :, 0:h], e[:, :, :, 0:h], ALU.mult))
                V.tensor_tensor(w[:, :, :, h:], qq[:, :, :, h:], e[:, :, :, h:], ALU.mult).then_inc(lev_w, 1)
                dve.wait_ge(lev_w, l + 1)
                dve.wait_ge(v_step, vn[0])

            level_decay(0)
            dve.wait_ge(lev_e, 1)
            dve.wait_ge(kf_ready, 1)
            mark(V.tensor_tensor(kb[:, :, 0:META], kf[:, :, 0:META], dm, ALU.mult))
            V.tensor_tensor(kb[:, :, META:], kf[:, :, META:], ed[0], ALU.mult).then_inc(kb_ready, 1)
            dve.wait_ge(kb_ready, 1)
            for l in range(len(LEVELS)):
                if l + 1 < len(LEVELS):
                    level_decay(l + 1)
                level_pair(l)
            dve.wait_ge(eb_ready, 1)
            mark(V.tensor_tensor(qb, qf, eb, ALU.mult))
            dve.wait_ge(kbT, 2)
            for ti in range(2):
                src = bank[5 + ti][:, :].rearrange("p (r h e) -> p r h e", r=4, h=2)
                for hp in range(2):
                    V.tensor_copy(k2[hp * HD:hp * HD + HD, 1::2, ti, :], src[HD:P, :, hp, :]).then_inc(k2_v, 1)
            src = bank[7][0:META, 0:256].rearrange("p (i h e) -> p i h e", i=2, h=2)
            for hp in range(2):
                V.tensor_copy(k2m[hp * HD:hp * HD + META, :, :], src[:, :, hp, :]).then_inc(k2_v, 1)
            dve.wait_ge(u_done, 1)
            step(V.tensor_copy(state[:, 0, :, :], bank[0][:, 0:P].rearrange("p (i e) -> p i e", i=2)))
            for c in range(1, NC_):
                u = bank[c // 4][:, (c % 4) * P:(c % 4) * P + P].rearrange("p (i e) -> p i e", i=2)
                for i in range(2):
                    ins = V.scalar_tensor_tensor(out=state[:, c, i, :], in0=state[:, c - 1, i, :],
                                                 scalar=eb[:, i, c * CHUNK - 1:c * CHUNK], in1=u[:, i, :],
                                                 op0=ALU.mult, op1=ALU.add)
                    if i == 0:
                        mark(ins)
                    elif c < NC_ - 1:
                        step(ins)
                    else:
                        ins.then_inc(state_done, 1)
            nl = len(LEVELS)
            for n in range(2 * (nl + 1)):
                ti, l = n % 2, (nl - n // 2)
                dve.wait_ge(g_done, n + 1)
                m = cst[:, K_MASK + l * CHUNK:K_MASK + (l + 1) * CHUNK].unsqueeze(1).to_broadcast([P, NC_, CHUNK])
                g = bank[2 + n % 2][:, :].rearrange("p (c t) -> p c t", t=CHUNK)
                a = A[:, ti, :].rearrange("p (c t) -> p c t", t=CHUNK)
                if n >= 2:
                    dve.wait_ge(g_used, n - 1)
                if l == nl:
                    V.tensor_tensor(a, g, m, ALU.mult).then_inc(g_used, 1)
                else:
                    V.copy_predicated(a, m.bitcast(I32), g).then_inc(g_used, 1)
            dve.wait_ge(mean_done, 1)
            for i in range(2):
                V.tensor_tensor(mixT[:, i, :], mixT[:, i, :], bank[7][:, :], ALU.subtract).then_inc(cen_done, 1)
            dve.wait_ge(crstd, 1)
            for i in range(2):
                V.tensor_tensor(mixT[:, i, :], mixT[:, i, :], ed[0][:, 0, :], ALU.mult).then_inc(cnorm, 1)
            for ti in range(2):
                dve.wait_ge(orstd, ti + 1)
                step(V.tensor_tensor(ed[1][:, ti, :], bank[ti][:, :], ed[1][:, ti, :], ALU.mult))
                V.scalar_tensor_tensor(out=mixT[:, 6 + ti, :], in0=ed[1][:, ti, :], scalar=cols[:, 76 + ti:77 + ti],
                                       in1=mixT[:, 6 + ti, :], op0=ALU.mult, op1=ALU.mult).then_inc(y_h, 1)

            def biased(u):
                dve.wait_ge(s_done, u + 1)
                p, g, i = u // 2, u % 2, u % 2
                if u >= 2:
                    dve.wait_ge(pT, u - 1)
                lo = HD if p == 0 else 0
                dist = cst[:, K_DIST + p * DW + lo:K_DIST + (p + 1) * DW]
                for h in range(4):
                    s = bank[2 * i + h % 2][:, (h // 2) * DW + lo:(h // 2 + 1) * DW]
                    mark(V.scalar_tensor_tensor(out=sc[i][:, h, lo:], in0=dist, scalar=2.0 ** -(4 * g + h + 1), in1=s,
                                                op0=ALU.mult, op1=ALU.add))
                dve.wait_ge(v_step, vn[0])
                if u < 2:
                    dve.wait_ge(d_sink, 16)
                step(V.tensor_reduce(mx[i], sc[i][:, :, lo:], AX, ALU.max))
                step(V.tensor_tensor(mx[i], mx[i], sink[:, 4 * g:4 * g + 4], ALU.max))
                step(V.tensor_scalar(mx[i], mx[i], -1.0, None, ALU.mult))
                V.tensor_tensor(es[i], mx[i], sink[:, 4 * g:4 * g + 4], ALU.add).then_inc(s_ready, 1)

            def normal(u):
                i = u % 2
                lo = HD if u < 2 else 0
                dve.wait_ge(p_exp, u + 1)
                step(V.tensor_tensor(rs[i], rs[i], es[i], ALU.add))
                step(V.reciprocal(rs[i], rs[i]))
                V.tensor_tensor(sc[i][:, :, lo:], sc[i][:, :, lo:], rs[i].unsqueeze(2).to_broadcast([P, 4, DW - lo]), ALU.mult)\
                    .then_inc(p_ready, 1)

            def tile_b(u):
                dve.wait_ge(pT, u + 1)
                if u >= 1:
                    dve.wait_ge(pv, u)
                V.tensor_copy(pb, bank[6][:, :]).then_inc(pb_ready, 1)

            U = 2 * NT
            biased(0)
            for u in range(U):
                if u + 1 < U:
                    biased(u + 1)
                normal(u)
                tile_b(u)

            dve.wait_ge(d_resid, 16)
            for j in range(NT):
                for n in range(2):
                    dve.wait_ge(oproj, 2 * j + n + 1)
                    h = xs[:, j, n * 512:(n + 1) * 512]
                    V.tensor_tensor(h, h, bank[2 * j + n][:, :], ALU.add).then_inc(h2_done, 1)
                if j == 0:
                    dve.wait_ge(d_gain, 48)
                dve.wait_ge(h2_done, 2 * j + 2)
                dve.wait_ge(fstat, j + 1)
                V.scalar_tensor_tensor(out=xf[:, j, :], in0=xs[:, j, :], scalar=rstd[:, j:j + 1], in1=gain,
                                       op0=ALU.mult, op1=ALU.mult).then_inc(xf_ready, 1)
            for j in range(NT):
                dve.wait_ge(xfT, j + 1)
                src = bank[2 * j][:, :].rearrange("p (k t) -> p k t", k=4)
                V.tensor_copy(mixT[:, 0:4, j * P:(j + 1) * P], src).then_inc(hfT_v, 1)

            def first_max(v, n, m, i, t, oh):
                iota = cst[:, K_IOTA:K_IOTA + n].unsqueeze(1).to_broadcast([P, NT, n])
                step(V.tensor_reduce(m, v, AX, ALU.max))
                step(V.tensor_tensor(t, v, m.unsqueeze(2).to_broadcast([P, NT, n]), ALU.is_equal))
                step(V.scalar_tensor_tensor(out=t, in0=t, scalar=-float(FAR), in1=iota, op0=ALU.mult, op1=ALU.add))
                step(V.tensor_reduce(i, t, AX, ALU.min))
                step(V.tensor_tensor(oh, t, i.unsqueeze(2).to_broadcast([P, NT, n]), ALU.is_equal))

            dve.wait_ge(logits, NT)
            step(V.tensor_tensor(logit, bank[0][:, 0:NT * NR].rearrange("p (j n) -> p j n", j=NT),
                                 rbias[:, :].unsqueeze(1).to_broadcast([P, NT, NR]), ALU.add))
            step(V.tensor_copy(glog, logit[:, :, 0:NG]))
            first_max(glog, NG, gm, gi, t4, oh4)
            V.tensor_tensor(gexp, glog, gm.unsqueeze(2).to_broadcast([P, NT, NG]), ALU.subtract).then_inc(gdiff, 1)
            step(V.tensor_scalar(oh4, oh4, -NEG, NEG, ALU.mult, ALU.add))
            for j in range(NT):
                ins = V.tensor_tensor(ev[:, j, :].rearrange("p (g e) -> p g e", g=NG),
                                      logit[:, j, NG:].rearrange("p (g e) -> p g e", g=NG),
                                      oh4[:, j, :].unsqueeze(2).to_broadcast([P, NG, EPG]), ALU.add)
                mark(ins)
            dve.wait_ge(v_step, vn[0])
            first_max(ev, NE, m1, i1, t32, oh1)
            step(V.scalar_tensor_tensor(out=ev, in0=oh1, scalar=3 * NEG, in1=ev, op0=ALU.mult, op1=ALU.add))
            first_max(ev, NE, m2, i2, t32, oh2)
            V.tensor_tensor(wd, m2, m1, ALU.subtract).then_inc(ediff, 1)
            V.tensor_tensor(both, oh1, oh2, ALU.add).then_inc(picks, 1)
            dve.wait_ge(gprob, 1)
            step(V.tensor_reduce(gsum, gexp, AX, ALU.add))
            dve.wait_ge(eprob, 1)
            step(V.tensor_scalar(w1, wd, 1.0, None, ALU.add))
            step(V.tensor_tensor(w1, w1, gsum, ALU.mult))
            step(V.reciprocal(w1, w1))
            step(V.tensor_tensor(w2, w1, wd, ALU.mult))
            dve.wait_ge(ranks, 1)
            mark(V.tensor_copy(rank, bank[1][:, 0:NT * NE].rearrange("p (j e) -> p j e", j=NT)))
            step(V.tensor_copy(count, bank[1][:, NT * NE:NT * NE + NE]))
            thr = cst[:, K_THR:K_THR + NTHR]
            step(V.tensor_tensor(over, count.unsqueeze(2).to_broadcast([P, NE, NTHR]),
                                 thr.unsqueeze(1).to_broadcast([P, NE, NTHR]), ALU.is_gt))
            step(V.tensor_reduce(extra, over, AX, ALU.add))
            ones = cst[:, K_ONE:K_ONE + NE]
            step(V.tensor_tensor_scan(incl, ones, extra, 0.0, ALU.mult, ALU.add))
            mark(V.tensor_tensor(first, incl, extra, ALU.subtract))
            step(V.tensor_tensor(below, incl.unsqueeze(1).to_broadcast([P, MORE, NE]),
                                 cst[:, K_IOTA:K_IOTA + MORE].unsqueeze(2).to_broadcast([P, MORE, NE]), ALU.is_le))
            step(V.tensor_reduce(over[:, 0:MORE, 0], below, AX, ALU.add))
            mark(V.tensor_scalar(tab[0:1, 1:1 + MORE], over[0:1, 0:MORE, 0], float(NE - 1), None, ALU.min))
            mark(V.tensor_copy(tab[0:1, 0:1], incl[0:1, NE - 1:NE]))
            for k, oh, ie in ((0, oh1, i1), (1, oh2, i2)):
                step(V.tensor_tensor(t32, oh, rank, ALU.mult))
                step(V.tensor_reduce(rk[k], t32, AX, ALU.add))
                step(V.tensor_tensor(t32, oh, first.unsqueeze(1).to_broadcast([P, NT, NE]), ALU.mult))
                step(V.tensor_reduce(bk[k], t32, AX, ALU.add))
                step(V.tensor_tensor(over4, rk[k].unsqueeze(2).to_broadcast([P, NT, NTHR]),
                                     thr.unsqueeze(1).to_broadcast([P, NT, NTHR]), ALU.is_ge))
                step(V.tensor_reduce(qk, over4, AX, ALU.add))
                step(V.scalar_tensor_tensor(out=ck[k], in0=qk, scalar=-float(BC), in1=rk[k], op0=ALU.mult, op1=ALU.add))
                step(V.tensor_tensor(bk[k], bk[k], qk, ALU.add))
                step(V.tensor_scalar(ie, ie, float(FAR), None, ALU.add))
                step(V.scalar_tensor_tensor(out=bk[k], in0=bk[k], scalar=float(NE - 1), in1=ie, op0=ALU.add, op1=ALU.subtract))
                step(V.tensor_scalar(q1, qk, 1.0, None, ALU.min))
                step(V.tensor_tensor(bk[k], bk[k], q1, ALU.mult))
                step(V.tensor_tensor(bk[k], bk[k], ie, ALU.add))
            step(V.tensor_scalar(tokf, cst[:, K_TOK:K_TOK + NT], -float(FAR), None, ALU.add))
            step(V.tensor_scalar(tokf2, tokf, float(SEQ), None, ALU.add))
            for k in range(2):
                for j in range(NT):
                    mark(V.tensor_scalar(slot_is[:, k, j, :], cst[:, K_IOTA:K_IOTA + BC], ck[k][:, j:j + 1], None, ALU.is_equal))
                    for w, v in ((0, tokf), (1, tokf2 if k else tokf)):
                        ins = V.tensor_scalar(block_is[:, k, j, w, :], cst[:, K_IOTA:K_IOTA + NBLK], bk[k][:, j:j + 1],
                                              v[:, j:j + 1], ALU.is_equal, ALU.mult)
                        mark(ins)
            dve.wait_ge(v_step, vn[0])
            V.memset(count[0:1, 0:1], 0.0).then_inc(match, 1)
            dve.wait_ge(slots, 1)
            V.tensor_scalar(idx, bank[2][:, 0:2 * NBLK], float(FAR), None, ALU.add).then_inc(routed, 1)

        @block.tensor
        def _(pe):
            T = nc.tensor
            pe.wait_ge(d_cst, 16)
            pe.wait_ge(d_par, 96)
            T.transpose(bank[6][:, 0:78], rows[:, :], ident[0:78, 0:78]).then_inc(par_T, 1)
            pe.wait_ge(xn_ready, 1)
            for k in range(KT):
                ins = T.transpose(bank[7][:, k * META:(k + 1) * META], meta_x[:, k * P:(k + 1) * P], ident[0:META, 0:META])
            ins.then_inc(metaT, 1)
            for j in range(NT):
                pe.wait_ge(xn_ready, j + 2)
                if j == 0:
                    pe.wait_ge(cols_ready, 1)
                    pe.wait_ge(hT_v, 1)
                for k in range(KT):
                    ins = T.transpose(bank[k][:, j * P:(j + 1) * P], xs[:, j, k * P:(k + 1) * P], ident)
                ins.then_inc(xT_done, 1)
            pe.wait_ge(hT_v, 5)
            pe.wait_ge(hT_a, 4)

            def freed(n):
                i = PROD.index(n) - 4
                old = [PROD[i]] if i >= 0 else []
                if n in WITH_META and WITH_META.index(n) >= 2:
                    old.append(WITH_META[WITH_META.index(n) - 2])
                for o in old:
                    if o[0] == "a":
                        pe.wait_ge(glu_done, int(o[1]) + 1)
                    else:
                        pe.wait_ge(evac, taken(o))

            def product_of(n):
                freed(n)
                out_b = pbank(n)
                if n[0] == "v":
                    pe.wait_ge(d_win[5], 16)
                    pe.wait_ge(d_win[6], 16)
                    rws = META if n == "vm" else P
                    t0 = 0 if n == "vm" else META + P * int(n[1])
                    for c0, n0, w in ((C_V, 0, P), (C_HI, P, 256)):
                        for k in range(KT):
                            ins = T.matmul(out_b[0:rws, n0:n0 + w], hT[:, k, t0:t0 + rws], w_in_sb[:, k, c0:c0 + w],
                                           start=(k == 0), stop=(k == KT - 1))
                else:
                    pe.wait_ge(d_win[LOAD_OF[n.rstrip("0123")]], 16)
                    for k in range(KT):
                        w = w_in_sb[:, k, COL[n]:COL[n] + P]
                        ins = T.matmul(out_b[:, :], w, hT[:, k, META:], start=(k == 0), stop=(k == KT - 1))
                        if n in WITH_META:
                            ins = T.matmul(mcols(n), w, hT[:, k, 0:META], start=(k == 0), stop=(k == KT - 1))
                ins.then_inc(product, 1)

            for n in PROD:
                product_of(n)

            pe.wait_ge(kb_ready, 1)
            for ti in range(2):
                for r in range(4):
                    T.transpose(bank[5 + ti][:, r * P:(r + 1) * P], kb[:, ti, META + r * P:META + (r + 1) * P], ident)
                ins = T.transpose(bank[7][0:META, ti * P:(ti + 1) * P], kb[:, ti, 0:META], ident)
                ins.then_inc(kbT, 1)
            pe.wait_ge(evac, len(EVAC))
            pe.wait_ge(k2_a, 4)
            pe.wait_ge(k2_v, 6)
            for c in range(NC_):
                o = bank[c // 4][:, (c % 4) * P:(c % 4) * P + P].rearrange("p (i e) -> p i e", i=2)
                for ti in range(2):
                    for hp in range(2):
                        s = slice(hp * HD, hp * HD + HD)
                        if c == 0:
                            sm = slice(hp * HD, hp * HD + META)
                            ins = T.matmul(o[s, ti, :], k2m[sm, ti, :], v2m[sm, ti, :], start=True, stop=True)
                        else:
                            ins = T.matmul(o[s, ti, :], k2[s, c - 1, ti, :], v2[s, c - 1, ti, :], start=True, stop=True)
            ins.then_inc(u_done, 1)
            pe.wait_ge(conv_done, 2)
            mean = cst[:, K_MEAN:K_MEAN + P]
            for i in range(2):
                ins = T.matmul(bank[7][:, :], mean, mixT[:, i, :], start=(i == 0), stop=(i == 1))
            ins.then_inc(mean_done, 1)
            nl = len(LEVELS)
            pe.wait_ge(kf_ready, 1)
            for n in range(2 * (nl + 1)):
                ti, l = n % 2, (nl - n // 2)
                if l < nl:
                    pe.wait_ge(lev_w, l + 1)
                if n >= 2:
                    pe.wait_ge(g_used, n - 1)
                for c in range(NC_):
                    for hp in range(2):
                        s = slice(hp * HD, hp * HD + HD)
                        t = slice(c * CHUNK, (c + 1) * CHUNK)
                        if l == nl:
                            kk, qq = kf[s, ti, META + c * CHUNK:META + (c + 1) * CHUNK], qf[s, ti, t]
                        else:
                            kk = qq = lev[l][s, ti, t]
                        ins = T.matmul(bank[2 + n % 2][s, t], kk, qq, start=True, stop=True)
                ins.then_inc(g_done, 1)
            pe.wait_ge(csq, 1)
            for i in range(2):
                ins = T.matmul(bank[4][:, :], mean, osq[:, i, :], start=(i == 0), stop=(i == 1))
            ins.then_inc(var_done, 1)
            pe.wait_ge(g_used, 2 * (nl + 1))
            pe.wait_ge(state_done, 1)
            for ti in range(2):
                for c in range(NC_):
                    for hp in range(2):
                        s = slice(hp * HD, hp * HD + HD)
                        t = slice(c * CHUNK, (c + 1) * CHUNK)
                        T.matmul(bank[ti][s, t], v2[s, c, ti, :], A[s, ti, t], start=True, stop=False)
                        ins = T.matmul(bank[ti][s, t], state[s, c, ti, :], qb[s, ti, t], start=False, stop=True)
                ins.then_inc(o_done, 1)
            for ti in range(2):
                pe.wait_ge(osq_done, ti + 1)
                T.matmul(bank[2 + ti][:, :], cst[:, K_HEAD:K_HEAD + P], osq[:, ti, :], start=True, stop=True).then_inc(ms_done, 1)

            def scores(u):
                p, g, i = u // 2, u % 2, u % 2
                if u >= 2:
                    pe.wait_ge(s_ready, u - 1)
                for h in range(4):
                    s = slice((h % 2) * HD, (h % 2) * HD + HD)
                    q = qT[s, 2 * g + h // 2, p * P:(p + 1) * P]
                    o = bank[2 * i + h % 2][:, (h // 2) * DW:(h // 2 + 1) * DW]
                    t0 = META + p * P
                    if p:
                        T.matmul(o[:, 0:HD], q, kT[s, g, t0 - CHUNK:t0], start=True, stop=True)
                    T.matmul(o[:, HD:HD + META], q, kT[s, g, 0:META], start=True, stop=True)
                    ins = T.matmul(o[:, HD + META:], q, kT[s, g, t0:t0 + P], start=True, stop=True)
                ins.then_inc(s_done, 1)

            def turn(u):
                pe.wait_ge(p_ready, u + 1)
                i = u % 2
                if u >= 1:
                    pe.wait_ge(pa_ready, u)
                    pe.wait_ge(pb_ready, u)
                lo = HD if u < 2 else 0
                for h in range(4):
                    T.transpose(bank[5][0:HD + META - lo, h * P:(h + 1) * P], sc[i][:, h, lo:HD + META], ident)
                    ins = T.transpose(bank[6][:, h * P:(h + 1) * P], sc[i][:, h, HD + META:], ident)
                ins.then_inc(pT, 1)

            def values(u):
                p, g = u // 2, u % 2
                pe.wait_ge(pa_ready, u + 1)
                pe.wait_ge(pb_ready, u + 1)
                if u >= 2:
                    pe.wait_ge(y_a, u - 1)
                for h in range(4):
                    o = bank[7 - 3 * (u % 2)][(h % 2) * HD:(h % 2) * HD + HD, (h // 2) * P:(h // 2 + 1) * P]
                    e = slice(g * HD, g * HD + HD)
                    if p == 0:
                        T.matmul(o, vm[0:META, e], pa[0:META, h * P:(h + 1) * P], start=True, stop=False)
                    else:
                        T.matmul(o, vp[0:HD + META, p, e], pa[0:HD + META, h * P:(h + 1) * P], start=True, stop=False)
                    ins = T.matmul(o, va[:, p, e], pb[:, h * P:(h + 1) * P], start=False, stop=True)
                ins.then_inc(pv, 1)

            pe.wait_ge(y_h, 2)
            pe.wait_ge(cen_done, 2)
            U = 2 * NT
            scores(0)
            for u in range(U):
                if u + 1 < U:
                    scores(u + 1)
                turn(u)
                values(u)

            for i in range(2):
                pe.wait_ge(d_wout[i], 16)
            pe.wait_ge(y_c, 2)
            pe.wait_ge(y_a, 2 * NT)
            for j in range(NT):
                for n in range(2):
                    for k in range(KT):
                        ins = T.matmul(bank[2 * j + n][:, :], mixT[:, k, j * P:(j + 1) * P], w_out_sb[:, k, n * 512:(n + 1) * 512],
                                       start=(k == 0), stop=(k == KT - 1))
                    ins.then_inc(oproj, 1)
            for j in range(NT):
                pe.wait_ge(xf_ready, j + 1)
                for k in range(KT):
                    ins = T.transpose(bank[2 * j + k // 4][:, (k % 4) * P:(k % 4 + 1) * P], xf[:, j, k * P:(k + 1) * P], ident)
                ins.then_inc(xfT, 1)
            pe.wait_ge(d_rt, 64)
            for j in range(NT):
                pe.wait_ge(hfT_a, j + 1)
                pe.wait_ge(hfT_v, j + 1)
                for k in range(KT):
                    ins = T.matmul(bank[0][:, j * NR:(j + 1) * NR], mixT[:, k, j * P:(j + 1) * P], wr[:, k, :],
                                   start=(k == 0), stop=(k == KT - 1))
                ins.then_inc(logits, 1)
            pe.wait_ge(picks, 1)
            tri, ones = cst[:, K_TRI:K_TRI + P], cst[:, K_ONE:K_ONE + P]
            for j in range(NT + 1):
                o = bank[1][:, j * NE:(j + 1) * NE]
                for i in range(j):
                    ins = T.matmul(o, ones, both[:, i, :], start=(i == 0), stop=(i == j - 1 and j == NT))
                if j < NT:
                    T.matmul(o, tri, both[:, j, :], start=(j == 0), stop=True)
            ins.then_inc(ranks, 1)
            pe.wait_ge(match, 1)
            for k in range(2):
                for j in range(NT):
                    ins = T.matmul(bank[2][:, 0:2 * NBLK], slot_is[:, k, j, :],
                                   block_is[:, k, j, :, :].rearrange("p w b -> p (w b)"),
                                   start=(k == j == 0), stop=(k == 1 and j == NT - 1))
            ins.then_inc(slots, 1)
        @block.gpsimd
        def _(pool):

            Q = nc.gpsimd
            Q.dma_start(wr[:, :, 0:NG], w_router_group[0].rearrange("(k p) n -> p k n", p=P)).then_inc(d_rt, 16)
            Q.dma_start(wr[:, :, NG:], w_router_expert[0].rearrange("(k p) n -> p k n", p=P)).then_inc(d_rt, 16)
            Q.dma_start(rbias[:, 0:NG], b_router_group[0:1, :].to_broadcast([P, NG])).then_inc(d_rt, 16)
            Q.dma_start(rbias[:, NG:], b_router_expert[0:1, :].to_broadcast([P, NE])).then_inc(d_rt, 16)
            Q.dma_start(gain, ffn_norm[0:1, :].to_broadcast([P, D])).then_inc(d_gain, 16)
            Q.dma_start(gain_out, final_norm.rearrange("(a d) -> a d", a=1).to_broadcast([P, D])).then_inc(d_gain, 32)

        mixer_ctx.close()

        split = sb("split", [P, 3, 2, PIECE], F32R)
        xT = sb("xT", [P, 2, 2, KT * BC], F32R)
        aT = sb("aT", [P, 2, 2 * BC], F32R)
        xg = [sb(f"xg{i}", [P, D])[:, :] for i in range(2)]
        yb = [sb(f"yb{i}", [P, D])[:, :] for i in range(2)]
        sg = sb("sg", [P, DE])[:, :]
        ab = sb("ab", [P, DE])[:, :]
        HI, LO = 0, 1

        def piece_views(c, part):
            if c < 2:
                return (lambda r: r.rearrange("p (w k n) -> p k w n", w=2, n=DE)), \
                    split[:, c, part, :].rearrange("p (k w n) -> p k w n", w=2, n=DE)
            return (lambda r: r), split[:, c, part, :]

        def plain(a):
            return a.bitcast(F32)

        def gate_up(T, out_b, u, c):
            w = [split[:, c, part, :].rearrange("p (k n) -> p k n", k=KT // 2) for part in (HI, LO)]
            for k in range(KT // 2):
                kk = c * (KT // 2) + k
                x_hi, x_lo = (xT[:, u, part, kk * BC:(kk + 1) * BC] for part in (HI, LO))
                T.matmul(out_b, x_hi, w[HI][:, k, :], start=(kk == 0), stop=False)
                T.matmul(out_b, x_hi, w[LO][:, k, :], start=False, stop=False)
                ins = T.matmul(out_b, x_lo, w[HI][:, k, :], start=False, stop=(kk == KT - 1))
            return ins

        def down(T):
            w = [split[:, 2, part, :].rearrange("p (f n) -> p f n", f=2) for part in (HI, LO)]
            for f in range(2):
                a_hi, a_lo = (aT[:, part, f * BC:(f + 1) * BC] for part in (HI, LO))
                for a, part, start, stop in ((a_hi, HI, f == 0, False), (a_hi, LO, False, False), (a_lo, HI, False, f == 1)):
                    for h in range(2):
                        ins = T.matmul(bank[5 + h][:, :], a, w[part][:, f, h * 512:(h + 1) * 512], start=start, stop=stop)
            return ins

        def turn_x(T, src):
            cols_of = src[:, :].rearrange("p (d k) -> p k d", k=KT)
            for k in range(KT):
                ins = T.transpose(bank[2 + k // 4][:, (k % 4) * BC:(k % 4 + 1) * BC], cols_of[:, k, :], ident)
            return ins

        def turn_act(T):
            cols_of = ab[:, :].rearrange("p (d f) -> p f d", f=2)
            for f in range(2):
                ins = T.transpose(bank[4][:, f * BC:(f + 1) * BC], cols_of[:, f, :], ident)
            return ins

        experts = ctx.enter_context(nc.Block())

        @experts.sync
        def _(sp):
            def load_step(g, r, only=(0, 1, 2)):
                for c in only:
                    slot = (3 * r + c) % RAW
                    if isinstance(g, int):
                        of = lambda w: w[0, 4 * g + r - (c == 2)]
                    else:
                        of = lambda w: w[0, bass.ds(g * 4 + (r - (c == 2)), 1)].rearrange("a k n -> (a k) n")
                    v = g * 12 + (3 * r + c - RAW)
                    sp.wait_ge(lo_done, through(v))
                    sp.sem_inc(passed, 1)
                    if c < 2:
                        load_gate_up(sp, of, c, slot, d_raw[slot])
                    else:
                        load_down(sp, of, slot, d_raw[slot])

            load_step(0, 1, (1, 2))
            load_step(0, 2)
            load_step(0, 3)
            with sp.Fori(1, NE // 4) as g:
                for r in range(4):
                    load_step(g, r)
            load_step(NE // 4, 0, (2,))

            more = sp.value_load(tab[0:1, 0:1], min_val=0, max_val=MORE)
            with sp.If(more > 0):
                with sp.Fori(0, more) as m:
                    e = sp.value_load(tab[0:1, bass.ds(m + 1, 1)], min_val=0, max_val=NE - 1)
                    of = lambda w: w[0, bass.ds(e, 1)].rearrange("a k n -> (a k) n")
                    sp.wait_ge(m_free, m + 1)
                    sp.sem_inc(passed, 1)
                    for c in range(2):
                        load_gate_up(sp, of, c, c, m_w)
                    load_down(sp, of, 2, m_w)
            for u in range(2):
                sp.wait_ge(d_sc[u], 16 * (NE // 2))
            sp.wait_ge(m_free, more + 1)
            sp.sem_inc(passed, 1)
            for j in range(NT):
                for k in range(2):
                    sp.dma_start(ye[k][:, j, :], expert_out[k * SEQ + j * P:k * SEQ + (j + 1) * P, :]).then_inc(d_ye[j], 16)
            for j in range(NT):
                sp.wait_ge(o_ready, j + 1)
                sp.dma_start(out[0, j * P:(j + 1) * P, :], xs[:, j, :]).then_inc(d_out, 16)
            sp.wait_ge(d_out, 16 * NT)

        @experts.scalar
        def _(act):
            A_ = nc.scalar
            an = [0]

            def hi_piece(c, slot):
                view, dst = piece_views(c, HI)
                return A_.activation(dst, view(raw[slot]), ACT.Copy)

            def hi(g, r, c):
                v = g * 12 + (3 * r + c)
                slot = (3 * r + c) % RAW
                if isinstance(v, int):
                    act.wait_ge(d_raw[slot], 32 * (v // RAW + (slot != 2)))
                    if v >= 3:
                        act.wait_ge(piece_used, through(v - 3))
                else:
                    act.wait_ge(d_raw[slot], g * 96 + 32 * ((3 * r + c) // RAW + (slot != 2)))
                    act.wait_ge(piece_used, through(v - 3))
                hi_piece(c, slot).then_inc(hi_done, 1)

            def x_hi(e, u):
                act.wait_ge(xT_made, e + 1)
                for h in range(2):
                    A_.activation(xT[:, u, HI, h * 512:(h + 1) * 512], bank[2 + h][:, :], ACT.Copy).then_inc(xT_hi, 1)

            def a_hi(e):
                act.wait_ge(aT_made, e + 1)
                A_.activation(aT[:, HI, :], bank[4][:, 0:2 * BC], ACT.Copy).then_inc(aT_hi, 1)

            def silu_of(g, r):
                e = g * 4 + r
                act.wait_ge(piece_used, through(g * 12 + (3 * r + 1)))
                if not isinstance(e, int) or e >= 1:
                    act.wait_ge(act_ready, e)
                A_.activation(sg, bank[r % 2][:, 0:DE], ACT.Silu).then_inc(sg_ready, 1)

            def y_out(g, r):
                u = (r - 1) % 2
                act.wait_ge(piece_used, through(g * 12 + (3 * r + 2)))
                n = g * 2 + (r - 1 - u) // 2
                if not isinstance(n, int) or n >= 1:
                    act.wait_ge(d_sc[u], n * 16)
                for h in range(2):
                    A_.activation(yb[u][:, h * 512:(h + 1) * 512], bank[5 + h][:, :], ACT.Copy).then_inc(y_ready, 1)

            def step_act(g, r, last=False):
                e = g * 4 + r
                busy = not isinstance(e, int) or e >= 1
                if busy:
                    hi(g, r, 2)
                    a_hi(e - 1)
                if not last:
                    x_hi(e + 1, (r + 1) % 2)
                    hi_next(g, r, 0)
                    silu_of(g, r)
                    hi_next(g, r, 1)
                if busy:
                    y_out(g, r)

            def hi_next(g, r, c):
                if r < 3:
                    hi(g, r + 1, c)
                else:
                    hi(g + 1, 0, c)

            x_hi(0, 0)
            hi(0, 0, 0)
            hi(0, 0, 1)
            for r in range(4):
                step_act(0, r)
            with act.Fori(1, NE // 4 - 1) as g:
                for r in range(4):
                    step_act(g, r)
            g = NE // 4 - 1
            for r in range(3):
                step_act(g, r)
            hi(g, 3, 2)
            a_hi(NE - 2)
            x_hi(NE, 0)
            silu_of(g, 3)
            y_out(g, 3)
            hi(NE // 4, 0, 2)
            a_hi(NE - 1)
            y_out(NE // 4, 0)

            more = act.value_load(tab[0:1, 0:1], min_val=0, max_val=MORE)
            with act.If(more > 0):
                with act.Fori(0, more) as m:
                    act.wait_ge(m_xT, m + 1)
                    for h in range(2):
                        A_.activation(xT[:, 0, HI, h * 512:(h + 1) * 512], bank[2 + h][:, :], ACT.Copy).then_inc(m_xhi, 1)
                    act.wait_ge(m_w, m * 96 + 96)
                    for c in range(3):
                        hi_piece(c, c).then_inc(m_hi, 1)
                    act.wait_ge(m_gu, m + 1)
                    A_.activation(sg, bank[0][:, 0:DE], ACT.Silu).then_inc(m_sg, 1)
                    act.wait_ge(m_aT, m + 1)
                    A_.activation(aT[:, HI, :], bank[4][:, 0:2 * BC], ACT.Copy).then_inc(m_ahi, 1)
                    act.wait_ge(m_down, m + 1)
                    for h in range(2):
                        A_.activation(yb[0][:, h * 512:(h + 1) * 512], bank[5 + h][:, :], ACT.Copy).then_inc(m_y, 1)

            act.preload_act_table_set("natural_log_exp_and_others")
            for j in range(NT):
                act.wait_ge(summed, j + 1)
                A_.activation(area_w[:, JUNK:JUNK + D], xs[:, j, :], ACT.Square, accum_out=ss[:, j:j + 1]).then_inc(nstep, 1)
                act.wait_ge(nstep, 2 * j + 1)
                A_.activation(rstd[:, j:j + 1], ss[:, j:j + 1], ACT.Ln, bias=eps, scale=1.0 / D).then_inc(nstep, 1)
                act.wait_ge(nstep, 2 * j + 2)
                A_.activation(rstd[:, j:j + 1], rstd[:, j:j + 1], ACT.Exp, scale=-0.5).then_inc(ostat, 1)

        @experts.vector
        def _(dve):
            V = nc.vector

            def lo_piece(c, slot):
                view, dst = piece_views(c, LO)
                _, top = piece_views(c, HI)
                return V.tensor_tensor(dst, view(raw[slot]), plain(top), ALU.subtract)

            def lo(g, r, c):
                dve.wait_ge(hi_done, through(g * 12 + (3 * r + c)))
                lo_piece(c, (3 * r + c) % RAW).then_inc(lo_done, 1)

            def lo_next(g, r, c):
                if r < 3:
                    lo(g, r + 1, c)
                else:
                    lo(g + 1, 0, c)

            def x_lo(e, u):
                for h in range(2):
                    dve.wait_ge(xT_hi, e * 2 + (h + 1))
                    s_ = slice(h * 512, (h + 1) * 512)
                    V.tensor_tensor(xT[:, u, LO, s_], bank[2 + h][:, :], plain(xT[:, u, HI, s_]), ALU.subtract).then_inc(xT_lo, 1)

            def a_lo(e):
                dve.wait_ge(aT_hi, e + 1)
                V.tensor_tensor(aT[:, LO, :], bank[4][:, 0:2 * BC], plain(aT[:, HI, :]), ALU.subtract).then_inc(aT_lo, 1)

            def gated(e, u):
                dve.wait_ge(sg_ready, e + 1)
                if not isinstance(e, int) or e >= 1:
                    dve.wait_ge(aT_made, e)
                V.tensor_tensor(ab, sg, bank[u][:, DE:2 * DE], ALU.mult).then_inc(act_ready, 1)

            def step_dve(g, r):
                e = g * 4 + r
                if not isinstance(e, int) or e >= 1:
                    lo(g, r, 2)
                    a_lo(e - 1)
                x_lo(e + 1, (r + 1) % 2)
                lo_next(g, r, 0)
                gated(e, r % 2)
                lo_next(g, r, 1)

            x_lo(0, 0)
            lo(0, 0, 0)
            lo(0, 0, 1)
            for r in range(4):
                step_dve(0, r)
            with dve.Fori(1, NE // 4 - 1) as g:
                for r in range(4):
                    step_dve(g, r)
            g = NE // 4 - 1
            for r in range(3):
                step_dve(g, r)
            lo(g, 3, 2)
            a_lo(NE - 2)
            x_lo(NE, 0)
            gated(NE - 1, 1)
            lo(NE // 4, 0, 2)
            a_lo(NE - 1)

            more = dve.value_load(tab[0:1, 0:1], min_val=0, max_val=MORE)
            with dve.If(more > 0):
                with dve.Fori(0, more) as m:
                    for h in range(2):
                        dve.wait_ge(m_xhi, m * 2 + (h + 1))
                        s_ = slice(h * 512, (h + 1) * 512)
                        V.tensor_tensor(xT[:, 0, LO, s_], bank[2 + h][:, :], plain(xT[:, 0, HI, s_]), ALU.subtract).then_inc(m_xlo, 1)
                    for c in range(3):
                        dve.wait_ge(m_hi, m * 3 + (c + 1))
                        lo_piece(c, c).then_inc(m_lo, 1)
                    dve.wait_ge(m_sg, m + 1)
                    V.tensor_tensor(ab, sg, bank[0][:, DE:2 * DE], ALU.mult).then_inc(m_act, 1)
                    dve.wait_ge(m_ahi, m + 1)
                    V.tensor_tensor(aT[:, LO, :], bank[4][:, 0:2 * BC], plain(aT[:, HI, :]), ALU.subtract).then_inc(m_alo, 1)

            for j in range(NT):
                dve.wait_ge(d_ye[j], 32)
                V.scalar_tensor_tensor(out=xs[:, j, :], in0=ye[0][:, j, :], scalar=w1[:, j:j + 1], in1=xs[:, j, :],
                                       op0=ALU.mult, op1=ALU.add).then_inc(first_sum, 1)
                dve.wait_ge(first_sum, j + 1)
                V.scalar_tensor_tensor(out=xs[:, j, :], in0=ye[1][:, j, :], scalar=w2[:, j:j + 1], in1=xs[:, j, :],
                                       op0=ALU.mult, op1=ALU.add).then_inc(summed, 1)
            for j in range(NT):
                dve.wait_ge(ostat, j + 1)
                V.scalar_tensor_tensor(out=xs[:, j, :], in0=xs[:, j, :], scalar=rstd[:, j:j + 1], in1=gain_out,
                                       op0=ALU.mult, op1=ALU.mult).then_inc(o_ready, 1)

        @experts.tensor
        def _(pe):
            T = nc.tensor

            def x_turn(e, u, n):
                pe.wait_ge(d_xg[u], n)
                if not isinstance(e, int) or e >= 1:
                    pe.wait_ge(xT_lo, e * 2)
                pe.sem_inc(passed, 1)
                turn_x(T, xg[u]).then_inc(xT_made, 1)

            def half(g, r, c):
                e = g * 4 + r
                pe.wait_ge(lo_done, through(g * 12 + (3 * r + c)))
                if c == 0:
                    pe.wait_ge(xT_lo, e * 2 + 2)
                    if not isinstance(e, int) or e >= 2:
                        pe.wait_ge(act_ready, e - 1)
                gate_up(T, bank[r % 2][:, :], r % 2, c).then_inc(piece_used, 1)

            def act_turn(e):
                pe.wait_ge(act_ready, e + 1)
                if not isinstance(e, int) or e >= 1:
                    pe.wait_ge(aT_lo, e)
                pe.sem_inc(passed, 1)
                turn_act(T).then_inc(aT_made, 1)

            def third(g, r):
                e = g * 4 + (r - 1)
                pe.wait_ge(lo_done, through(g * 12 + (3 * r + 2)))
                pe.wait_ge(aT_lo, e + 1)
                if not isinstance(e, int) or e >= 1:
                    pe.wait_ge(y_ready, e * 2)
                down(T).then_inc(piece_used, 1)

            def step_pe(g, r):
                e = g * 4 + r
                busy = not isinstance(e, int) or e >= 1
                half(g, r, 0)
                if busy:
                    act_turn(e - 1)
                x_turn(e + 1, (r + 1) % 2, g * 32 + 16 * ((r + 1) // 2 + 1))
                half(g, r, 1)
                if busy:
                    third(g, r)

            x_turn(0, 0, 16)
            for r in range(4):
                step_pe(0, r)
            with pe.Fori(1, NE // 4) as g:
                for r in range(4):
                    step_pe(g, r)
            act_turn(NE - 1)
            third(NE // 4, 0)

            more = pe.value_load(tab[0:1, 0:1], min_val=0, max_val=MORE)
            with pe.If(more > 0):
                with pe.Fori(0, more) as m:
                    pe.wait_ge(m_xg, m * 16 + 16)
                    pe.sem_inc(passed, 1)
                    turn_x(T, xg[0]).then_inc(m_xT, 1)
                    pe.wait_ge(m_xlo, m * 2 + 2)
                    for c in range(2):
                        pe.wait_ge(m_lo, m * 3 + (c + 1))
                        ins = gate_up(T, bank[0][:, :], 0, c)
                    ins.then_inc(m_gu, 1)
                    pe.wait_ge(m_act, m + 1)
                    pe.sem_inc(passed, 1)
                    turn_act(T).then_inc(m_aT, 1)
                    pe.wait_ge(m_alo, m + 1)
                    pe.wait_ge(m_lo, m * 3 + 3)
                    down(T).then_inc(m_down, 1)

        @experts.gpsimd
        def _(pool):
            Q = nc.gpsimd
            for i in range(2):
                Q.memset(xg[i], 0.0).then_inc(xg_clear, 1)
            pool.wait_ge(xg_clear, 2)

            def gather(u, column, steps, d):
                Q.tensor_copy(col_g[u], idx[:, column]).then_inc(col_ready, 1)
                pool.wait_ge(col_ready, steps)
                pool.sem_inc(passed, 1)
                Q.indirect_dma_start(xg[u], None, normed, bass.IndirectOffsetOnAxis(ap=col_g[u].bitcast(U32), axis=0),
                                     bounds_check=SEQ - 1, oob_is_err=False).then_inc(d, 16)

            def scatter(u, column, steps, d):
                Q.tensor_copy(col_s[u], idx[:, column]).then_inc(col_ready, 1)
                pool.wait_ge(col_ready, steps)
                pool.sem_inc(passed, 1)
                Q.indirect_dma_start(expert_out, bass.IndirectOffsetOnAxis(ap=col_s[u].bitcast(U32), axis=0), yb[u], None,
                                     bounds_check=2 * SEQ - 1, oob_is_err=False).then_inc(d, 16)

            def step_pool(g, r):
                e = g * 4 + r
                pool.wait_ge(xT_made, e + 1)
                pool.sem_inc(passed, 1)
                at_g = slice(e + 2, e + 3) if isinstance(e, int) else bass.ds(e + 2, 1)
                gather(r % 2, at_g, 3 if isinstance(e, int) and e == 0 else e * 2 + 2, d_xg[r % 2])
                if not isinstance(e, int) or e >= 1:
                    pool.wait_ge(y_ready, e * 2)
                    pool.sem_inc(passed, 1)
                    at_s = slice(NBLK + e - 1, NBLK + e) if isinstance(e, int) else bass.ds(e + (NBLK - 1), 1)
                    scatter((r - 1) % 2, at_s, e * 2 + 3, d_sc[(r - 1) % 2])

            gather(0, slice(0, 1), 1, d_xg[0])
            gather(1, slice(1, 2), 2, d_xg[1])
            for r in range(4):
                step_pool(0, r)
            with pool.Fori(1, NE // 4) as g:
                for r in range(4):
                    step_pool(g, r)
            pool.wait_ge(y_ready, 2 * NE)
            scatter(1, slice(NBLK + NE - 1, NBLK + NE), 2 * NE + 2, d_sc[1])
            for u in range(2):
                pool.wait_ge(d_xg[u], 16 * (NE // 2 + 1))
                pool.wait_ge(d_sc[u], 16 * (NE // 2))
            pool.sem_inc(m_free, 1)
            more = pool.value_load(tab[0:1, 0:1], min_val=0, max_val=MORE)
            with pool.If(more > 0):
                with pool.Fori(0, more) as m:
                    pool.wait_ge(m_free, m + 1)
                    pool.sem_inc(passed, 1)
                    gather(0, bass.ds(m + NE, 1), m * 2 + (2 * NE + 3), m_xg)
                    pool.wait_ge(m_y, m * 2 + 2)
                    pool.sem_inc(passed, 1)
                    scatter(0, bass.ds(m + (NBLK + NE), 1), m * 2 + (2 * NE + 4), m_sc)
                    pool.wait_ge(m_sc, m * 16 + 16)
                    pool.sem_inc(m_free, 1)


_INS = ["x", "meta_tokens", "mix_norm", "w_in", "conv_dw_w", "conv_dw_b", "conv_ln_g", "conv_ln_b", "attn_sinks",
        "hgrn_norm_g", "w_out", "ffn_norm", "w_router_group", "b_router_group", "w_router_expert",
        "b_router_expert", "w_exp_gate", "w_exp_up", "w_exp_down", "final_norm"]


def kernel(**inputs):
    import numpy as _np
    import concourse.bacc as _bacc
    from concourse import mybir as _mybir
    from concourse.bass_utils import run_bass_kernel_spmd as _run

    nc = _bacc.Bacc("TRN2", target_bir_lowering=False, num_devices=1)
    arrays, args = {}, []
    for name in _INS:
        a = _np.ascontiguousarray(inputs[name])
        arrays[f"in_{name}"] = a
        args.append(nc.dram_tensor(f"in_{name}", a.shape, _mybir.dt.from_np(a.dtype), kind="ExternalInput").ap())
    arrays["in_table"] = shape_constants()
    args.append(nc.dram_tensor("in_table", arrays["in_table"].shape, F32, kind="ExternalInput").ap())
    normed = nc.dram_tensor("normed", (SEQ, D), F32, kind="Internal").ap()
    expert_out = nc.dram_tensor("expert_out", (2 * SEQ, D), F32, kind="Internal").ap()
    out = nc.dram_tensor("out_0", (1, SEQ, D), F32, kind="ExternalOutput").ap()
    trunk(nc, *args, normed, expert_out, out)
    r = _run(nc, [arrays], core_ids=[0])
    return r.results[0]["out_0"]
```

```python
import numpy as np
import concourse.bass as bass
from concourse import mybir
from contextlib import ExitStack

F32 = mybir.dt.float32
F32R = mybir.dt.float32r
I32 = mybir.dt.int32
U32 = mybir.dt.uint32
ALU = mybir.AluOpType
ACT = mybir.ActivationFunctionType
AX = mybir.AxisListType.X

P = 128
D = 1024
KT = D // P
SEQ = 512
NT = SEQ // P
META = 16
CHUNK = 64
NC_ = SEQ // CHUNK
TAPS = 31
HD = 64
NQ, NKV = 8, 2
NE, NG, EPG = 32, 4, 8
DE = 256
EPS = 1e-6
LEVELS = (32, 16, 8, 4, 2, 1)
BC = 128
MORE = 2 * SEQ // BC
NBLK = NE + MORE
XS = 4
HALF = BC // 2
FEW = HALF // 2
T_SIZE = 1 + MORE
FAR = 8192
NEG = -1.0e30

C_A, C_GATE, C_Q, C_K, C_V = 0, 256, 512, 1024, 1152
C_HQ, C_HF, C_HI, C_HG = 1280, 1536, 1792, 2048
D_IN = 2304

K_ID = 0
K_ONE = K_ID + P
K_EPS = K_ONE + P
K_FIRST = K_EPS + 1
K_TRI = K_FIRST
K_MEAN = K_TRI + P
K_HEAD = K_MEAN + P
K_RESET = K_HEAD + P
K_MASK = K_RESET + SEQ
K_DIST = K_MASK + (len(LEVELS) + 1) * CHUNK
DW = CHUNK + META + P
K_IOTA = K_DIST + NT * DW
K_TOK = K_IOTA + P
K_THR = K_TOK + NT
NTHR = SEQ // BC - 1
K_ALL = K_THR + NTHR


def shape_constants():
    c = np.zeros((P, K_ALL), np.float32)
    i = np.arange(P)
    c[:, K_ID:K_ID + P] = np.eye(P)
    c[:, K_TRI:K_TRI + P] = i[:, None] < i[None, :]
    c[:, K_ONE:K_ONE + P] = 1.0
    c[:, K_MEAN:K_MEAN + P] = 1.0 / 256
    c[:, K_HEAD:K_HEAD + P] = (i[:, None] // HD == i[None, :] // HD) / HD
    c[:, K_RESET:K_RESET + SEQ] = np.arange(SEQ)[None] % CHUNK != 0
    s, t = i[:, None] % CHUNK, np.arange(CHUNK)[None, :]
    for n, h in enumerate(LEVELS):
        same = s // (2 * h) == t // (2 * h)
        c[:, K_MASK + n * CHUNK:K_MASK + (n + 1) * CHUNK] = same & (s % (2 * h) < h) & (t % (2 * h) >= h)
    n = len(LEVELS)
    c[:, K_MASK + n * CHUNK:K_MASK + (n + 1) * CHUNK] = s == t
    for p in range(NT):
        q = META + P * p + i[:, None]
        k = np.concatenate([META + P * p - CHUNK + np.arange(CHUNK), np.arange(META), META + P * p + np.arange(P)])
        d = -np.abs(q - k[None, :]).astype(np.float32)
        d[CHUNK:, :CHUNK] = NEG
        d[:CHUNK, CHUNK + META + CHUNK:] = NEG
        c[:, K_DIST + p * DW:K_DIST + (p + 1) * DW] = d
    c[:, K_IOTA:K_IOTA + P] = np.arange(P)[None]
    c[:, K_TOK:K_TOK + NT] = i[:, None] + P * np.arange(NT)[None]
    c[:, K_THR:K_THR + NTHR] = BC * np.arange(1, NTHR + 1)[None]
    c[:, K_EPS] = EPS
    return c


def trunk(nc, x, meta_tokens, mix_norm, w_in, conv_dw_w, conv_dw_b, conv_ln_g, conv_ln_b, attn_sinks,
          hgrn_norm_g, w_out, ffn_norm, w_router_group, b_router_group, w_router_expert,
          b_router_expert, w_exp_gate, w_exp_up, w_exp_down, final_norm, table, normed, expert_out, out):
    ctx = ExitStack()
    with ctx:
        mixer_ctx = ExitStack()

        def sb(name, shape, dt=F32, of=ctx):
            return of.enter_context(nc.sbuf_tensor(name, shape, dt))

        def sem(name):
            return ctx.enter_context(nc.semaphore(name))

        bank = [ctx.enter_context(nc.psum_tensor(f"bank{i}", [P, 512], F32)) for i in range(8)]

        area_w = sb("area_w", [P, KT * D_IN])
        area_x = sb("area_x", [P, NT * D])
        cst = sb("cst", [P, K_ALL])
        cols = sb("cols", [P, 78])
        sink = sb("sink", [P, NQ])
        stat = sb("stat", [P, 64])
        rbias = sb("rbias", [P, NG + NE])
        gain_out = sb("gain_out", [P, D])[:, :]
        w1, w2 = sb("w1", [P, NT])[:, :], sb("w2", [P, NT])[:, :]
        idx = sb("idx", [HALF, 4 * NBLK], I32)[:, :].rearrange("p (h b) -> p h b", h=2)
        tab = sb("tab", [1, T_SIZE + NE + XS], I32)
        col_g = [sb(f"col_g{i}", [HALF, 2], I32)[:, :] for i in range(XS)]
        col_s = [sb(f"col_s{i}", [HALF, 2], I32)[:, :] for i in range(2)]
        area_h = sb("area_h", [P, KT * (META + SEQ)], of=mixer_ctx)
        area_m = sb("area_m", [P, KT * SEQ], of=mixer_ctx)
        area_g = sb("area_g", [P, 18240], of=mixer_ctx)

        at = [0]

        def cut(area, n, shape=None):
            a = area[:, at[0]:at[0] + n]
            at[0] += n
            return a

        rows = area_m[0:78, 0:P]
        w_in_sb = area_w[:, :].rearrange("p (k n) -> p k n", k=KT)
        w_out_sb = area_w[:, 0:KT * D].rearrange("p (k n) -> p k n", k=KT)
        xs = area_x[:, :].rearrange("p (j d) -> p j d", j=NT)
        hT = area_h[:, :].rearrange("p (k t) -> p k t", k=KT)
        mixT = area_m[:, :].rearrange("p (k t) -> p k t", k=KT)
        TT = META + SEQ
        glu = cut(area_g, 2 * (TAPS - 1 + TT)).rearrange("p (c t) -> p c t", c=2)
        qf = cut(area_g, 2 * SEQ).rearrange("p (c t) -> p c t", c=2)
        kf = cut(area_g, 2 * TT).rearrange("p (c t) -> p c t", c=2)
        lf_flat = cut(area_g, 2 * TT)
        lf = lf_flat.rearrange("p (c t) -> p c t", c=2)
        squares = lf_flat[:, 0:D]
        b = cut(area_g, 2 * TT).rearrange("p (c t) -> p c t", c=2)
        eb = cut(area_g, 2 * SEQ).rearrange("p (c t) -> p c t", c=2)
        qb = cut(area_g, 2 * SEQ).rearrange("p (c t) -> p c t", c=2)
        kb = cut(area_g, 2 * TT).rearrange("p (c t) -> p c t", c=2)
        lev = [area_x[:, n * 1024:(n + 1) * 1024].rearrange("p (c t) -> p c t", c=2) for n in range(4)]
        lev += [cut(area_g, 2 * SEQ).rearrange("p (c t) -> p c t", c=2) for n in range(2)]
        v2 = cut(area_g, NC_ * 128).rearrange("p (c i e) -> p c i e", c=NC_, i=2)
        v2m = cut(area_g, 128).rearrange("p (i e) -> p i e", i=2)
        qT = cut(area_g, 4 * SEQ).rearrange("p (c t) -> p c t", c=4)
        kT = cut(area_g, 2 * TT).rearrange("p (c t) -> p c t", c=2)
        va = cut(area_g, NT * P).rearrange("p (j e) -> p j e", j=NT)
        vp = cut(area_g, NT * P).rearrange("p (j e) -> p j e", j=NT)
        vm = cut(area_g, P)
        zt_flat = cut(area_g, 2 * TT)
        zt = zt_flat.rearrange("p (c t) -> p c t", c=2)
        meta_x = zt_flat[0:META, 0:D]
        gain = cut(area_g, D)
        wr = cut(area_g, KT * (NG + NE)).rearrange("p (k n) -> p k n", k=KT)
        hgrn_cols = [w_in_sb[:, k, C_HQ:C_HQ + 1024] for k in range(3, 7)]
        k2 = hgrn_cols[0].rearrange("p (c i e) -> p c i e", c=NC_, i=2)
        k2m = w_in_sb[:, 7, D_IN - 128:].rearrange("p (i e) -> p i e", i=2)
        state = hgrn_cols[1].rearrange("p (c i e) -> p c i e", c=NC_, i=2)
        A = hgrn_cols[2].rearrange("p (c t) -> p c t", c=2)
        osq = hgrn_cols[3].rearrange("p (c t) -> p c t", c=2)
        at[0] = 6 * D_IN + C_HQ - 4 * DW
        sc = [cut(area_w, 4 * DW).rearrange("p (h k) -> p h k", h=4) for _ in range(3)]
        pa = cut(area_w, 512)
        pb = cut(area_w, 512)
        mx = [cut(area_w, 4) for _ in range(3)]
        rs = [cut(area_w, 4) for _ in range(3)]
        es = [cut(area_w, 4) for _ in range(3)]
        assert at[0] <= KT * D_IN
        sig = area_m[:, 2 * SEQ:2 * SEQ + 2 * TT].rearrange("p (c t) -> p c t", c=2)
        ed = [area_m[:, 2 * SEQ:4 * SEQ].rearrange("p (c t) -> p c t", c=2),
              area_m[:, 4 * SEQ:6 * SEQ].rearrange("p (c t) -> p c t", c=2)]
        dm = stat[:, 32:64].rearrange("p (c t) -> p c t", c=2)
        QUERY_BANK = (4, 5, 6, 5)
        o_sb, o_factor = kb[:, :, 0:SEQ], b[:, :, 0:SEQ]
        ident = cst[:, K_ID:K_ID + P]
        eps = cst[:, K_EPS:K_EPS + 1]
        one = cst[:, K_ONE:K_ONE + 1]
        ss, rstd = stat[:, 0:5], stat[:, 5:10]

        d_cst, d_rest, d_par, d_meta, d_sink = sem("d_cst"), sem("d_rest"), sem("d_par"), sem("d_meta"), sem("d_sink")
        d_x = [sem(f"d_x{j}") for j in range(NT)]
        d_win = [sem(f"d_win{i}") for i in range(8)]
        d_wout = [sem("d_wout0"), sem("d_wout1")]
        d_resid = sem("d_resid")
        sumsq = sem("sumsq"); rstd_ready = sem("rstd_ready"); xn_ready = sem("xn_ready")
        par_T = sem("par_T"); cols_ready = sem("cols_ready")
        xT_done = sem("xT_done"); metaT = sem("metaT"); hT_v = sem("hT_v"); hT_a = sem("hT_a")
        product = sem("product"); evac = sem("evac"); glu_done = sem("glu_done")
        a_step = sem("a_step"); v_step = sem("v_step")
        softplus = sem("softplus"); gates = sem("gates"); kf_ready = sem("kf_ready")
        b_ready = sem("b_ready"); eb_ready = sem("eb_ready"); lev_d = sem("lev_d"); lev_e = sem("lev_e"); lev_w = sem("lev_w")
        kb_ready = sem("kb_ready"); kbT = sem("kbT"); k2_a = sem("k2_a"); k2_v = sem("k2_v")
        u_done = sem("u_done"); state_done = sem("state_done"); g_done = sem("g_done"); g_used = sem("g_used")
        o_done = sem("o_done"); o_taken = sem("o_taken"); osq_done = sem("osq_done"); ms_done = sem("ms_done"); orstd = sem("orstd"); y_h = sem("y_h")
        conv_done = sem("conv_done"); mean_done = sem("mean_done"); cen_done = sem("cen_done")
        csq = sem("csq"); var_done = sem("var_done"); crstd = sem("crstd"); cnorm = sem("cnorm"); y_c = sem("y_c")
        s_done = sem("s_done"); s_ready = sem("s_ready"); p_exp = sem("p_exp"); p_ready = sem("p_ready")
        pT = sem("pT"); pa_ready = sem("pa_ready"); pb_ready = sem("pb_ready"); pv = sem("pv"); y_a = sem("y_a")
        q_made = sem("q_made"); q_out = sem("q_out"); pads = sem("pads")

        PIECE = 2 * KT // 2 * DE
        RAW = 6
        piece_at = [KT * D + i * PIECE for i in range(RAW - 1)] + [0]
        piece_at = [piece_at[i] for i in (0, 1, 2, 4, 3, 5)]
        raw = [area_w[:, a:a + PIECE] for a in piece_at]
        JUNK = NT * 2 * D
        xf = area_h[:, 0:NT * D].rearrange("p (j d) -> p j d", j=NT)
        ye = [area_w[:, i * NT * D:(i + 1) * NT * D].rearrange("p (j d) -> p j d", j=NT) for i in range(2)]
        at[0] = 0
        NR = NG + NE
        logit = cut(area_g, NT * NR).rearrange("p (j n) -> p j n", j=NT)
        glog, gexp = (cut(area_g, NT * NG).rearrange("p (j n) -> p j n", j=NT) for _ in range(2))
        t4, oh4 = (cut(area_g, NT * NG).rearrange("p (j n) -> p j n", j=NT) for _ in range(2))
        ev, t32, both, rank = (cut(area_g, NT * NE).rearrange("p (j n) -> p j n", j=NT) for _ in range(4))
        picked, of_pick = (cut(area_g, 2 * NT * NE).rearrange("p (k j n) -> p k j n", k=2, j=NT) for _ in range(2))
        oh1, oh2 = picked[:, 0], picked[:, 1]
        count, extra, incl, first = (cut(area_g, NE) for _ in range(4))
        over = cut(area_g, NE * NTHR).rearrange("p (e m) -> p e m", e=NE)
        over4 = cut(area_g, 2 * NT * NTHR).rearrange("p (k j m) -> p k j m", k=2, j=NT)
        gm, gi, m1, m2, gsum, wd, tokf = (cut(area_g, NT) for _ in range(7))
        i12, qk, q1, rk, bk, ck = (cut(area_g, 2 * NT).rearrange("p (k j) -> p k j", k=2) for _ in range(6))
        i1, i2 = i12[:, 0], i12[:, 1]
        below = cut(area_g, MORE * NE).rearrange("p (m e) -> p m e", m=MORE)
        slot_is = cut(area_g, 2 * NT * BC).rearrange("p (k j c) -> p k j c", k=2, j=NT)
        block_is = cut(area_g, 2 * NT * 2 * NBLK).rearrange("p (k j w b) -> p k j w b", k=2, j=NT, w=2)
        size = cut(area_g, NE)[0:1]
        slot_to = cut(area_g, 2 * NBLK)[0:HALF].rearrange("p (h b) -> p h b", h=2)
        assert at[0] <= 16924

        oproj = sem("oproj"); h2_done = sem("h2_done"); fstat = sem("fstat"); xf_ready = sem("xf_ready")
        d_norm = sem("d_norm"); xfT = sem("xfT"); hfT_a = sem("hfT_a"); hfT_v = sem("hfT_v"); d_rt = sem("d_rt"); d_gain = sem("d_gain")
        logits = sem("logits"); gdiff = sem("gdiff"); gprob = sem("gprob"); ediff = sem("ediff"); eprob = sem("eprob")
        picks = sem("picks"); ranks = sem("ranks"); match = sem("match"); slots = sem("slots"); routed = sem("routed")
        d_raw = [sem(f"d_raw{i}") for i in range(RAW)]
        hi_done = sem("hi_done"); lo_done = sem("lo_done"); piece_used = sem("piece_used")
        d_xg = [sem(f"d_xg{i}") for i in range(XS)]; d_sc = [sem(f"d_sc{i}") for i in range(2)]
        xg_clear = sem("xg_clear"); xT_made = sem("xT_made"); xT_hi = sem("xT_hi"); xT_lo = sem("xT_lo")
        nstep = sem("nstep"); first_sum = sem("first_sum")
        sg_ready = sem("sg_ready"); act_ready = sem("act_ready")
        aT_made = sem("aT_made"); aT_hi = sem("aT_hi"); aT_lo = sem("aT_lo"); y_ready = sem("y_ready")
        col_ready = sem("col_ready")
        m_free = sem("m_free"); m_w = sem("m_w"); m_xg = sem("m_xg"); m_hi = sem("m_hi"); m_lo = sem("m_lo")
        m_xT = sem("m_xT"); m_xhi = sem("m_xhi"); m_xlo = sem("m_xlo"); m_gu = sem("m_gu"); m_sg = sem("m_sg"); m_act = sem("m_act")
        m_aT = sem("m_aT"); m_ahi = sem("m_ahi"); m_alo = sem("m_alo"); m_down = sem("m_down"); m_y = sem("m_y"); m_sc = sem("m_sc")
        d_ye = [sem(f"d_ye{j}") for j in range(NT)]; summed = sem("summed"); ostat = sem("ostat"); o_ready = sem("o_ready"); d_out = sem("d_out")

        passed = sem("passed")

        PROD = (["gate0", "gate1", "a0", "a1", "hq0", "hq1", "hg0", "hg1", "hf0", "hf1", "k",
                 "v0", "v1", "v2", "v3", "vm"])
        WITH_META = ["gate0", "gate1", "a0", "a1", "hf0", "hf1", "k"]
        COL = {"gate0": C_GATE, "gate1": C_GATE + P, "a0": C_A, "a1": C_A + P, "hq0": C_HQ, "hq1": C_HQ + P,
               "hg0": C_HG, "hg1": C_HG + P, "hf0": C_HF, "hf1": C_HF + P, "k": C_K}
        LOADS = [(C_GATE, 256), (C_A, 256), (C_HQ, 256), (C_HG, 256), (C_HF, 256), (C_K, 256), (C_HI, 256), (C_Q, 512)]
        LOAD_OF = {"gate": 0, "a": 1, "hq": 2, "hg": 3, "hf": 4, "k": 5, "v": 6}
        EVAC = [n for n in PROD if n not in ("a0", "a1")]

        def made(n):
            return PROD.index(n) + 1

        def taken(n):
            return EVAC.index(n) + 1

        def pbank(n):
            return bank[PROD.index(n) % 4]

        def mcols(n):
            return bank[4 + WITH_META.index(n) % 2][:, 0:META]

        def first_rows(w, e, half):
            return e(w).rearrange("(p k) n -> p k n", k=KT)[:, half * (KT // 2):(half + 1) * (KT // 2), :]

        def load_gate_up(sp, e, half, slot, d):
            v = raw[slot].rearrange("p (w k n) -> p w k n", w=2, n=DE)
            sp.dma_start(v[:, 0], first_rows(w_exp_gate, e, half)).then_inc(d, 16)
            sp.dma_start(v[:, 1], first_rows(w_exp_up, e, half)).then_inc(d, 16)

        def load_down(sp, e, slot, d):
            v = raw[slot].rearrange("p (f n) -> p f n", f=2)
            s_ = e(w_exp_down).rearrange("(p f) n -> p f n", f=2)
            for f in range(2):
                sp.dma_start(v[:, f], s_[:, f]).then_inc(d, 16)

        def through(v):
            if isinstance(v, int) and v < 2:
                return v + 1
            return v - 2 if isinstance(v, int) and v == 3 * NE + 2 else v

        block = mixer_ctx.enter_context(nc.Block())

        @block.sync
        def _(sp):
            sp.dma_start(meta_x[:, :], meta_tokens).then_inc(d_meta, 16)
            for j in range(NT):
                sp.dma_start(xs[:, j, :], x[0, j * P:(j + 1) * P, :]).then_inc(d_x[j], 16)
            sp.dma_start(cst[:, K_FIRST:], table[:, K_FIRST:]).then_inc(d_rest, 16)
            w_v = w_in[0].rearrange("(k p) n -> p k n", p=P)
            for i, (c0, n) in enumerate(LOADS):
                sp.dma_start(w_in_sb[:, :, c0:c0 + n], w_v[:, :, c0:c0 + n]).then_inc(d_win[i], 16)
            sp.wait_ge(q_made, 4)
            wo_v = w_out[0].rearrange("(k p) n -> p k n", p=P)
            for i in range(2):
                sp.dma_start(w_out_sb[:, :, i * 512:(i + 1) * 512], wo_v[:, :, i * 512:(i + 1) * 512]).then_inc(d_wout[i], 16)
            sp.wait_ge(g_done, 14)
            sp.dma_start(xs, x[0].rearrange("(j p) d -> p j d", p=P)).then_inc(d_resid, 16)

            sp.wait_ge(y_h, 2)
            load_gate_up(sp, lambda w: w[0, 0], 0, 0, d_raw[0])
            load_gate_up(sp, lambda w: w[0, 0], 1, 1, d_raw[1])
            sp.wait_ge(y_a, 2 * NT)
            load_gate_up(sp, lambda w: w[0, 1], 0, 3, d_raw[3])
            sp.wait_ge(oproj, 2 * NT)
            load_gate_up(sp, lambda w: w[0, 1], 1, 4, d_raw[4])
            load_down(sp, lambda w: w[0, 0], 5, d_raw[5])
            for j in range(NT):
                sp.wait_ge(xf_ready, j + 1)
                sp.dma_start(normed[j * P:(j + 1) * P, :], xf[:, j, :]).then_inc(d_norm, 16)
            sp.wait_ge(d_norm, 16 * NT)
            sp.wait_ge(routed, 2)

        @block.scalar
        def _(act):
            an = [0]

            def step(ins):
                an[0] += 1
                ins.then_inc(a_step, 1)
                act.wait_ge(a_step, an[0])

            act.dma_start(cst[:, 0:K_FIRST], table[:, 0:K_FIRST]).then_inc(d_cst, 16)
            act.dma_start(rows[0:62, :], conv_dw_w[0].rearrange("t (c p) -> (t c) p", p=P)).then_inc(d_par, 16)
            act.dma_start(rows[62:70, :], mix_norm[0].rearrange("(c p) -> c p", p=P)).then_inc(d_par, 16)
            for i, a in enumerate((conv_dw_b, conv_ln_g, conv_ln_b, hgrn_norm_g)):
                act.dma_start(rows[70 + 2 * i:72 + 2 * i, :], a[0].rearrange("(c p) -> c p", p=P)).then_inc(d_par, 16)
            act.dma_start(sink[:, :], attn_sinks.to_broadcast([P, NQ])).then_inc(d_sink, 16)
            act.wait_ge(d_cst, 16)
            act.preload_act_table_set("natural_log_exp_and_others")
            for j in [4, 0, 1, 2, 3]:
                rws = META if j == 4 else P
                src = meta_x[:, :] if j == 4 else xs[:, j, :]
                act.wait_ge(d_meta if j == 4 else d_x[j], 16)
                junk = area_g[0:rws, 2 * (TAPS - 1 + TT):2 * (TAPS - 1 + TT) + D]
                step(nc.scalar.activation(junk, src, ACT.Square, accum_out=ss[0:rws, j:j + 1]))
                step(nc.scalar.activation(rstd[0:rws, j:j + 1], ss[0:rws, j:j + 1], ACT.Ln, bias=eps[0:rws], scale=1.0 / D))
                nc.scalar.activation(rstd[0:rws, j:j + 1], rstd[0:rws, j:j + 1], ACT.Exp, scale=-0.5).then_inc(rstd_ready, 1)
            act.wait_ge(rstd_ready, 5)
            act.wait_ge(xT_done, NT)
            act.wait_ge(cols_ready, 1)
            for k in range(1, KT, 2):
                nc.scalar.activation(hT[:, k, META:], bank[k][:, :], ACT.Copy, scale=cols[:, 62 + k:63 + k]).then_inc(hT_a, 1)
            for n in EVAC:
                act.wait_ge(product, made(n))
                src = pbank(n)
                i = int(n[1:]) if n[1:].isdigit() else int(n[-1]) if n[-1].isdigit() else 0
                if n.startswith("gate"):
                    nc.scalar.activation(sig[:, i, 0:META], mcols(n), ACT.Sigmoid).then_inc(a_step, 1); an[0] += 1
                    nc.scalar.activation(sig[:, i, META:], src[:, :], ACT.Sigmoid).then_inc(evac, 1)
                elif n.startswith("hq"):
                    nc.scalar.activation(qf[:, i, :], src[:, :], ACT.Silu).then_inc(evac, 1)
                elif n.startswith("hg"):
                    nc.scalar.activation(mixT[:, 6 + i, :], src[:, :], ACT.Silu).then_inc(evac, 1)
                elif n.startswith("hf"):
                    nc.scalar.activation(zt[:, i, 0:META], mcols(n), ACT.Identity).then_inc(a_step, 1); an[0] += 1
                    nc.scalar.activation(zt[:, i, META:], src[:, :], ACT.Identity).then_inc(evac, 1)
                    if i == 1:
                        act.wait_ge(evac, taken(n))
                        act.wait_ge(a_step, an[0])
                        act.preload_act_table_set("natural_log_exp_and_others")
                        step(nc.scalar.activation(lf, zt, ACT.Abs))
                        step(nc.scalar.activation(lf, lf, ACT.Exp, scale=-1.0))
                        nc.scalar.activation(b, lf, ACT.Ln, bias=one).then_inc(softplus, 1)
                        act.wait_ge(gates, 2)
                        nc.scalar.activation(kf, kf, ACT.Exp, scale=-1.0).then_inc(kf_ready, 1)
                elif n == "k":
                    for g in range(2):
                        for half in range(2):
                            dst, s = slice(half * HD, half * HD + HD), slice(g * HD, g * HD + HD)
                            nc.scalar.activation(kT[dst, g, 0:META], mcols(n)[s, :], ACT.Copy).then_inc(a_step, 1); an[0] += 1
                            last = nc.scalar.activation(kT[dst, g, META:], src[s, :], ACT.Copy)
                            if g == half == 1:
                                last.then_inc(evac, 1)
                            else:
                                last.then_inc(a_step, 1); an[0] += 1
                elif n == "vm":
                    act.wait_ge(pads, 1)
                    for j in range(1, NT):
                        nc.scalar.activation(vp[HD:HD + META, j, :], src[0:META, 0:P], ACT.Copy).then_inc(a_step, 1); an[0] += 1
                    nc.scalar.activation(vm[0:META, :], src[0:META, 0:P], ACT.Copy).then_inc(a_step, 1); an[0] += 1
                    s = src[0:META, P:P + 256].rearrange("p (i h e) -> p i h e", i=2, h=2)
                    nc.scalar.activation(v2m[0:META], s[:, :, 0, :], ACT.Copy).then_inc(a_step, 1); an[0] += 1
                    nc.scalar.activation(v2m[HD:HD + META], s[:, :, 1, :], ACT.Copy).then_inc(evac, 1)
                elif n.startswith("v"):
                    nc.scalar.activation(va[:, i, :], src[:, 0:P], ACT.Copy).then_inc(a_step, 1); an[0] += 1
                    if i + 1 < NT:
                        nc.scalar.activation(vp[0:HD, i + 1, :], src[HD:P, 0:P], ACT.Copy).then_inc(a_step, 1); an[0] += 1
                    s = src[:, P:P + 256].rearrange("p (i h e) -> p i h e", i=2, h=2)
                    for cp in range(2):
                        for hp in range(2):
                            last = nc.scalar.activation(v2[hp * HD:hp * HD + HD, 2 * i + cp, :, :],
                                                        s[cp * HD:cp * HD + HD, :, hp, :], ACT.Copy)
                            if cp == hp == 1:
                                last.then_inc(evac, 1)
                            else:
                                last.then_inc(a_step, 1); an[0] += 1
                if n == "k":
                    act.wait_ge(b_ready, 1)
                    nc.scalar.activation(eb, b[:, :, META:], ACT.Exp).then_inc(eb_ready, 1)
                    act.wait_ge(lev_d, 1)
                    nc.scalar.activation(dm, dm, ACT.Exp).then_inc(a_step, 1); an[0] += 1
                    nc.scalar.activation(ed[0], ed[0], ACT.Exp).then_inc(lev_e, 1)
                for l in {"v0": [0], "v1": [1], "v2": [2], "v3": [3], "vm": [4, 5]}.get(n, []):
                    act.wait_ge(lev_d, l + 2)
                    e = ed[(l + 1) % 2]
                    nc.scalar.activation(e, e, ACT.Exp).then_inc(lev_e, 1)
            act.wait_ge(kbT, 2)
            for ti in range(2):
                src = bank[5 + ti][:, :].rearrange("p (r h e) -> p r h e", r=4, h=2)
                for hp in range(2):
                    nc.scalar.activation(k2[hp * HD:hp * HD + HD, 0::2, ti, :], src[0:HD, :, hp, :], ACT.Copy).then_inc(k2_a, 1)
            def queries_out(i):
                act.wait_ge(q_made, i + 1)
                nc.scalar.activation(qT[:, i, :], bank[QUERY_BANK[i]][:, :], ACT.Copy, scale=HD ** -0.5).then_inc(q_out, 1)

            queries_out(0)
            act.wait_ge(cen_done, 2)
            nc.scalar.activation(osq, mixT[:, 0:2, :], ACT.Square).then_inc(csq, 1)
            act.wait_ge(var_done, 1)
            step(nc.scalar.activation(ed[0][:, 0, :], bank[4][:, :], ACT.Ln, bias=eps))
            nc.scalar.activation(ed[0][:, 0, :], ed[0][:, 0, :], ACT.Exp, scale=-0.5).then_inc(crstd, 1)
            for i in range(1, 4):
                queries_out(i)
            act.wait_ge(cnorm, 2)
            for i in range(2):
                nc.scalar.activation(mixT[:, i, :], mixT[:, i, :], ACT.Silu, scale=cols[:, 72 + i:73 + i],
                                     bias=cols[:, 74 + i:75 + i]).then_inc(y_c, 1)
            act.preload_act_table_set("natural_log_exp_and_others")

            def head_squares(ti):
                act.wait_ge(o_taken, ti + 1)
                nc.scalar.activation(qf[:, ti, :], o_sb[:, ti, :], ACT.Square).then_inc(osq_done, 1)

            def head_factor(ti):
                act.wait_ge(ms_done, ti + 1)
                step(nc.scalar.activation(o_factor[:, ti, :], bank[7][:, :], ACT.Ln, bias=eps))
                nc.scalar.activation(o_factor[:, ti, :], o_factor[:, ti, :], ACT.Exp, scale=-0.5).then_inc(orstd, 1)

            def probs(u):
                act.wait_ge(s_ready, u + 1)
                i = u % 3
                for h in range(4):
                    lo = HD if u < 2 else 0
                    nc.scalar.activation(sc[i][:, h, lo:], sc[i][:, h, lo:], ACT.Exp, bias=mx[i][:, h:h + 1],
                                         accum_out=rs[i][:, h:h + 1]).then_inc(a_step, 1); an[0] += 1
                nc.scalar.activation(es[i], es[i], ACT.Exp).then_inc(p_exp, 1)

            def tile_a(u):
                act.wait_ge(pT, u + 1)
                if u >= 1:
                    act.wait_ge(pv, u)
                lo = META if u < 2 else HD + META
                nc.scalar.activation(pa[0:lo, :], bank[5][0:lo, :], ACT.Copy).then_inc(pa_ready, 1)

            def heads_out(u):
                act.wait_ge(pv, u + 1)
                p, g = u // 2, u % 2
                if u == 0:
                    act.wait_ge(cnorm, 2)
                src = bank[4][:, 0:256].rearrange("p (i t) -> p i t", i=2)
                nc.scalar.activation(mixT[:, 2 + 2 * g:4 + 2 * g, p * P:(p + 1) * P], src, ACT.Copy).then_inc(y_a, 1)

            def second_norm(j):
                act.wait_ge(h2_done, 2 * j + 2)
                step(nc.scalar.activation(squares, xs[:, j, :], ACT.Square, accum_out=ss[:, j:j + 1]))
                step(nc.scalar.activation(rstd[:, j:j + 1], ss[:, j:j + 1], ACT.Ln, bias=eps, scale=1.0 / D))
                nc.scalar.activation(rstd[:, j:j + 1], rstd[:, j:j + 1], ACT.Exp, scale=-0.5).then_inc(fstat, 1)

            def router_half(j):
                act.wait_ge(xfT, j + 1)
                src = bank[2 * j + 1][:, :].rearrange("p (k t) -> p k t", k=4)
                nc.scalar.activation(mixT[:, 4:8, j * P:(j + 1) * P], src, ACT.Copy).then_inc(hfT_a, 1)

            U = 2 * NT
            probs(0)
            for u in range(U):
                if u + 1 < U:
                    probs(u + 1)
                tile_a(u)
                if u < 2:
                    head_squares(u)
                heads_out(u)
                if u < 2:
                    head_factor(u)
                if u >= 4 and u % 2 == 0:
                    second_norm(u // 2 - 2)
            second_norm(2)
            router_half(0)
            router_half(1)
            second_norm(3)
            router_half(2)
            router_half(3)
            act.wait_ge(gdiff, 1)
            nc.scalar.activation(gexp, gexp, ACT.Exp).then_inc(gprob, 1)
            act.wait_ge(ediff, 1)
            nc.scalar.activation(wd, wd, ACT.Exp).then_inc(eprob, 1)

        @block.vector
        def _(dve):
            vn = [0]

            def step(ins):
                vn[0] += 1
                ins.then_inc(v_step, 1)
                dve.wait_ge(v_step, vn[0])

            def mark(ins):
                vn[0] += 1
                ins.then_inc(v_step, 1)
                return vn[0]

            V = nc.vector
            mark(V.memset(glu[:, :, 0:TAPS - 1], 0.0))
            V.memset(vp[:, :, :], 0.0).then_inc(pads, 1)
            dve.wait_ge(par_T, 1)
            V.tensor_copy(cols[:, :], bank[6][:, 0:78]).then_inc(cols_ready, 1)
            dve.wait_ge(cols_ready, 1)
            for n, j in enumerate([4, 0, 1, 2, 3]):
                dve.wait_ge(rstd_ready, n + 1)
                if j == 4:
                    V.tensor_scalar(meta_x[:, :], meta_x[:, :], rstd[0:META, 4:5], None, ALU.mult).then_inc(xn_ready, 1)
                else:
                    V.tensor_scalar(xs[:, j, :], xs[:, j, :], rstd[:, j:j + 1], None, ALU.mult).then_inc(xn_ready, 1)
                if j == 0:
                    dve.wait_ge(metaT, 1)
                    V.tensor_tensor(hT[:, :, 0:META], bank[7][:, 0:P].rearrange("p (k t) -> p k t", k=KT),
                                    cols[:, 62:70].unsqueeze(2).to_broadcast([P, KT, META]), ALU.mult).then_inc(hT_v, 1)
            dve.wait_ge(xT_done, NT)
            for k in range(0, KT, 2):
                V.tensor_scalar(hT[:, k, META:], bank[k][:, :], cols[:, 62 + k:63 + k], None, ALU.mult).then_inc(hT_v, 1)
            dve.wait_ge(evac, taken("gate1"))
            for i in range(2):
                n = f"a{i}"
                dve.wait_ge(product, made(n))
                mark(V.tensor_tensor(glu[:, i, TAPS - 1:TAPS - 1 + META], mcols(n), sig[:, i, 0:META], ALU.mult))
                V.tensor_tensor(glu[:, i, TAPS - 1 + META:], pbank(n)[:, :], sig[:, i, META:], ALU.mult).then_inc(glu_done, 1)
            dve.wait_ge(glu_done, 2)
            dve.wait_ge(v_step, vn[0])
            last = [0, 0]
            for t in range(TAPS):
                for i in range(2):
                    src = glu[:, i, META + t:META + t + SEQ]
                    w = cols[:, 2 * t + i:2 * t + i + 1]
                    if t == 0:
                        last[i] = mark(V.tensor_scalar(mixT[:, i, :], src, w, cols[:, 70 + i:71 + i], ALU.mult, ALU.add))
                    else:
                        dve.wait_ge(v_step, last[i])
                        ins = V.scalar_tensor_tensor(out=mixT[:, i, :], in0=src, scalar=w, in1=mixT[:, i, :],
                                                     op0=ALU.mult, op1=ALU.add)
                        if t == TAPS - 1:
                            ins.then_inc(conv_done, 1)
                        else:
                            last[i] = mark(ins)
            dve.wait_ge(d_rest, 16)
            dve.wait_ge(softplus, 1)
            V.scalar_tensor_tensor(out=lf, in0=zt, scalar=0.0, in1=b, op0=ALU.min, op1=ALU.subtract).then_inc(gates, 1)
            V.scalar_tensor_tensor(out=kf, in0=zt, scalar=0.0, in1=b, op0=ALU.max, op1=ALU.add).then_inc(gates, 1)
            dve.wait_ge(gates, 2)
            for i in range(2):
                mark(V.tensor_tensor_scan(b[:, i, 0:META], cst[:, K_ONE:K_ONE + META], lf[:, i, 0:META], 0.0, ALU.mult, ALU.add))
                ins = V.tensor_tensor_scan(b[:, i, META:], cst[:, K_RESET:K_RESET + SEQ], lf[:, i, META:], 0.0, ALU.mult, ALU.add)
                if i == 0:
                    mark(ins)
                else:
                    ins.then_inc(b_ready, 1)
            dve.wait_ge(b_ready, 1)
            dve.wait_ge(v_step, vn[0])
            bc = b[:, :, META:].rearrange("p i (c t) -> p i c t", t=CHUNK)
            mark(V.tensor_tensor(dm, b[:, :, META - 1:META].to_broadcast([P, 2, META]), b[:, :, 0:META], ALU.subtract))
            V.tensor_tensor(ed[0].rearrange("p i (c t) -> p i c t", t=CHUNK),
                            bc[:, :, :, CHUNK - 1:CHUNK].to_broadcast([P, 2, NC_, CHUNK]), bc, ALU.subtract).then_inc(lev_d, 1)

            def level_decay(l):
                h = LEVELS[l]
                e = ed[(l + 1) % 2].rearrange("p i (c t) -> p i c t", t=2 * h)
                bl = b[:, :, META:].rearrange("p i (c t) -> p i c t", t=2 * h)
                mid = bl[:, :, :, h - 1:h].to_broadcast([P, 2, SEQ // (2 * h), h])
                mark(V.tensor_tensor(e[:, :, :, 0:h], mid, bl[:, :, :, 0:h], ALU.subtract))
                V.tensor_tensor(e[:, :, :, h:], bl[:, :, :, h:], mid, ALU.subtract).then_inc(lev_d, 1)

            def level_pair(l):
                h = LEVELS[l]
                dve.wait_ge(lev_e, l + 2)
                e = ed[(l + 1) % 2].rearrange("p i (c t) -> p i c t", t=2 * h)
                w = lev[l].rearrange("p i (c t) -> p i c t", t=2 * h)
                kk = kf[:, :, META:].rearrange("p i (c t) -> p i c t", t=2 * h)
                qq = qf.rearrange("p i (c t) -> p i c t", t=2 * h)
                mark(V.tensor_tensor(w[:, :, :, 0:h], kk[:, :, :, 0:h], e[:, :, :, 0:h], ALU.mult))
                V.tensor_tensor(w[:, :, :, h:], qq[:, :, :, h:], e[:, :, :, h:], ALU.mult).then_inc(lev_w, 1)
                dve.wait_ge(lev_w, l + 1)
                dve.wait_ge(v_step, vn[0])

            level_decay(0)
            dve.wait_ge(lev_e, 1)
            dve.wait_ge(kf_ready, 1)
            mark(V.tensor_tensor(kb[:, :, 0:META], kf[:, :, 0:META], dm, ALU.mult))
            V.tensor_tensor(kb[:, :, META:], kf[:, :, META:], ed[0], ALU.mult).then_inc(kb_ready, 1)
            dve.wait_ge(kb_ready, 1)
            for l in range(len(LEVELS)):
                if l + 1 < len(LEVELS):
                    level_decay(l + 1)
                level_pair(l)
            dve.wait_ge(eb_ready, 1)
            mark(V.tensor_tensor(qb, qf, eb, ALU.mult))
            dve.wait_ge(kbT, 2)
            for ti in range(2):
                src = bank[5 + ti][:, :].rearrange("p (r h e) -> p r h e", r=4, h=2)
                for hp in range(2):
                    V.tensor_copy(k2[hp * HD:hp * HD + HD, 1::2, ti, :], src[HD:P, :, hp, :]).then_inc(k2_v, 1)
            src = bank[7][0:META, 0:256].rearrange("p (i h e) -> p i h e", i=2, h=2)
            for hp in range(2):
                V.tensor_copy(k2m[hp * HD:hp * HD + META, :, :], src[:, :, hp, :]).then_inc(k2_v, 1)
            dve.wait_ge(u_done, 1)
            step(V.tensor_copy(state[:, 0, :, :], bank[0][:, 0:P].rearrange("p (i e) -> p i e", i=2)))
            for c in range(1, NC_):
                u = bank[c // 4][:, (c % 4) * P:(c % 4) * P + P].rearrange("p (i e) -> p i e", i=2)
                for i in range(2):
                    ins = V.scalar_tensor_tensor(out=state[:, c, i, :], in0=state[:, c - 1, i, :],
                                                 scalar=eb[:, i, c * CHUNK - 1:c * CHUNK], in1=u[:, i, :],
                                                 op0=ALU.mult, op1=ALU.add)
                    if i == 0:
                        mark(ins)
                    elif c < NC_ - 1:
                        step(ins)
                    else:
                        ins.then_inc(state_done, 1)
            dve.wait_ge(mean_done, 1)
            for i in range(2):
                V.tensor_tensor(mixT[:, i, :], mixT[:, i, :], bank[7][:, :], ALU.subtract).then_inc(cen_done, 1)
            nl = len(LEVELS)
            for n in range(2 * (nl + 1)):
                ti, l = n % 2, (nl - n // 2)
                dve.wait_ge(g_done, n + 1)
                m = cst[:, K_MASK + l * CHUNK:K_MASK + (l + 1) * CHUNK].unsqueeze(1).to_broadcast([P, NC_, CHUNK])
                g = bank[2 + n % 2][:, :].rearrange("p (c t) -> p c t", t=CHUNK)
                a = A[:, ti, :].rearrange("p (c t) -> p c t", t=CHUNK)
                if n >= 2:
                    dve.wait_ge(g_used, n - 1)
                if l == nl:
                    V.tensor_tensor(a, g, m, ALU.mult).then_inc(g_used, 1)
                else:
                    V.copy_predicated(a, m.bitcast(I32), g).then_inc(g_used, 1)
            dve.wait_ge(crstd, 1)
            for i in range(2):
                V.tensor_tensor(mixT[:, i, :], mixT[:, i, :], ed[0][:, 0, :], ALU.mult).then_inc(cnorm, 1)
            def biased(u):
                dve.wait_ge(s_done, u + 1)
                p, g, i = u // 2, u % 2, u % 3
                if u >= 3:
                    dve.wait_ge(pT, u - 2)
                lo = HD if p == 0 else 0
                dist = cst[:, K_DIST + p * DW + lo:K_DIST + (p + 1) * DW]
                for h in range(4):
                    s = bank[2 * (u % 2) + h % 2][:, (h // 2) * DW + lo:(h // 2 + 1) * DW]
                    mark(V.scalar_tensor_tensor(out=sc[i][:, h, lo:], in0=dist, scalar=2.0 ** -(4 * g + h + 1), in1=s,
                                                op0=ALU.mult, op1=ALU.add))
                dve.wait_ge(v_step, vn[0])
                if u < 2:
                    dve.wait_ge(d_sink, 16)
                step(V.tensor_reduce(mx[i], sc[i][:, :, lo:], AX, ALU.max))
                step(V.tensor_tensor(mx[i], mx[i], sink[:, 4 * g:4 * g + 4], ALU.max))
                step(V.tensor_scalar(mx[i], mx[i], -1.0, None, ALU.mult))
                V.tensor_tensor(es[i], mx[i], sink[:, 4 * g:4 * g + 4], ALU.add).then_inc(s_ready, 1)

            def normal(u):
                i = u % 3
                lo = HD if u < 2 else 0
                dve.wait_ge(p_exp, u + 1)
                step(V.tensor_tensor(rs[i], rs[i], es[i], ALU.add))
                step(V.reciprocal(rs[i], rs[i]))
                V.tensor_tensor(sc[i][:, :, lo:], sc[i][:, :, lo:], rs[i].unsqueeze(2).to_broadcast([P, 4, DW - lo]), ALU.mult)\
                    .then_inc(p_ready, 1)

            def tile_b(u):
                dve.wait_ge(pT, u + 1)
                if u >= 1:
                    dve.wait_ge(pv, u)
                V.tensor_copy(pb, bank[6][:, :]).then_inc(pb_ready, 1)

            def hgrn_take(ti):
                dve.wait_ge(o_done, ti + 1)
                V.tensor_copy(o_sb[:, ti, :], bank[7][:, :]).then_inc(o_taken, 1)

            def hgrn_out(ti):
                dve.wait_ge(orstd, ti + 1)
                step(V.tensor_tensor(o_sb[:, ti, :], o_sb[:, ti, :], o_factor[:, ti, :], ALU.mult))
                V.scalar_tensor_tensor(out=mixT[:, 6 + ti, :], in0=o_sb[:, ti, :], scalar=cols[:, 76 + ti:77 + ti],
                                       in1=mixT[:, 6 + ti, :], op0=ALU.mult, op1=ALU.mult).then_inc(y_h, 1)

            def residual(i):
                j, n = i // 2, i % 2
                dve.wait_ge(oproj, i + 1)
                if i == 0:
                    dve.wait_ge(d_resid, 16)
                h = xs[:, j, n * 512:(n + 1) * 512]
                V.tensor_tensor(h, h, bank[7][:, :], ALU.add).then_inc(h2_done, 1)

            def normed_rows(j):
                if j == 0:
                    dve.wait_ge(d_gain, 48)
                dve.wait_ge(h2_done, 2 * j + 2)
                dve.wait_ge(fstat, j + 1)
                V.scalar_tensor_tensor(out=xf[:, j, :], in0=xs[:, j, :], scalar=rstd[:, j:j + 1], in1=gain,
                                       op0=ALU.mult, op1=ALU.mult).then_inc(xf_ready, 1)

            def router_half(j):
                dve.wait_ge(xfT, j + 1)
                src = bank[2 * j][:, :].rearrange("p (k t) -> p k t", k=4)
                V.tensor_copy(mixT[:, 0:4, j * P:(j + 1) * P], src).then_inc(hfT_v, 1)

            U = 2 * NT
            biased(0)
            biased(1)
            for u in range(U):
                normal(u)
                if 1 <= u <= 2:
                    hgrn_out(u - 1)
                if u >= 3:
                    residual(u - 3)
                if u + 2 < U:
                    biased(u + 2)
                tile_b(u)
                if u < 2:
                    hgrn_take(u)
                if u >= 5 and u % 2 == 1:
                    normed_rows((u - 5) // 2)
            residual(5)
            router_half(0)
            router_half(1)
            normed_rows(2)
            residual(6)
            residual(7)
            normed_rows(3)
            router_half(2)
            router_half(3)

            def first_max(v, n, m, i, t, oh):
                iota = cst[:, K_IOTA:K_IOTA + n].unsqueeze(1).to_broadcast([P, NT, n])
                step(V.tensor_reduce(m, v, AX, ALU.max))
                step(V.tensor_tensor(t, v, m.unsqueeze(2).to_broadcast([P, NT, n]), ALU.is_equal))
                step(V.scalar_tensor_tensor(out=t, in0=t, scalar=-float(FAR), in1=iota, op0=ALU.mult, op1=ALU.add))
                step(V.tensor_reduce(i, t, AX, ALU.min))
                step(V.tensor_tensor(oh, t, i.unsqueeze(2).to_broadcast([P, NT, n]), ALU.is_equal))

            dve.wait_ge(logits, NT)
            step(V.tensor_tensor(logit, bank[0][:, 0:NT * NR].rearrange("p (j n) -> p j n", j=NT),
                                 rbias[:, :].unsqueeze(1).to_broadcast([P, NT, NR]), ALU.add))
            step(V.tensor_copy(glog, logit[:, :, 0:NG]))
            first_max(glog, NG, gm, gi, t4, oh4)
            V.tensor_tensor(gexp, glog, gm.unsqueeze(2).to_broadcast([P, NT, NG]), ALU.subtract).then_inc(gdiff, 1)
            step(V.tensor_scalar(oh4, oh4, -NEG, NEG, ALU.mult, ALU.add))
            for j in range(NT):
                ins = V.tensor_tensor(ev[:, j, :].rearrange("p (g e) -> p g e", g=NG),
                                      logit[:, j, NG:].rearrange("p (g e) -> p g e", g=NG),
                                      oh4[:, j, :].unsqueeze(2).to_broadcast([P, NG, EPG]), ALU.add)
                mark(ins)
            dve.wait_ge(v_step, vn[0])
            first_max(ev, NE, m1, i1, t32, oh1)
            step(V.scalar_tensor_tensor(out=ev, in0=oh1, scalar=3 * NEG, in1=ev, op0=ALU.mult, op1=ALU.add))
            first_max(ev, NE, m2, i2, t32, oh2)
            V.tensor_tensor(wd, m2, m1, ALU.subtract).then_inc(ediff, 1)
            V.tensor_tensor(both, oh1, oh2, ALU.add).then_inc(picks, 1)
            dve.wait_ge(gprob, 1)
            step(V.tensor_reduce(gsum, gexp, AX, ALU.add))
            dve.wait_ge(eprob, 1)
            step(V.tensor_scalar(w1, wd, 1.0, None, ALU.add))
            step(V.tensor_tensor(w1, w1, gsum, ALU.mult))
            step(V.reciprocal(w1, w1))
            step(V.tensor_tensor(w2, w1, wd, ALU.mult))
            dve.wait_ge(ranks, 1)
            mark(V.tensor_copy(rank, bank[1][:, 0:NT * NE].rearrange("p (j e) -> p j e", j=NT)))
            step(V.tensor_copy(count, bank[1][:, NT * NE:NT * NE + NE]))
            thr = cst[:, K_THR:K_THR + NTHR]
            step(V.tensor_tensor(over, count.unsqueeze(2).to_broadcast([P, NE, NTHR]),
                                 thr.unsqueeze(1).to_broadcast([P, NE, NTHR]), ALU.is_gt))
            step(V.tensor_reduce(extra, over, AX, ALU.add))
            ones = cst[:, K_ONE:K_ONE + NE]
            step(V.tensor_tensor_scan(incl, ones, extra, 0.0, ALU.mult, ALU.add))
            mark(V.tensor_tensor(first, incl, extra, ALU.subtract))
            step(V.tensor_tensor(below, incl.unsqueeze(1).to_broadcast([P, MORE, NE]),
                                 cst[:, K_IOTA:K_IOTA + MORE].unsqueeze(2).to_broadcast([P, MORE, NE]), ALU.is_le))
            step(V.tensor_reduce(over[:, 0:MORE, 0], below, AX, ALU.add))
            mark(V.tensor_scalar(tab[0:1, 1:1 + MORE], over[0:1, 0:MORE, 0], float(NE - 1), None, ALU.min))
            step(V.tensor_scalar(size, count[0:1, :], float(HALF), None, ALU.is_gt))
            mark(V.scalar_tensor_tensor(out=tab[0:1, T_SIZE:T_SIZE + NE], in0=count[0:1, :], scalar=float(FEW), in1=size,
                                        op0=ALU.is_gt, op1=ALU.add))
            mark(V.memset(tab[0:1, T_SIZE + NE:], 0))
            mark(V.tensor_copy(tab[0:1, 0:1], incl[0:1, NE - 1:NE]))
            two = [P, 2, NT, NE]
            step(V.tensor_tensor(of_pick, picked, rank.unsqueeze(1).to_broadcast(two), ALU.mult))
            mark(V.tensor_reduce(rk, of_pick, AX, ALU.add))
            step(V.tensor_tensor(picked, picked, first.unsqueeze(1).unsqueeze(1).to_broadcast(two), ALU.mult))
            mark(V.tensor_reduce(bk, picked, AX, ALU.add))
            mark(V.tensor_scalar(i12, i12, float(FAR), None, ALU.add))
            step(V.tensor_tensor(over4, rk.unsqueeze(3).to_broadcast([P, 2, NT, NTHR]),
                                 thr.unsqueeze(1).unsqueeze(1).to_broadcast([P, 2, NT, NTHR]), ALU.is_ge))
            step(V.tensor_reduce(qk, over4, AX, ALU.add))
            mark(V.scalar_tensor_tensor(out=ck, in0=qk, scalar=-float(BC), in1=rk, op0=ALU.mult, op1=ALU.add))
            mark(V.tensor_scalar(q1, qk, 1.0, None, ALU.min))
            step(V.tensor_tensor(bk, bk, qk, ALU.add))
            step(V.scalar_tensor_tensor(out=bk, in0=bk, scalar=float(NE - 1), in1=i12, op0=ALU.add, op1=ALU.subtract))
            step(V.tensor_tensor(bk, bk, q1, ALU.mult))
            mark(V.tensor_tensor(bk, bk, i12, ALU.add))
            step(V.tensor_scalar(tokf, cst[:, K_TOK:K_TOK + NT], -float(FAR), None, ALU.add))
            for k in range(2):
                for j in range(NT):
                    mark(V.tensor_scalar(slot_is[:, k, j, :], cst[:, K_IOTA:K_IOTA + BC], ck[:, k, j:j + 1], None, ALU.is_equal))
                    mark(V.tensor_scalar(block_is[:, k, j, 0, :], cst[:, K_IOTA:K_IOTA + NBLK], bk[:, k, j:j + 1],
                                         tokf[:, j:j + 1], ALU.is_equal, ALU.mult))
                    if k:
                        mark(V.tensor_scalar(block_is[:, k, j, 1, :], cst[:, K_IOTA:K_IOTA + NBLK], bk[:, k, j:j + 1],
                                             float(SEQ), ALU.is_equal, ALU.mult))
            dve.wait_ge(v_step, vn[0])
            V.memset(count[0:1, 0:1], 0.0).then_inc(match, 1)
            dve.wait_ge(slots, 1)
            for h in range(2):
                part = bank[2][h * HALF:(h + 1) * HALF, :]
                mark(V.tensor_scalar(idx[:, h, 0:NBLK], part[:, 0:NBLK], float(FAR), None, ALU.add))
                mark(V.tensor_scalar(slot_to[:, h, :], part[:, 0:NBLK], float(FAR), None, ALU.add))
            dve.wait_ge(v_step, vn[0])
            for h in range(2):
                V.tensor_tensor(idx[:, h, NBLK:], slot_to[:, h, :], bank[2][h * HALF:(h + 1) * HALF, NBLK:2 * NBLK], ALU.add)\
                    .then_inc(routed, 1)

        @block.tensor
        def _(pe):
            T = nc.tensor
            pe.wait_ge(d_cst, 16)
            pe.wait_ge(d_par, 96)
            T.transpose(bank[6][:, 0:78], rows[:, :], ident[0:78, 0:78]).then_inc(par_T, 1)
            pe.wait_ge(xn_ready, 1)
            for k in range(KT):
                ins = T.transpose(bank[7][:, k * META:(k + 1) * META], meta_x[:, k * P:(k + 1) * P], ident[0:META, 0:META])
            ins.then_inc(metaT, 1)
            for j in range(NT):
                pe.wait_ge(xn_ready, j + 2)
                if j == 0:
                    pe.wait_ge(cols_ready, 1)
                    pe.wait_ge(hT_v, 1)
                for k in range(KT):
                    ins = T.transpose(bank[k][:, j * P:(j + 1) * P], xs[:, j, k * P:(k + 1) * P], ident)
                ins.then_inc(xT_done, 1)
            pe.wait_ge(hT_v, 5)
            pe.wait_ge(hT_a, 4)

            def freed(n):
                i = PROD.index(n) - 4
                old = [PROD[i]] if i >= 0 else []
                if n in WITH_META and WITH_META.index(n) >= 2:
                    old.append(WITH_META[WITH_META.index(n) - 2])
                for o in old:
                    if o[0] == "a":
                        pe.wait_ge(glu_done, int(o[1]) + 1)
                    else:
                        pe.wait_ge(evac, taken(o))

            def product_of(n):
                freed(n)
                out_b = pbank(n)
                if n[0] == "v":
                    pe.wait_ge(d_win[5], 16)
                    pe.wait_ge(d_win[6], 16)
                    rws = META if n == "vm" else P
                    t0 = 0 if n == "vm" else META + P * int(n[1])
                    for c0, n0, w in ((C_V, 0, P), (C_HI, P, 256)):
                        for k in range(KT):
                            ins = T.matmul(out_b[0:rws, n0:n0 + w], hT[:, k, t0:t0 + rws], w_in_sb[:, k, c0:c0 + w],
                                           start=(k == 0), stop=(k == KT - 1))
                else:
                    pe.wait_ge(d_win[LOAD_OF[n.rstrip("0123")]], 16)
                    for k in range(KT):
                        w = w_in_sb[:, k, COL[n]:COL[n] + P]
                        ins = T.matmul(out_b[:, :], w, hT[:, k, META:], start=(k == 0), stop=(k == KT - 1))
                        if n in WITH_META:
                            ins = T.matmul(mcols(n), w, hT[:, k, 0:META], start=(k == 0), stop=(k == KT - 1))
                ins.then_inc(product, 1)

            for n in PROD:
                product_of(n)

            pe.wait_ge(kb_ready, 1)
            for ti in range(2):
                for r in range(4):
                    T.transpose(bank[5 + ti][:, r * P:(r + 1) * P], kb[:, ti, META + r * P:META + (r + 1) * P], ident)
                ins = T.transpose(bank[7][0:META, ti * P:(ti + 1) * P], kb[:, ti, 0:META], ident)
                ins.then_inc(kbT, 1)
            rest = [(i, k) for i in range(4) for k in range(KT)]

            def some_queries(count):
                for i, k in rest[:count]:
                    if k == 0 and i == 0:
                        pe.wait_ge(d_win[7], 16)
                    if i == 3 and k == 0:
                        pe.wait_ge(q_out, 2)
                    ins = T.matmul(bank[QUERY_BANK[i]][:, :], w_in_sb[:, k, C_Q + i * P:C_Q + (i + 1) * P], hT[:, k, META:],
                                   start=(k == 0), stop=(k == KT - 1))
                    if k == KT - 1:
                        ins.then_inc(q_made, 1)
                del rest[:count]

            pe.wait_ge(evac, taken("k"))
            some_queries(KT)
            pe.wait_ge(evac, len(EVAC))
            pe.wait_ge(k2_a, 4)
            pe.wait_ge(k2_v, 6)
            for c in range(NC_):
                o = bank[c // 4][:, (c % 4) * P:(c % 4) * P + P].rearrange("p (i e) -> p i e", i=2)
                for ti in range(2):
                    for hp in range(2):
                        s = slice(hp * HD, hp * HD + HD)
                        if c == 0:
                            sm = slice(hp * HD, hp * HD + META)
                            ins = T.matmul(o[s, ti, :], k2m[sm, ti, :], v2m[sm, ti, :], start=True, stop=True)
                        else:
                            ins = T.matmul(o[s, ti, :], k2[s, c - 1, ti, :], v2[s, c - 1, ti, :], start=True, stop=True)
            ins.then_inc(u_done, 1)
            pe.wait_ge(conv_done, 2)
            pe.wait_ge(d_rest, 16)
            mean = cst[:, K_MEAN:K_MEAN + P]
            for i in range(2):
                ins = T.matmul(bank[7][:, :], mean, mixT[:, i, :], start=(i == 0), stop=(i == 1))
            ins.then_inc(mean_done, 1)
            def scores(u):
                p, g, i = u // 2, u % 2, u % 2
                if u >= 2:
                    pe.wait_ge(s_ready, u - 1)
                for h in range(4):
                    s = slice((h % 2) * HD, (h % 2) * HD + HD)
                    q = qT[s, 2 * g + h // 2, p * P:(p + 1) * P]
                    o = bank[2 * i + h % 2][:, (h // 2) * DW:(h // 2 + 1) * DW]
                    t0 = META + p * P
                    if p:
                        T.matmul(o[:, 0:HD], q, kT[s, g, t0 - CHUNK:t0], start=True, stop=True)
                    T.matmul(o[:, HD:HD + META], q, kT[s, g, 0:META], start=True, stop=True)
                    ins = T.matmul(o[:, HD + META:], q, kT[s, g, t0:t0 + P], start=True, stop=True)
                ins.then_inc(s_done, 1)

            nl = len(LEVELS)
            pe.wait_ge(kf_ready, 1)
            for n in range(2 * (nl + 1)):
                ti, l = n % 2, (nl - n // 2)
                if l < nl:
                    pe.wait_ge(lev_w, l + 1)
                if n >= 2:
                    pe.wait_ge(g_used, n - 1)
                for c in range(NC_):
                    for hp in range(2):
                        s = slice(hp * HD, hp * HD + HD)
                        t = slice(c * CHUNK, (c + 1) * CHUNK)
                        if l == nl:
                            kk, qq = kf[s, ti, META + c * CHUNK:META + (c + 1) * CHUNK], qf[s, ti, t]
                        else:
                            kk = qq = lev[l][s, ti, t]
                        ins = T.matmul(bank[2 + n % 2][s, t], kk, qq, start=True, stop=True)
                ins.then_inc(g_done, 1)
                some_queries(2)
                if n == 3:
                    pe.wait_ge(csq, 1)
                    pe.wait_ge(q_out, 1)
                    for i in range(2):
                        ins = T.matmul(bank[4][:, :], mean, osq[:, i, :], start=(i == 0), stop=(i == 1))
                    ins.then_inc(var_done, 1)
            pe.wait_ge(g_used, 2 * (nl + 1))
            pe.wait_ge(state_done, 1)
            pe.wait_ge(q_out, 4)
            scores(0)
            scores(1)

            def hgrn_output(ti):
                if ti == 0:
                    pe.wait_ge(cen_done, 2)
                else:
                    pe.wait_ge(orstd, ti)
                for c in range(NC_):
                    for hp in range(2):
                        s = slice(hp * HD, hp * HD + HD)
                        t = slice(c * CHUNK, (c + 1) * CHUNK)
                        T.matmul(bank[7][s, t], v2[s, c, ti, :], A[s, ti, t], start=True, stop=False)
                        ins = T.matmul(bank[7][s, t], state[s, c, ti, :], qb[s, ti, t], start=False, stop=True)
                ins.then_inc(o_done, 1)

            def hgrn_means(ti):
                pe.wait_ge(osq_done, ti + 1)
                T.matmul(bank[7][:, :], cst[:, K_HEAD:K_HEAD + P], qf[:, ti, :], start=True, stop=True).then_inc(ms_done, 1)

            def turn(u):
                pe.wait_ge(p_ready, u + 1)
                i = u % 3
                if u >= 1:
                    pe.wait_ge(pa_ready, u)
                    pe.wait_ge(pb_ready, u)
                lo = HD if u < 2 else 0
                for h in range(4):
                    T.transpose(bank[5][0:HD + META - lo, h * P:(h + 1) * P], sc[i][:, h, lo:HD + META], ident)
                    ins = T.transpose(bank[6][:, h * P:(h + 1) * P], sc[i][:, h, HD + META:], ident)
                ins.then_inc(pT, 1)

            def values(u):
                p, g = u // 2, u % 2
                pe.wait_ge(pa_ready, u + 1)
                pe.wait_ge(pb_ready, u + 1)
                if u >= 1:
                    pe.wait_ge(y_a, u)
                for h in range(4):
                    o = bank[4][(h % 2) * HD:(h % 2) * HD + HD, (h // 2) * P:(h // 2 + 1) * P]
                    e = slice(g * HD, g * HD + HD)
                    if p == 0:
                        T.matmul(o, vm[0:META, e], pa[0:META, h * P:(h + 1) * P], start=True, stop=False)
                    else:
                        T.matmul(o, vp[0:HD + META, p, e], pa[0:HD + META, h * P:(h + 1) * P], start=True, stop=False)
                    ins = T.matmul(o, va[:, p, e], pb[:, h * P:(h + 1) * P], start=False, stop=True)
                ins.then_inc(pv, 1)

            def project(i):
                j, n = i // 2, i % 2
                if i == 0:
                    pe.wait_ge(y_c, 2)
                    pe.wait_ge(y_h, 2)
                if n == 0:
                    pe.wait_ge(y_a, 2 * j + 2)
                if j == 0:
                    pe.wait_ge(d_wout[n], 16)
                if i >= 1:
                    pe.wait_ge(h2_done, i)
                for k in range(KT):
                    ins = T.matmul(bank[7][:, :], mixT[:, k, j * P:(j + 1) * P], w_out_sb[:, k, n * 512:(n + 1) * 512],
                                   start=(k == 0), stop=(k == KT - 1))
                ins.then_inc(oproj, 1)

            def router_turn(j):
                pe.wait_ge(xf_ready, j + 1)
                for k in range(KT):
                    ins = T.transpose(bank[2 * j + k // 4][:, (k % 4) * P:(k % 4 + 1) * P], xf[:, j, k * P:(k + 1) * P], ident)
                ins.then_inc(xfT, 1)

            def router(j):
                if j == 0:
                    pe.wait_ge(d_rt, 64)
                pe.wait_ge(hfT_a, j + 1)
                pe.wait_ge(hfT_v, j + 1)
                for k in range(KT):
                    ins = T.matmul(bank[0][:, j * NR:(j + 1) * NR], mixT[:, k, j * P:(j + 1) * P], wr[:, k, :],
                                   start=(k == 0), stop=(k == KT - 1))
                ins.then_inc(logits, 1)

            pe.wait_ge(crstd, 1)
            U = 2 * NT
            for u in range(U):
                if u + 2 < U:
                    scores(u + 2)
                turn(u)
                if u < 2:
                    hgrn_output(u)
                else:
                    project(u - 2)
                values(u)
                if u < 2:
                    hgrn_means(u)
            router_turn(0)
            router_turn(1)
            project(6)
            router(0)
            router(1)
            project(7)
            router_turn(2)
            router_turn(3)
            router(2)
            router(3)
            pe.wait_ge(picks, 1)
            tri, ones = cst[:, K_TRI:K_TRI + P], cst[:, K_ONE:K_ONE + P]
            for j in range(NT + 1):
                o = bank[1][:, j * NE:(j + 1) * NE]
                for i in range(j):
                    ins = T.matmul(o, ones, both[:, i, :], start=(i == 0), stop=(i == j - 1 and j == NT))
                if j < NT:
                    T.matmul(o, tri, both[:, j, :], start=(j == 0), stop=True)
            ins.then_inc(ranks, 1)
            pe.wait_ge(match, 1)
            for k in range(2):
                for j in range(NT):
                    T.matmul(bank[2][:, 0:NBLK], slot_is[:, k, j, :], block_is[:, k, j, 0, :],
                             start=(k == j == 0), stop=(k == 1 and j == NT - 1))
            for j in range(NT):
                ins = T.matmul(bank[2][:, NBLK:2 * NBLK], slot_is[:, 1, j, :], block_is[:, 1, j, 1, :],
                               start=(j == 0), stop=(j == NT - 1))
            ins.then_inc(slots, 1)
        @block.gpsimd
        def _(pool):

            Q = nc.gpsimd
            pool.wait_ge(product, 1)
            Q.dma_start(wr[:, :, 0:NG], w_router_group[0].rearrange("(k p) n -> p k n", p=P)).then_inc(d_rt, 16)
            Q.dma_start(wr[:, :, NG:], w_router_expert[0].rearrange("(k p) n -> p k n", p=P)).then_inc(d_rt, 16)
            Q.dma_start(rbias[:, 0:NG], b_router_group[0:1, :].to_broadcast([P, NG])).then_inc(d_rt, 16)
            Q.dma_start(rbias[:, NG:], b_router_expert[0:1, :].to_broadcast([P, NE])).then_inc(d_rt, 16)
            Q.dma_start(gain, ffn_norm[0:1, :].to_broadcast([P, D])).then_inc(d_gain, 16)
            Q.dma_start(gain_out, final_norm.rearrange("(a d) -> a d", a=1).to_broadcast([P, D])).then_inc(d_gain, 32)

        mixer_ctx.close()

        split = sb("split", [P, 3, 2, PIECE], F32R)
        xT = sb("xT", [P, 2, 2, KT * BC], F32R)
        aT = sb("aT", [P, 2, 2 * BC], F32R)
        xg = [sb(f"xg{i}", [P, D])[:, :] for i in range(XS)]
        yb = [sb(f"yb{i}", [P, D])[:, :] for i in range(2)]
        sg = sb("sg", [P, DE])[:, :]
        ab = sb("ab", [P, DE])[:, :]
        HI, LO = 0, 1

        def piece_views(c, part):
            if c < 2:
                return (lambda r: r.rearrange("p (w k n) -> p k w n", w=2, n=DE)), \
                    split[:, c, part, :].rearrange("p (k w n) -> p k w n", w=2, n=DE)
            return (lambda r: r), split[:, c, part, :]

        def plain(a):
            return a.bitcast(F32)

        def gate_up(T, out_b, u, c):
            w = [split[:, c, part, :].rearrange("p (k n) -> p k n", k=KT // 2) for part in (HI, LO)]
            for k in range(KT // 2):
                kk = c * (KT // 2) + k
                x_hi, x_lo = (xT[:, u, part, kk * BC:(kk + 1) * BC] for part in (HI, LO))
                T.matmul(out_b, x_hi, w[HI][:, k, :], start=(kk == 0), stop=False)
                T.matmul(out_b, x_hi, w[LO][:, k, :], start=False, stop=False)
                ins = T.matmul(out_b, x_lo, w[HI][:, k, :], start=False, stop=(kk == KT - 1))
            return ins

        def down(T):
            w = [split[:, 2, part, :].rearrange("p (f n) -> p f n", f=2) for part in (HI, LO)]
            for f in range(2):
                a_hi, a_lo = (aT[:, part, f * BC:(f + 1) * BC] for part in (HI, LO))
                for a, part, start, stop in ((a_hi, HI, f == 0, False), (a_hi, LO, False, False), (a_lo, HI, False, f == 1)):
                    for h in range(2):
                        ins = T.matmul(bank[5 + h][:, :], a, w[part][:, f, h * 512:(h + 1) * 512], start=start, stop=stop)
            return ins

        def turn_x(T, src):
            cols_of = src[:, :].rearrange("p (d k) -> p k d", k=KT)
            for k in range(KT):
                ins = T.transpose(bank[2 + k // 4][:, (k % 4) * BC:(k % 4 + 1) * BC], cols_of[:, k, :], ident)
            return ins

        def turn_act(T):
            cols_of = ab[:, :].rearrange("p (d f) -> p f d", f=2)
            for f in range(2):
                ins = T.transpose(bank[4][:, f * BC:(f + 1) * BC], cols_of[:, f, :], ident)
            return ins

        experts = ctx.enter_context(nc.Block())

        @experts.sync
        def _(sp):
            def load_step(g, r, only=(0, 1, 2)):
                for c in only:
                    slot = (3 * r + c) % RAW
                    if isinstance(g, int):
                        of = lambda w: w[0, 4 * g + r - (c == 2)]
                    else:
                        of = lambda w: w[0, bass.ds(g * 4 + (r - (c == 2)), 1)].rearrange("a k n -> (a k) n")
                    v = g * 12 + (3 * r + c - RAW)
                    sp.wait_ge(lo_done, through(v))
                    sp.sem_inc(passed, 1)
                    if c < 2:
                        load_gate_up(sp, of, c, slot, d_raw[slot])
                    else:
                        load_down(sp, of, slot, d_raw[slot])

            load_step(0, 2)
            load_step(0, 3)
            with sp.Fori(1, NE // 4) as g:
                for r in range(4):
                    load_step(g, r)
            load_step(NE // 4, 0, (2,))

            more = sp.value_load(tab[0:1, 0:1], min_val=0, max_val=MORE)
            with sp.If(more > 0):
                with sp.Fori(0, more) as m:
                    e = sp.value_load(tab[0:1, bass.ds(m + 1, 1)], min_val=0, max_val=NE - 1)
                    of = lambda w: w[0, bass.ds(e, 1)].rearrange("a k n -> (a k) n")
                    sp.wait_ge(m_free, m + 1)
                    sp.sem_inc(passed, 1)
                    for c in range(2):
                        load_gate_up(sp, of, c, c, m_w)
                    load_down(sp, of, 2, m_w)
            for u in range(2):
                sp.wait_ge(d_sc[u], 32 * (NE // 2))
            sp.wait_ge(m_free, more + 1)
            sp.sem_inc(passed, 1)
            for j in range(NT):
                for k in range(2):
                    sp.dma_start(ye[k][:, j, :], expert_out[k * SEQ + j * P:k * SEQ + (j + 1) * P, :]).then_inc(d_ye[j], 16)
            for j in range(NT):
                sp.wait_ge(o_ready, j + 1)
                sp.dma_start(out[0, j * P:(j + 1) * P, :], xs[:, j, :]).then_inc(d_out, 16)
            sp.wait_ge(d_out, 16 * NT)

        @experts.scalar
        def _(act):
            A_ = nc.scalar
            an = [0]

            def hi_piece(c, slot):
                view, dst = piece_views(c, HI)
                return A_.activation(dst, view(raw[slot]), ACT.Copy)

            def hi(g, r, c):
                v = g * 12 + (3 * r + c)
                slot = (3 * r + c) % RAW
                if isinstance(v, int):
                    act.wait_ge(d_raw[slot], 32 * (v // RAW + (slot != 2)))
                    if v >= 3:
                        act.wait_ge(piece_used, through(v - 3))
                else:
                    act.wait_ge(d_raw[slot], g * (32 * 12 // RAW) + 32 * ((3 * r + c) // RAW + (slot != 2)))
                    act.wait_ge(piece_used, through(v - 3))
                hi_piece(c, slot).then_inc(hi_done, 1)

            def x_hi(e, u):
                act.wait_ge(xT_made, e + 1)
                for h in range(2):
                    A_.activation(xT[:, u, HI, h * 512:(h + 1) * 512], bank[2 + h][:, :], ACT.Copy).then_inc(xT_hi, 1)

            def a_hi(e):
                act.wait_ge(aT_made, e + 1)
                A_.activation(aT[:, HI, :], bank[4][:, 0:2 * BC], ACT.Copy).then_inc(aT_hi, 1)

            def silu_of(g, r):
                e = g * 4 + r
                act.wait_ge(piece_used, through(g * 12 + (3 * r + 1)))
                if not isinstance(e, int) or e >= 1:
                    act.wait_ge(act_ready, e)
                A_.activation(sg, bank[r % 2][:, 0:DE], ACT.Silu).then_inc(sg_ready, 1)

            def y_out(g, r):
                u = (r - 1) % 2
                act.wait_ge(piece_used, through(g * 12 + (3 * r + 2)))
                n = g * 2 + (r - 1 - u) // 2
                if not isinstance(n, int) or n >= 1:
                    act.wait_ge(d_sc[u], n * 32)
                for h in range(2):
                    A_.activation(yb[u][:, h * 512:(h + 1) * 512], bank[5 + h][:, :], ACT.Copy).then_inc(y_ready, 1)

            def step_act(g, r, last=False):
                e = g * 4 + r
                busy = not isinstance(e, int) or e >= 1
                if busy:
                    hi(g, r, 2)
                    a_hi(e - 1)
                if not last:
                    x_hi(e + 1, (r + 1) % 2)
                    hi_next(g, r, 0)
                    silu_of(g, r)
                    hi_next(g, r, 1)
                if busy:
                    y_out(g, r)

            def hi_next(g, r, c):
                if r < 3:
                    hi(g, r + 1, c)
                else:
                    hi(g + 1, 0, c)

            hi(0, 0, 0)
            hi(0, 0, 1)
            x_hi(0, 0)
            for r in range(4):
                step_act(0, r)
            with act.Fori(1, NE // 4 - 1) as g:
                for r in range(4):
                    step_act(g, r)
            g = NE // 4 - 1
            for r in range(3):
                step_act(g, r)
            hi(g, 3, 2)
            a_hi(NE - 2)
            x_hi(NE, 0)
            silu_of(g, 3)
            y_out(g, 3)
            hi(NE // 4, 0, 2)
            a_hi(NE - 1)
            y_out(NE // 4, 0)

            more = act.value_load(tab[0:1, 0:1], min_val=0, max_val=MORE)
            with act.If(more > 0):
                with act.Fori(0, more) as m:
                    act.wait_ge(m_xT, m + 1)
                    for h in range(2):
                        A_.activation(xT[:, 0, HI, h * 512:(h + 1) * 512], bank[2 + h][:, :], ACT.Copy).then_inc(m_xhi, 1)
                    act.wait_ge(m_w, m * 96 + 96)
                    for c in range(3):
                        hi_piece(c, c).then_inc(m_hi, 1)
                    act.wait_ge(m_gu, m + 1)
                    A_.activation(sg, bank[0][:, 0:DE], ACT.Silu).then_inc(m_sg, 1)
                    act.wait_ge(m_aT, m + 1)
                    A_.activation(aT[:, HI, :], bank[4][:, 0:2 * BC], ACT.Copy).then_inc(m_ahi, 1)
                    act.wait_ge(m_down, m + 1)
                    for h in range(2):
                        A_.activation(yb[0][:, h * 512:(h + 1) * 512], bank[5 + h][:, :], ACT.Copy).then_inc(m_y, 1)

            act.preload_act_table_set("natural_log_exp_and_others")
            for j in range(NT):
                act.wait_ge(summed, j + 1)
                A_.activation(area_w[:, JUNK:JUNK + D], xs[:, j, :], ACT.Square, accum_out=ss[:, j:j + 1]).then_inc(nstep, 1)
                act.wait_ge(nstep, 2 * j + 1)
                A_.activation(rstd[:, j:j + 1], ss[:, j:j + 1], ACT.Ln, bias=eps, scale=1.0 / D).then_inc(nstep, 1)
                act.wait_ge(nstep, 2 * j + 2)
                A_.activation(rstd[:, j:j + 1], rstd[:, j:j + 1], ACT.Exp, scale=-0.5).then_inc(ostat, 1)

        @experts.vector
        def _(dve):
            V = nc.vector

            def lo_piece(c, slot):
                view, dst = piece_views(c, LO)
                _, top = piece_views(c, HI)
                return V.tensor_tensor(dst, view(raw[slot]), plain(top), ALU.subtract)

            def lo(g, r, c):
                dve.wait_ge(hi_done, through(g * 12 + (3 * r + c)))
                lo_piece(c, (3 * r + c) % RAW).then_inc(lo_done, 1)

            def lo_next(g, r, c):
                if r < 3:
                    lo(g, r + 1, c)
                else:
                    lo(g + 1, 0, c)

            def x_lo(e, u):
                for h in range(2):
                    dve.wait_ge(xT_hi, e * 2 + (h + 1))
                    s_ = slice(h * 512, (h + 1) * 512)
                    V.tensor_tensor(xT[:, u, LO, s_], bank[2 + h][:, :], plain(xT[:, u, HI, s_]), ALU.subtract).then_inc(xT_lo, 1)

            def a_lo(e):
                dve.wait_ge(aT_hi, e + 1)
                V.tensor_tensor(aT[:, LO, :], bank[4][:, 0:2 * BC], plain(aT[:, HI, :]), ALU.subtract).then_inc(aT_lo, 1)

            def gated(e, u):
                dve.wait_ge(sg_ready, e + 1)
                if not isinstance(e, int) or e >= 1:
                    dve.wait_ge(aT_made, e)
                V.tensor_tensor(ab, sg, bank[u][:, DE:2 * DE], ALU.mult).then_inc(act_ready, 1)

            def step_dve(g, r):
                e = g * 4 + r
                if not isinstance(e, int) or e >= 1:
                    lo(g, r, 2)
                    a_lo(e - 1)
                x_lo(e + 1, (r + 1) % 2)
                lo_next(g, r, 0)
                gated(e, r % 2)
                lo_next(g, r, 1)

            for i in range(XS):
                V.memset(xg[i], 0.0).then_inc(xg_clear, 1)
            lo(0, 0, 0)
            lo(0, 0, 1)
            x_lo(0, 0)
            for r in range(4):
                step_dve(0, r)
            with dve.Fori(1, NE // 4 - 1) as g:
                for r in range(4):
                    step_dve(g, r)
            g = NE // 4 - 1
            for r in range(3):
                step_dve(g, r)
            lo(g, 3, 2)
            a_lo(NE - 2)
            x_lo(NE, 0)
            gated(NE - 1, 1)
            lo(NE // 4, 0, 2)
            a_lo(NE - 1)

            more = dve.value_load(tab[0:1, 0:1], min_val=0, max_val=MORE)
            with dve.If(more > 0):
                with dve.Fori(0, more) as m:
                    for h in range(2):
                        dve.wait_ge(m_xhi, m * 2 + (h + 1))
                        s_ = slice(h * 512, (h + 1) * 512)
                        V.tensor_tensor(xT[:, 0, LO, s_], bank[2 + h][:, :], plain(xT[:, 0, HI, s_]), ALU.subtract).then_inc(m_xlo, 1)
                    for c in range(3):
                        dve.wait_ge(m_hi, m * 3 + (c + 1))
                        lo_piece(c, c).then_inc(m_lo, 1)
                    dve.wait_ge(m_sg, m + 1)
                    V.tensor_tensor(ab, sg, bank[0][:, DE:2 * DE], ALU.mult).then_inc(m_act, 1)
                    dve.wait_ge(m_ahi, m + 1)
                    V.tensor_tensor(aT[:, LO, :], bank[4][:, 0:2 * BC], plain(aT[:, HI, :]), ALU.subtract).then_inc(m_alo, 1)

            def row_sum(j):
                dve.wait_ge(d_ye[j], 32)
                V.scalar_tensor_tensor(out=xs[:, j, :], in0=ye[0][:, j, :], scalar=w1[:, j:j + 1], in1=xs[:, j, :],
                                       op0=ALU.mult, op1=ALU.add).then_inc(first_sum, 1)
                dve.wait_ge(first_sum, j + 1)
                V.scalar_tensor_tensor(out=xs[:, j, :], in0=ye[1][:, j, :], scalar=w2[:, j:j + 1], in1=xs[:, j, :],
                                       op0=ALU.mult, op1=ALU.add).then_inc(summed, 1)

            def row_norm(j):
                dve.wait_ge(ostat, j + 1)
                V.scalar_tensor_tensor(out=xs[:, j, :], in0=xs[:, j, :], scalar=rstd[:, j:j + 1], in1=gain_out,
                                       op0=ALU.mult, op1=ALU.mult).then_inc(o_ready, 1)

            row_sum(0)
            for j in range(1, NT):
                row_sum(j)
                row_norm(j - 1)
            row_norm(NT - 1)

        @experts.tensor
        def _(pe):
            T = nc.tensor

            def x_turn(e, s, n):
                pe.wait_ge(d_xg[s], n)
                if not isinstance(e, int) or e >= 1:
                    pe.wait_ge(xT_lo, e * 2)
                pe.sem_inc(passed, 1)
                turn_x(T, xg[s]).then_inc(xT_made, 1)

            def half(g, r, c):
                e = g * 4 + r
                pe.wait_ge(lo_done, through(g * 12 + (3 * r + c)))
                if c == 0:
                    pe.wait_ge(xT_lo, e * 2 + 2)
                    if not isinstance(e, int) or e >= 2:
                        pe.wait_ge(act_ready, e - 1)
                gate_up(T, bank[r % 2][:, :], r % 2, c).then_inc(piece_used, 1)

            def act_turn(e):
                pe.wait_ge(act_ready, e + 1)
                if not isinstance(e, int) or e >= 1:
                    pe.wait_ge(aT_lo, e)
                pe.sem_inc(passed, 1)
                turn_act(T).then_inc(aT_made, 1)

            def third(g, r):
                e = g * 4 + (r - 1)
                pe.wait_ge(lo_done, through(g * 12 + (3 * r + 2)))
                pe.wait_ge(aT_lo, e + 1)
                if not isinstance(e, int) or e >= 1:
                    pe.wait_ge(y_ready, e * 2)
                down(T).then_inc(piece_used, 1)

            def step_pe(g, r):
                e = g * 4 + r
                busy = not isinstance(e, int) or e >= 1
                half(g, r, 0)
                if busy:
                    act_turn(e - 1)
                x_turn(e + 1, (r + 1) % XS, g * 32 + 32 * ((r + 1) // XS + 1))
                half(g, r, 1)
                if busy:
                    third(g, r)

            x_turn(0, 0, 32)
            for r in range(4):
                step_pe(0, r)
            with pe.Fori(1, NE // 4) as g:
                for r in range(4):
                    step_pe(g, r)
            act_turn(NE - 1)
            third(NE // 4, 0)

            more = pe.value_load(tab[0:1, 0:1], min_val=0, max_val=MORE)
            with pe.If(more > 0):
                with pe.Fori(0, more) as m:
                    pe.wait_ge(m_xg, m * 32 + 32)
                    pe.sem_inc(passed, 1)
                    turn_x(T, xg[0]).then_inc(m_xT, 1)
                    pe.wait_ge(m_xlo, m * 2 + 2)
                    for c in range(2):
                        pe.wait_ge(m_lo, m * 3 + (c + 1))
                        ins = gate_up(T, bank[0][:, :], 0, c)
                    ins.then_inc(m_gu, 1)
                    pe.wait_ge(m_act, m + 1)
                    pe.sem_inc(passed, 1)
                    turn_act(T).then_inc(m_aT, 1)
                    pe.wait_ge(m_alo, m + 1)
                    pe.wait_ge(m_lo, m * 3 + 3)
                    down(T).then_inc(m_down, 1)

        @experts.gpsimd
        def _(pool):
            Q = nc.gpsimd
            def size_of(e):
                at_t = slice(T_SIZE + e, T_SIZE + e + 1) if isinstance(e, int) else bass.ds(e + T_SIZE, 1)
                return pool.value_load(tab[0:1, at_t], min_val=0, max_val=2)

            def column(dst, at_c, steps):
                Q.tensor_copy(dst.unsqueeze(2), idx[:, :, at_c]).then_inc(col_ready, 1)
                pool.wait_ge(col_ready, steps)
                pool.sem_inc(passed, 1)

            def rows_in(s, h, d, n=HALF):
                Q.indirect_dma_start(xg[s][h * HALF:h * HALF + n, :], None, normed,
                                     bass.IndirectOffsetOnAxis(ap=col_g[s][0:n, h:h + 1].bitcast(U32), axis=0),
                                     bounds_check=SEQ - 1, oob_is_err=False).then_inc(d, 16)

            def rows_out(u, h, d, n=HALF):
                Q.indirect_dma_start(expert_out, bass.IndirectOffsetOnAxis(ap=col_s[u][0:n, h:h + 1].bitcast(U32), axis=0),
                                     yb[u][h * HALF:h * HALF + n, :], None, bounds_check=2 * SEQ - 1, oob_is_err=False).then_inc(d, 16)

            def move(rows_of, s, d, e):
                rows = size_of(e)
                with pool.If(rows < 1):
                    rows_of(s, 0, d, FEW)
                with pool.If(rows > 0):
                    rows_of(s, 0, d)
                with pool.If(rows > 1):
                    rows_of(s, 1, d)
                with pool.If(rows < 2):
                    rows_of(s, 1, d, 2)

            def step_pool(g, r):
                e = g * 4 + r
                s = (r + 3) % XS
                if not isinstance(e, int) or e >= 1:
                    pool.wait_ge(xT_made, e)
                    pool.sem_inc(passed, 1)
                at_c = slice(e + 3, e + 4) if isinstance(e, int) else bass.ds(e + 3, 1)
                if isinstance(e, int) and e == 0:
                    pool.wait_ge(xg_clear, XS)
                column(col_g[s], at_c, 4 if isinstance(e, int) and e == 0 else e * 2 + 3)
                move(rows_in, s, d_xg[s], e + 3)
                if not isinstance(e, int) or e >= 1:
                    pool.wait_ge(y_ready, e * 2)
                    pool.sem_inc(passed, 1)
                    u = (r - 1) % 2
                    at_c = slice(NBLK + e - 1, NBLK + e) if isinstance(e, int) else bass.ds(e + (NBLK - 1), 1)
                    column(col_s[u], at_c, e * 2 + 4)
                    move(rows_out, u, d_sc[u], e - 1)

            for e in range(3):
                column(col_g[e], slice(e, e + 1), e + 1)
                pool.wait_ge(xg_clear, e + 1)
                move(rows_in, e, d_xg[e], e)
            for r in range(4):
                step_pool(0, r)
            with pool.Fori(1, NE // 4) as g:
                for r in range(4):
                    step_pool(g, r)
            pool.wait_ge(y_ready, 2 * NE)
            column(col_s[1], slice(NBLK + NE - 1, NBLK + NE), 2 * NE + 3)
            move(rows_out, 1, d_sc[1], NE - 1)
            for s in range(XS):
                pool.wait_ge(d_xg[s], 32 * (NE // XS + (s < 3)))
            for u in range(2):
                pool.wait_ge(d_sc[u], 32 * (NE // 2))
            pool.sem_inc(m_free, 1)
            more = pool.value_load(tab[0:1, 0:1], min_val=0, max_val=MORE)
            with pool.If(more > 0):
                with pool.Fori(0, more) as m:
                    pool.wait_ge(m_free, m + 1)
                    pool.sem_inc(passed, 1)
                    column(col_g[0], bass.ds(m + NE, 1), m * 2 + (2 * NE + 4))
                    for h in range(2):
                        rows_in(0, h, m_xg)
                    pool.wait_ge(m_y, m * 2 + 2)
                    pool.sem_inc(passed, 1)
                    column(col_s[0], bass.ds(m + (NBLK + NE), 1), m * 2 + (2 * NE + 5))
                    for h in range(2):
                        rows_out(0, h, m_sc)
                    pool.wait_ge(m_sc, m * 32 + 32)
                    pool.sem_inc(m_free, 1)


_INS = ["x", "meta_tokens", "mix_norm", "w_in", "conv_dw_w", "conv_dw_b", "conv_ln_g", "conv_ln_b", "attn_sinks",
        "hgrn_norm_g", "w_out", "ffn_norm", "w_router_group", "b_router_group", "w_router_expert",
        "b_router_expert", "w_exp_gate", "w_exp_up", "w_exp_down", "final_norm"]


def kernel(**inputs):
    import numpy as _np
    import concourse.bacc as _bacc
    from concourse import mybir as _mybir
    from concourse.bass_utils import run_bass_kernel_spmd as _run

    nc = _bacc.Bacc("TRN2", target_bir_lowering=False, num_devices=1)
    arrays, args = {}, []
    for name in _INS:
        a = _np.ascontiguousarray(inputs[name])
        arrays[f"in_{name}"] = a
        args.append(nc.dram_tensor(f"in_{name}", a.shape, _mybir.dt.from_np(a.dtype), kind="ExternalInput").ap())
    arrays["in_table"] = shape_constants()
    args.append(nc.dram_tensor("in_table", arrays["in_table"].shape, F32, kind="ExternalInput").ap())
    normed = nc.dram_tensor("normed", (SEQ, D), F32, kind="Internal").ap()
    expert_out = nc.dram_tensor("expert_out", (2 * SEQ, D), F32, kind="Internal").ap()
    out = nc.dram_tensor("out_0", (1, SEQ, D), F32, kind="ExternalOutput").ap()
    trunk(nc, *args, normed, expert_out, out)
    r = _run(nc, [arrays], core_ids=[0])
    return r.results[0]["out_0"]
```
